# Optimizing a Trainium2 kernel written in Bass

```python
import math
import numpy as np
import jax, jax.numpy as jnp
from jax import lax

D_MODEL = 1024
BATCH = 1
SEQ = 256
DEPTH = 2

DN_HEADS = 4
DN_HEAD_DIM = 128
DN_WIDTH = DN_HEADS * DN_HEAD_DIM
DN_CONV = 4
DN_CHUNK = 64
SWA_HEADS = 8
SWA_HEAD_DIM = 64
SWA_WIDTH = SWA_HEADS * SWA_HEAD_DIM
DILATED_CONFIGS = ((128, 1), (512, 4), (2048, 16))
ATTN_BLOCK = 128
ROPE_THETA = 500000.0
ROPE_DIM = SWA_HEAD_DIM // 4
D_MIX = DN_WIDTH + SWA_WIDTH
IN_SPLITS = (3 * DN_WIDTH, DN_WIDTH, DN_HEADS, DN_HEADS, SWA_WIDTH, SWA_WIDTH, SWA_WIDTH)
IN_WIDTH = sum(IN_SPLITS)
D_FF = 2816
FFN_CONV = 3
NORM_EPS = 1e-6


def _rmsnorm(x, w):
    xf = x.astype(jnp.float32)
    y = xf * lax.rsqrt(jnp.mean(xf * xf, axis=-1, keepdims=True) + NORM_EPS)
    return (y * w.astype(jnp.float32)).astype(x.dtype)

def _l2norm(x):
    xf = x.astype(jnp.float32)
    return xf * lax.rsqrt(jnp.sum(xf * xf, axis=-1, keepdims=True) + NORM_EPS)

def _causal_dwconv(x, w):
    K = w.shape[0]
    S = x.shape[1]
    xp = jnp.pad(x, ((0, 0), (K - 1, 0), (0, 0)))
    y = xp[:, 0:S] * w[0]
    for j in range(1, K):
        y = y + xp[:, j:j + S] * w[j]
    return y

def _rope_tables(S):
    pos = jnp.arange(S, dtype=jnp.float32)
    inv_freq = ROPE_THETA ** (-jnp.arange(0, ROPE_DIM, 2, dtype=jnp.float32) / ROPE_DIM)
    ang = pos[:, None] * inv_freq[None, :]
    return jnp.cos(ang), jnp.sin(ang)

def _partial_rope(x, cos, sin):
    half = ROPE_DIM // 2
    c = cos[None, :, None, :].astype(x.dtype)
    s = sin[None, :, None, :].astype(x.dtype)
    x1, x2, rest = x[..., :half], x[..., half:ROPE_DIM], x[..., ROPE_DIM:]
    return jnp.concatenate([x1 * c - x2 * s, x2 * c + x1 * s, rest], axis=-1)

def _gated_delta_rule(q, k, v, g, beta):
    B, S, H, Dk = q.shape
    Dv = v.shape[-1]
    C = DN_CHUNK
    n = S // C
    f32 = jnp.float32

    def chunks(t):
        return t.astype(f32).reshape(B, n, C, H, -1).transpose(0, 3, 1, 2, 4)

    q = chunks(q) * (Dk ** -0.5)
    k = chunks(k)
    v = chunks(v)
    g = g.astype(f32).reshape(B, n, C, H).transpose(0, 3, 1, 2)
    beta = beta.astype(f32).reshape(B, n, C, H).transpose(0, 3, 1, 2)
    G = jnp.cumsum(g, axis=-1)
    idx = jnp.arange(C)
    incl = idx[:, None] >= idx[None, :]
    strict = idx[:, None] > idx[None, :]
    gamma = jnp.exp(jnp.where(incl, G[..., :, None] - G[..., None, :], -jnp.inf))
    kb = k * beta[..., None]
    a_kk = jnp.where(strict, jnp.einsum('bhnid,bhnjd->bhnij', kb, k) * gamma, 0.0)
    tri = a_kk + jnp.eye(C, dtype=f32)
    rhs = jnp.concatenate([v * beta[..., None], kb * jnp.exp(G)[..., None]], axis=-1)
    sol = lax.linalg.triangular_solve(tri, rhs, left_side=True, lower=True, unit_diagonal=True)
    u, w = sol[..., :Dv], sol[..., Dv:]
    qk = jnp.einsum('bhnid,bhnjd->bhnij', q, k) * gamma
    qg = q * jnp.exp(G)[..., None]
    kd = k * jnp.exp(G[..., -1:] - G)[..., None]
    dc = jnp.exp(G[..., -1])

    def step(state, xs):
        u_c, w_c, qk_c, qg_c, kd_c, dc_c = xs
        v_new = u_c - jnp.einsum('bhcd,bhde->bhce', w_c, state)
        o_c = jnp.einsum('bhcd,bhde->bhce', qg_c, state) + jnp.einsum('bhij,bhje->bhie', qk_c, v_new)
        state = state * dc_c[..., None, None] + jnp.einsum('bhcd,bhce->bhde', kd_c, v_new)
        return state, o_c

    xs = tuple(jnp.moveaxis(t, 2, 0) for t in (u, w, qk, qg, kd, dc))
    state0 = jnp.zeros((B, H, Dk, Dv), f32)
    _, o = lax.scan(step, state0, xs)
    return o.transpose(1, 0, 3, 2, 4).reshape(B, S, H, Dv)

def _causal_window_attention(q, k, v, span):
    N, L, H, Dh = q.shape
    nb = -(-L // ATTN_BLOCK)
    pad = nb * ATTN_BLOCK - L
    qb = jnp.pad(q, ((0, 0), (0, pad), (0, 0), (0, 0))).reshape(N, nb, ATTN_BLOCK, H, Dh)

    def kv_blocks(t):
        t = jnp.pad(t, ((0, 0), (ATTN_BLOCK, pad), (0, 0), (0, 0))).reshape(N, nb + 1, ATTN_BLOCK, H, Dh)
        return jnp.concatenate([t[:, :-1], t[:, 1:]], axis=2)

    kw, vw = kv_blocks(k), kv_blocks(v)
    s = jnp.einsum('nbqhd,nbkhd->nbhqk', qb, kw, preferred_element_type=jnp.float32)
    qi = jnp.arange(ATTN_BLOCK)[:, None]
    ki = jnp.arange(2 * ATTN_BLOCK)[None, :]
    dist = qi + ATTN_BLOCK - ki
    key_pos = jnp.arange(nb)[:, None, None] * ATTN_BLOCK - ATTN_BLOCK + ki[None]
    valid = (dist >= 0) & (dist <= span) & (key_pos >= 0)
    s = jnp.where(valid[None, :, None], s, -jnp.inf)
    lse = jax.nn.logsumexp(s, axis=-1)
    p = jnp.exp(s - lse[..., None])
    o = jnp.einsum('nbhqk,nbkhd->nbqhd', p, vw.astype(jnp.float32))
    o = o.reshape(N, nb * ATTN_BLOCK, H, Dh)[:, :L]
    lse = lse.transpose(0, 1, 3, 2).reshape(N, nb * ATTN_BLOCK, H)[:, :L]
    return o, lse

def _dilated_attention(q, k, v):
    B, S, H, Dh = q.shape
    q = q * (Dh ** -0.5)
    outs, lses = [], []
    for window, dil in DILATED_CONFIGS:
        L = S // dil

        def by_residue(t):
            return t.reshape(B, L, dil, H, Dh).transpose(0, 2, 1, 3, 4).reshape(B * dil, L, H, Dh)

        o, lse = _causal_window_attention(by_residue(q), by_residue(k), by_residue(v), window // dil)
        outs.append(o.reshape(B, dil, L, H, Dh).transpose(0, 2, 1, 3, 4).reshape(B, S, H, Dh))
        lses.append(lse.reshape(B, dil, L, H).transpose(0, 2, 1, 3).reshape(B, S, H))
    wts = jax.nn.softmax(jnp.stack(lses), axis=0)
    o = jnp.einsum('gbsh,gbshd->bshd', wts, jnp.stack(outs))
    return o.astype(v.dtype)

def _hybrid_mixer(h, cos, sin, w_in, dn_conv, dn_a_log, dn_dt_bias, dn_out_norm, w_out):
    B, S, _ = h.shape
    proj = h @ w_in
    a_qkv, a_z, a_b, a_a, b_q, b_k, b_v = jnp.split(proj, np.cumsum(IN_SPLITS)[:-1], axis=-1)
    a_qkv = jax.nn.silu(_causal_dwconv(a_qkv, dn_conv))
    aq, ak, av = jnp.split(a_qkv, 3, axis=-1)
    heads_a = lambda t: t.reshape(B, S, DN_HEADS, DN_HEAD_DIM)
    aq, ak, av = _l2norm(heads_a(aq)), _l2norm(heads_a(ak)), heads_a(av)
    beta = jax.nn.sigmoid(a_b.astype(jnp.float32))
    g = -jnp.exp(dn_a_log.astype(jnp.float32)) * jax.nn.softplus(a_a.astype(jnp.float32) + dn_dt_bias.astype(jnp.float32))
    o_a = _gated_delta_rule(aq, ak, av, g, beta).astype(h.dtype)
    o_a = _rmsnorm(o_a, dn_out_norm) * jax.nn.silu(heads_a(a_z))
    heads_b = lambda t: t.reshape(B, S, SWA_HEADS, SWA_HEAD_DIM)
    bq = _partial_rope(heads_b(b_q), cos, sin)
    bk = _partial_rope(heads_b(b_k), cos, sin)
    o_b = _dilated_attention(bq, bk, heads_b(b_v))
    mixed = jnp.concatenate([o_a.reshape(B, S, DN_WIDTH), o_b.reshape(B, S, SWA_WIDTH)], axis=-1)
    return mixed @ w_out

def _conv_glu_ffn(h, ffn_up, ffn_conv, ffn_conv_bias, ffn_down):
    u = _causal_dwconv(h @ ffn_up, ffn_conv) + ffn_conv_bias
    gate, val = jnp.split(u, 2, axis=-1)
    return (jax.nn.gelu(gate, approximate=True) * val) @ ffn_down

def first_inputs(seed: int = 0) -> dict:
    key = jax.random.key(seed)
    ks = jax.random.split(key, 16)
    f32 = jnp.float32

    def normal(k, shape, scale):
        return jax.random.normal(k, shape, f32) * scale

    def gain(k, shape):
        return 1.0 + 0.02 * jax.random.normal(k, shape, f32)

    x = normal(ks[0], (BATCH, SEQ, D_MODEL), 1.0)
    pre_mix_norm = gain(ks[1], (DEPTH, D_MODEL))
    w_in = normal(ks[2], (DEPTH, D_MODEL, IN_WIDTH), D_MODEL ** -0.5)
    dn_conv = normal(ks[3], (DEPTH, DN_CONV, 3 * DN_WIDTH), DN_CONV ** -0.5)
    dn_a_log = jnp.log(jax.random.uniform(ks[4], (DEPTH, DN_HEADS), f32, 1.0, 16.0))
    dt = jnp.exp(jax.random.uniform(ks[5], (DEPTH, DN_HEADS), f32, math.log(1e-3), math.log(1e-1)))
    dn_dt_bias = dt + jnp.log(-jnp.expm1(-dt))
    dn_out_norm = gain(ks[6], (DEPTH, DN_HEAD_DIM))
    w_out = normal(ks[7], (DEPTH, D_MIX, D_MODEL), D_MIX ** -0.5)
    post_mix_norm = gain(ks[8], (DEPTH, D_MODEL))
    pre_ffn_norm = gain(ks[9], (DEPTH, D_MODEL))
    ffn_up = normal(ks[10], (DEPTH, D_MODEL, 2 * D_FF), D_MODEL ** -0.5)
    ffn_conv = normal(ks[11], (DEPTH, FFN_CONV, 2 * D_FF), FFN_CONV ** -0.5)
    ffn_conv_bias = normal(ks[12], (DEPTH, 2 * D_FF), 0.02)
    ffn_down = normal(ks[13], (DEPTH, D_FF, D_MODEL), D_FF ** -0.5)
    post_ffn_norm = gain(ks[14], (DEPTH, D_MODEL))
    return {"x": x, "pre_mix_norm": pre_mix_norm, "w_in": w_in, "dn_conv": dn_conv,
            "dn_a_log": dn_a_log, "dn_dt_bias": dn_dt_bias, "dn_out_norm": dn_out_norm,
            "w_out": w_out, "post_mix_norm": post_mix_norm, "pre_ffn_norm": pre_ffn_norm,
            "ffn_up": ffn_up, "ffn_conv": ffn_conv, "ffn_conv_bias": ffn_conv_bias,
            "ffn_down": ffn_down, "post_ffn_norm": post_ffn_norm}

def first_block(x, pre_mix_norm, w_in, dn_conv, dn_a_log, dn_dt_bias, dn_out_norm, w_out,
              post_mix_norm, pre_ffn_norm, ffn_up, ffn_conv, ffn_conv_bias, ffn_down, post_ffn_norm):
    S = x.shape[1]
    cos, sin = _rope_tables(S)
    for l in range(DEPTH):
        h = _rmsnorm(x, pre_mix_norm[l])
        h = _hybrid_mixer(h, cos, sin, w_in[l], dn_conv[l], dn_a_log[l], dn_dt_bias[l], dn_out_norm[l], w_out[l])
        x = x + _rmsnorm(h, post_mix_norm[l])
        h = _rmsnorm(x, pre_ffn_norm[l])
        h = _conv_glu_ffn(h, ffn_up[l], ffn_conv[l], ffn_conv_bias[l], ffn_down[l])
        x = x + _rmsnorm(h, post_ffn_norm[l])
    return x


DEPTH_2 = 1

HEAD_DIM = D_MODEL // 16
GLA_HEADS = 4
GLA_DK = HEAD_DIM // 2
GLA_DV = HEAD_DIM
GLA_GATE_RANK = 16
GLA_GATE_TAU = 16.0
GLA_CHUNK = 64
CONV_CH = 4 * HEAD_DIM
CONV_GROUPS = 4
CONV_WIDTH = 31
DIFF_HEADS = 4
DIFF_D = HEAD_DIM
Q_BLOCK = 128
D_MIX_2 = GLA_HEADS * GLA_DV + CONV_CH + DIFF_HEADS * 2 * DIFF_D
IN_SPLITS_2 = (GLA_HEADS * GLA_DK, GLA_HEADS * GLA_DK, GLA_HEADS * GLA_DV, GLA_GATE_RANK,
             GLA_HEADS * GLA_DV, 2 * CONV_CH, DIFF_HEADS * 2 * DIFF_D,
             DIFF_HEADS * 2 * DIFF_D, DIFF_HEADS * 2 * DIFF_D)
N_IN = sum(IN_SPLITS_2)
N_GROUPS = 4
EXPERTS_PER_GROUP = 4
N_EXPERTS = N_GROUPS * EXPERTS_PER_GROUP
TOP_K = 2
D_EXPERT = D_MODEL // 4
EPS = 1e-6


def rms_norm(x, g):
    xf = x.astype(jnp.float32)
    y = xf * lax.rsqrt(jnp.mean(xf * xf, axis=-1, keepdims=True) + EPS)
    return (y * g.astype(jnp.float32)).astype(x.dtype)

def gla_mixer(q, k, v, gate_lr, out_gate, w_gate, b_gate, norm_g):
    B, S, _ = q.shape
    dt = q.dtype
    f32 = jnp.float32
    H, DK, DV, C = GLA_HEADS, GLA_DK, GLA_DV, GLA_CHUNK
    nc = S // C
    log_a = jax.nn.log_sigmoid((gate_lr @ w_gate + b_gate).astype(f32)) / GLA_GATE_TAU

    def to_chunks(t, d):
        return t.astype(f32).reshape(B, nc, C, H, d).transpose(1, 0, 3, 2, 4)

    qc = to_chunks(q, DK) * (DK ** -0.5)
    kc = to_chunks(k, DK)
    vc = to_chunks(v, DV)
    gc = to_chunks(log_a, DK)
    causal = jnp.tril(jnp.ones((C, C), dtype=bool))

    def step(state, inp):
        qi, ki, vi, gi = inp
        b = jnp.cumsum(gi, axis=2)
        o_inter = jnp.einsum('bhik,bhkv->bhiv', qi * jnp.exp(b), state)
        diff = b[:, :, :, None, :] - b[:, :, None, :, :]
        decay = jnp.exp(jnp.where(causal[:, :, None], diff, -jnp.inf))
        scores = jnp.einsum('bhik,bhjk,bhijk->bhij', qi, ki, decay)
        o = o_inter + jnp.einsum('bhij,bhjv->bhiv', scores, vi)
        b_last = b[:, :, -1:, :]
        new_state = (jnp.exp(b_last[:, :, 0, :])[..., None] * state
                     + jnp.einsum('bhjk,bhjv->bhkv', ki * jnp.exp(b_last - b), vi))
        return new_state, o

    s0 = jnp.zeros((B, H, DK, DV), f32)
    _, o = lax.scan(step, s0, (qc, kc, vc, gc))
    o = o.transpose(1, 0, 3, 2, 4).reshape(B, S, H, DV)
    o = rms_norm(o, norm_g).reshape(B, S, H * DV)
    o = o * jax.nn.silu(out_gate.astype(f32))
    return o.astype(dt)

def conv_mixer(u, w, b, gn_g, gn_b):
    dt = u.dtype
    a, gt = jnp.split(u, 2, axis=-1)
    z = a * jax.nn.sigmoid(gt)
    zp = jnp.pad(z, ((0, 0), (CONV_WIDTH - 1, 0), (0, 0)))
    y = lax.conv_general_dilated(zp, w[:, None, :].astype(dt), (1,), 'VALID',
                                 dimension_numbers=('NWC', 'WIO', 'NWC'),
                                 feature_group_count=CONV_CH) + b
    B, S, _ = y.shape
    yf = y.astype(jnp.float32).reshape(B, S, CONV_GROUPS, CONV_CH // CONV_GROUPS)
    mu = jnp.mean(yf, axis=-1, keepdims=True)
    var = jnp.mean(jnp.square(yf - mu), axis=-1, keepdims=True)
    yn = ((yf - mu) * lax.rsqrt(var + EPS)).reshape(B, S, CONV_CH)
    yn = yn * gn_g.astype(jnp.float32) + gn_b.astype(jnp.float32)
    return jax.nn.silu(yn).astype(dt)

def diff_attention(q, k, v, qn_g, kn_g, lq1, lk1, lq2, lk2, subln_g, lambda_init):
    B, S, _ = q.shape
    H, D = DIFF_HEADS, DIFF_D
    f32 = jnp.float32
    qh = rms_norm(q.reshape(B, S, H, 2, D), qn_g).transpose(0, 2, 3, 1, 4)
    kh = rms_norm(k.reshape(B, S, H, 2, D), kn_g).transpose(0, 2, 3, 1, 4)
    vh = v.reshape(B, S, H, 2 * D).transpose(0, 2, 1, 3)
    lam = (jnp.exp(jnp.sum(lq1.astype(f32) * lk1.astype(f32)))
           - jnp.exp(jnp.sum(lq2.astype(f32) * lk2.astype(f32))) + lambda_init)
    scale = D ** -0.5
    k_pos = jnp.arange(S)

    def block(i):
        start = i * Q_BLOCK
        qb = lax.dynamic_slice_in_dim(qh, start, Q_BLOCK, axis=3)
        s = jnp.einsum('bhmqd,bhmkd->bhmqk', qb, kh).astype(f32) * scale
        q_pos = start + jnp.arange(Q_BLOCK)
        s = jnp.where(k_pos[None, :] <= q_pos[:, None], s, -jnp.inf)
        p = jax.nn.softmax(s, axis=-1)
        a = p[:, :, 0] - lam * p[:, :, 1]
        return jnp.einsum('bhqk,bhkv->bhqv', a.astype(vh.dtype), vh)

    o = lax.map(block, jnp.arange(S // Q_BLOCK))
    o = o.transpose(1, 0, 3, 2, 4).reshape(B, S, H, 2 * D)
    o = rms_norm(o, subln_g) * (1.0 - lambda_init)
    return o.reshape(B, S, H * 2 * D)

def hier_moe(h, wg, bg, we, be, w_gate, w_up, w_down):
    B, S, D = h.shape
    f32 = jnp.float32
    t = h.reshape(-1, D)
    T = t.shape[0]
    glog = (t @ wg + bg).astype(f32)
    gprob = jax.nn.softmax(glog, axis=-1)
    g_onehot = jax.nn.one_hot(jnp.argmax(glog, axis=-1), N_GROUPS, dtype=f32)
    p_group = jnp.sum(gprob * g_onehot, axis=-1, keepdims=True)
    elog = (t @ we + be).astype(f32).reshape(T, N_GROUPS, EXPERTS_PER_GROUP)
    elog_sel = jnp.einsum('tge,tg->te', elog, g_onehot)
    eprob = jax.nn.softmax(elog_sel, axis=-1)
    top_p, top_i = lax.top_k(eprob, TOP_K)
    top_p = top_p / jnp.sum(top_p, axis=-1, keepdims=True)
    w_local = jnp.sum(jax.nn.one_hot(top_i, EXPERTS_PER_GROUP, dtype=f32) * top_p[..., None], axis=1)
    gates = (g_onehot[:, :, None] * w_local[:, None, :]).reshape(T, N_EXPERTS) * p_group
    gates = gates.astype(t.dtype)
    y = jnp.zeros_like(t)
    for e in range(N_EXPERTS):
        hid = jax.nn.silu(t @ w_gate[e]) * (t @ w_up[e])
        y = y + gates[:, e:e + 1] * (hid @ w_down[e])
    return y.reshape(B, S, D)

def second_inputs(seed: int = 0) -> dict:
    key = jax.random.key(seed)
    ks = jax.random.split(key, 32)
    L, D, f32 = DEPTH_2, D_MODEL, jnp.float32

    def nrm(k, shape, scale):
        return jax.random.normal(k, shape, f32) * scale

    def gain(k, shape):
        return 1.0 + 0.02 * jax.random.normal(k, shape, f32)

    return {
        'x': nrm(ks[0], (BATCH, SEQ, D), 1.0),
        'mix_norm_g': gain(ks[1], (L, D)),
        'w_in': nrm(ks[2], (L, D, N_IN), D ** -0.5),
        'gla_gate_w': nrm(ks[3], (L, GLA_GATE_RANK, GLA_HEADS * GLA_DK), GLA_GATE_RANK ** -0.5),
        'gla_gate_b': nrm(ks[4], (L, GLA_HEADS * GLA_DK), 0.1),
        'gla_norm_g': gain(ks[5], (L, GLA_DV)),
        'conv_w': nrm(ks[6], (L, CONV_WIDTH, CONV_CH), CONV_WIDTH ** -0.5),
        'conv_b': nrm(ks[7], (L, CONV_CH), 0.02),
        'conv_norm_g': gain(ks[8], (L, CONV_CH)),
        'conv_norm_b': nrm(ks[9], (L, CONV_CH), 0.02),
        'diff_qnorm_g': gain(ks[10], (L, DIFF_D)),
        'diff_knorm_g': gain(ks[11], (L, DIFF_D)),
        'diff_lq1': nrm(ks[12], (L, DIFF_D), 0.1),
        'diff_lk1': nrm(ks[13], (L, DIFF_D), 0.1),
        'diff_lq2': nrm(ks[14], (L, DIFF_D), 0.1),
        'diff_lk2': nrm(ks[15], (L, DIFF_D), 0.1),
        'diff_subln_g': gain(ks[16], (L, 2 * DIFF_D)),
        'w_out': nrm(ks[17], (L, D_MIX_2, D), D_MIX_2 ** -0.5),
        'ffn_norm_g': gain(ks[18], (L, D)),
        'router_group_w': nrm(ks[19], (L, D, N_GROUPS), D ** -0.5),
        'router_group_b': nrm(ks[20], (L, N_GROUPS), 0.01),
        'router_expert_w': nrm(ks[21], (L, D, N_EXPERTS), D ** -0.5),
        'router_expert_b': nrm(ks[22], (L, N_EXPERTS), 0.01),
        'expert_w_gate': nrm(ks[23], (L, N_EXPERTS, D, D_EXPERT), D ** -0.5),
        'expert_w_up': nrm(ks[24], (L, N_EXPERTS, D, D_EXPERT), D ** -0.5),
        'expert_w_down': nrm(ks[25], (L, N_EXPERTS, D_EXPERT, D), D_EXPERT ** -0.5),
    }

def second_block(x, mix_norm_g, w_in, gla_gate_w, gla_gate_b, gla_norm_g, conv_w, conv_b,
              conv_norm_g, conv_norm_b, diff_qnorm_g, diff_knorm_g, diff_lq1, diff_lk1,
              diff_lq2, diff_lk2, diff_subln_g, w_out, ffn_norm_g, router_group_w,
              router_group_b, router_expert_w, router_expert_b, expert_w_gate, expert_w_up,
              expert_w_down):
    offsets = [int(o) for o in np.cumsum(IN_SPLITS_2)[:-1]]
    for l in range(DEPTH_2):
        hn = rms_norm(x, mix_norm_g[l])
        proj = hn @ w_in[l]
        gq, gk, gv, glr, gog, cu, dq, dk, dv = jnp.split(proj, offsets, axis=-1)
        o_gla = gla_mixer(gq, gk, gv, glr, gog, gla_gate_w[l], gla_gate_b[l], gla_norm_g[l])
        o_conv = conv_mixer(cu, conv_w[l], conv_b[l], conv_norm_g[l], conv_norm_b[l])
        lambda_init = 0.8 - 0.6 * math.exp(-0.3 * l)
        o_diff = diff_attention(dq, dk, dv, diff_qnorm_g[l], diff_knorm_g[l], diff_lq1[l],
                                diff_lk1[l], diff_lq2[l], diff_lk2[l], diff_subln_g[l], lambda_init)
        mix = jnp.concatenate([o_gla, o_conv, o_diff], axis=-1)
        x = x + mix @ w_out[l]
        x = x + hier_moe(rms_norm(x, ffn_norm_g[l]), router_group_w[l], router_group_b[l],
                         router_expert_w[l], router_expert_b[l], expert_w_gate[l],
                         expert_w_up[l], expert_w_down[l])
    return x


def setup_inputs(seed=0):
    out = dict(first_inputs(seed))
    for name, value in second_inputs(seed + 1).items():
        if name != "x":
            out[name + "_2"] = value
    return out


def reference(
    x, pre_mix_norm, w_in, dn_conv, dn_a_log, dn_dt_bias, dn_out_norm, w_out, post_mix_norm,
    pre_ffn_norm, ffn_up, ffn_conv, ffn_conv_bias, ffn_down, post_ffn_norm, mix_norm_g_2,
    w_in_2, gla_gate_w_2, gla_gate_b_2, gla_norm_g_2, conv_w_2, conv_b_2, conv_norm_g_2,
    conv_norm_b_2, diff_qnorm_g_2, diff_knorm_g_2, diff_lq1_2, diff_lk1_2, diff_lq2_2,
    diff_lk2_2, diff_subln_g_2, w_out_2, ffn_norm_g_2, router_group_w_2, router_group_b_2,
    router_expert_w_2, router_expert_b_2, expert_w_gate_2, expert_w_up_2, expert_w_down_2,
):
    x = first_block(
        x, pre_mix_norm, w_in, dn_conv, dn_a_log, dn_dt_bias, dn_out_norm, w_out, post_mix_norm,
        pre_ffn_norm, ffn_up, ffn_conv, ffn_conv_bias, ffn_down, post_ffn_norm,
    )
    return second_block(
        x, mix_norm_g_2, w_in_2, gla_gate_w_2, gla_gate_b_2, gla_norm_g_2, conv_w_2, conv_b_2,
        conv_norm_g_2, conv_norm_b_2, diff_qnorm_g_2, diff_knorm_g_2, diff_lq1_2, diff_lk1_2,
        diff_lq2_2, diff_lk2_2, diff_subln_g_2, w_out_2, ffn_norm_g_2, router_group_w_2,
        router_group_b_2, router_expert_w_2, router_expert_b_2, expert_w_gate_2, expert_w_up_2,
        expert_w_down_2,
    )


_drawn_inputs = setup_inputs


def setup_inputs(seed=0):
    import zlib

    import numpy as np

    out = dict(_drawn_inputs(seed))
    spreads = {}
    factors = {'post_ffn_norm': 2.752,
     'mix_norm_g_2': 5.645,
     'gla_gate_b_2': 8.0,
     'gla_norm_g_2': 42.7,
     'conv_b_2': 29.059,
     'conv_norm_g_2': 200.0,
     'conv_norm_b_2': 200.0,
     'diff_qnorm_g_2': 8.0,
     'diff_knorm_g_2': 8.0,
     'diff_lq2_2': 8.0,
     'diff_lk2_2': 8.0,
     'diff_subln_g_2': 153.756,
     'ffn_norm_g_2': 16.119,
     'router_group_b_2': 109.532,
     'router_expert_b_2': 135.128}
    for name, (base, spread) in spreads.items():
        noise = np.random.default_rng([zlib.crc32(name.encode()), seed]).standard_normal(out[name].shape)
        drawn = base * np.exp(spread * noise) if base else spread * noise
        out[name] = __import__('jax').numpy.asarray(drawn.astype(out[name].dtype))
    for name, factor in factors.items():
        out[name] = (out[name] * factor).astype(out[name].dtype)
    return out
```

```python
from contextlib import ExitStack

import concourse.bass as bass
import numpy as np
from concourse import mybir

ALU = mybir.AluOpType
ACT = mybir.ActivationFunctionType
AX_X = mybir.AxisListType.X
F32 = mybir.dt.float32

P = 128
S = 256
NT = S // P
D = 1024
KD = D // P
DEPTH = 2
EPS = 1e-6
NEG = -1e30

DNH, CONV = 4, 4
FF = 2816
NP_FF = FF // P
FCONV = 3
SWAH, SWAD = 8, 64
DIL = ((128, 1), (512, 4), (2048, 16))
ROPE_THETA, ROPE_DIM = 500000.0, 16
LEVELS = 7

GH, GDK, GDV, GRANK, GTAU = 4, 32, 64, 16, 16.0
GB = 32
NGB = S // GB
CW = 31
DFH = 4
LAMBDA_INIT = 0.2
NG, NEG_E, NE = 4, 4, 16
NR = NG + NE

RING = 6
T_Z, T_BQ, T_BV, T_WOUT, T_UP, T_DOWN = 12, 16, 24, 28, 36, 80
LAYER_TILES = T_DOWN + NP_FF * KD // 8
LAYER_ROUNDS = LAYER_TILES // RING
T2 = DEPTH * LAYER_TILES
U_CONV, U_GOG, U_GV, U_DQ, U_DV, U_WOUT, U_EXP = 2, 6, 8, 10, 18, 22, 30
ALL_TILES = T2 + U_EXP + NE * RING
assert LAYER_TILES % RING == 0 and (T2 + U_EXP) % RING == 0 and T_UP % RING == 0
PAIRS = RING // 2
FFN_LOOPS = NP_FF // PAIRS
CREDITS = PAIRS
EX_CREDITS = 2
NORM2 = DEPTH * 4
CONV_VALUES = (U_CONV, U_CONV + 2)


def evacuated(u):
    return sum(i not in CONV_VALUES for i in range(u + 1))


def columns(*widths):
    at, out = 0, {}
    for name, w in widths:
        out[name] = (at, at + w)
        at += w
    return out, at


C_COLS, C_W = columns(
    ("ident", P), ("ones", P), ("bd64", P), ("rot", P), ("cos", S), ("sin", S), ("decmask", P),
    ("level", LEVELS * P), ("dilmask", 3 * P), ("causal", 3 * P), ("eps", 1), ("gmask", GB),
    ("selhead", GH), ("first4", 4), ("ones256", S))
A_COLS, A_W = columns(
    ("pre", KD), ("conv", 12 * CONV), ("onorm", 1), ("alog", 1), ("dt", 1), ("post", KD), ("wba", KD * 64))
F_COLS, F_W = columns(("pre", KD), ("conv", NP_FF * 2 * FCONV), ("bias", NP_FF * 2), ("post", KD))
B_COLS, B_W = columns(
    ("mix", KD), ("ffn", KD), ("wglr", KD * GRANK), ("wrt", KD * NR), ("glab", 1), ("glan", 1),
    ("convw", 2 * CW), ("convb", 2), ("cng", 2), ("cnb", 2), ("qn", 1), ("kn", 1), ("lam", 4),
    ("subln", 1), ("gatew", P), ("rbias", NR))

DVE_LINKS, POOL_LINKS = 106, 4
FFN_LINKS = 4


class Chain:

    def __init__(self, engine, sem, start):
        self.engine, self.sem, self.start, self.n = engine, sem, start, 0

    def mark(self, ins):
        self.n += 1
        ins.then_inc(self.sem, 1)

    def dep(self):
        self.engine.wait_ge(self.sem, self.start + self.n)


class Arena:

    def __init__(self, region, width):
        self.region, self.width, self.at = region, width, 0

    def take(self, *shape):
        n = int(np.prod(shape))
        assert self.at + n <= self.width, (self.at, n, self.width)
        v = self.region[:, self.at:self.at + n]
        self.at += n
        names = " ".join("abcd"[:len(shape)])
        sizes = {k: s for k, s in zip("abcd", shape)}
        return v if len(shape) == 1 else v.rearrange(f"p ({names}) -> p {names}", **sizes)


def block_program(nc, xt, wtiles, consts, packa, packf, packb, out):
    v, a, pl, t = nc.vector, nc.scalar, nc.gpsimd, nc.tensor
    ctx = ExitStack()
    with ctx:
        def sb(name, *shape):
            return ctx.enter_context(nc.sbuf_tensor(name, [P, *shape], F32))

        def sem(name):
            return ctx.enter_context(nc.semaphore(name))

        x = sb("x", KD, S)
        h = sb("h", KD, S)
        sq = sb("sq", KD, S)
        y = sb("y", KD, S)
        ring = sb("ring", RING, 1024)
        cst = sb("cst", C_W)
        pa = sb("pa", A_W)
        pf = sb("pf", F_W)
        pb = sb("pb", B_W)
        std = sb("std", S)
        rstd = sb("rstd", S)
        mix = sb("mix", KD, S)
        ARENA = 29700
        credit = sb("credit", 16)
        region = sb("region", ARENA)

        ar = Arena(region, ARENA)
        qkvc = ar.take(12, S)
        qkvs = ar.take(12, S)
        sqk = ar.take(8, S)
        ropet = ar.take(8, S)
        raw = ar.take(8, S)
        zs = ar.take(DNH, S)
        vtok = ar.take(NT, 512)
        rows = ar.take(S)
        cols = ar.take(NT, 64)
        rin = ar.take(8, S)
        gam = ar.take(DNH, S)
        bbc = ar.take(DNH, S)
        spt = region[:, ar.at - 8 * S:ar.at - 2 * S].rearrange("p (j s) -> p j s", j=6)
        eg1 = ar.take(DNH, P)
        kbg = ar.take(DNH, P)
        qg = ar.take(DNH, P)
        bp = ar.take(DNH * NT, P)
        qkt = ar.take(DNH * NT, P)
        vb = ar.take(DNH * NT, P)
        kd = ar.take(DNH, P)
        uinv = ar.take(DNH * NT, P)
        vnew = ar.take(2, DNH, P)
        st1 = ar.take(DNH, P)
        resid = ar.take(DNH, P)
        ot = ar.take(DNH, S)
        att_max = ar.take(16)
        att_z = ar.take(16)
        att_rz = ar.take(16)
        pt = ar.take(2, 3 * P)
        prob = region[:, 24 * S:24 * S + 8 * 3 * P].rearrange("p (i k) -> p i k", i=8)
        qkn = qkvc[:, 0:8, :]
        units = dict(u=DNH * NT, k=P)
        tinv = region[:, 24 * S:28 * S].rearrange("p (u k) -> p u k", **units)
        xs = region[:, 28 * S:32 * S].rearrange("p (u k) -> p u k", **units)
        bl = region[:, 32 * S:40 * S].rearrange("p (w u k) -> p w u k", w=2, **units)

        ar = Arena(region, ARENA)
        hid = ar.take(NP_FF * S)
        glu_g = ar.take(PAIRS, S)
        glu_v = ar.take(PAIRS, S)
        glu_a = ar.take(PAIRS, S)

        ar = Arena(region, ARENA)
        g_q = ar.take(S)
        g_k = ar.take(S)
        g_og = ar.take(2, S)
        g_v = ar.take(NT, S)
        g_lr = ar.take(S)
        g_c = ar.take(S)
        g_b = ar.take(S)
        g_ki = ar.take(NGB - 1, S)
        g_ke = ar.take(NGB - 1, S)
        g_qe = ar.take(S)
        g_pr = ar.take(GB, P)
        g_st = ar.take(GH, NT, S)
        g_o = ar.take(2, S)
        g_sq = ar.take(2, S)
        g_std = ar.take(2, S)
        g_rs = ar.take(2, S)
        c_sg = ar.take(2, S)
        c_z = ar.take(2, S + CW - 1)
        c_y = ar.take(2, S)
        c_sq = ar.take(2, S)
        c_std = ar.take(2, S)
        c_rs = ar.take(2, S)
        d_raw = ar.take(8, S)
        d_sq = ar.take(8, S)
        d_std = ar.take(8, S)
        d_v = ar.take(NT, 512)
        d_prob = ar.take(8, 3 * P)
        g_sp = region[:, ar.at - 24 * P:ar.at - 12 * P].rearrange("p (j s) -> p j s", j=6)
        d_max = ar.take(16)
        d_z = ar.take(16)
        d_rz = ar.take(16)
        d_pt = ar.take(2, 3 * P)
        d_o, d_osq, d_ostd = y[:, 0:4, :], sq[:, 0:4, :], sq[:, 4:8, :]
        lam_p = ar.take(2)
        lam_e = ar.take(2)
        nlam = ar.take(1)
        ngb = ar.take(1)
        ar = Arena(region, ARENA)
        r_log = ar.take(NT, NR)
        r_max = ar.take(NT)
        r_eq = ar.take(NT, 4)
        r_w = ar.take(NT, 4)
        r_m2 = ar.take(NT)
        r_oh = ar.take(NT, 4)
        r_e = ar.take(NT, 4)
        r_sum = ar.take(NT)
        r_pg = ar.take(NT)
        r_pro = ar.take(NT, 16)
        r_sel = ar.take(NT, 4)
        r_l1 = ar.take(NT)
        r_o1 = ar.take(NT, 4)
        r_s2 = ar.take(NT, 4)
        r_l2 = ar.take(NT)
        r_o2 = ar.take(NT, 4)
        r_d = ar.take(NT)
        r_e2 = ar.take(NT)
        r_u = ar.take(NT)
        r_w1 = ar.take(NT)
        r_w2 = ar.take(NT)
        r_t1 = ar.take(NT, 4)
        r_t2 = ar.take(NT, 4)
        r_gate = ar.take(NT, NE)
        gate_t = ar.take(S)
        gate_bc = ar.take(NE * S)
        e_act = ar.take(2, S)
        e_up = ar.take(2, S)
        e_hid = ar.take(2, S)

        bank = [ctx.enter_context(nc.psum_tensor(f"bank{i}", [P, 512], F32)) for i in range(8)]

        def cc(name, i=0, w=None, rows_=slice(0, P)):
            first, end = C_COLS[name]
            w = end - first if w is None else w
            return cst[rows_, first + i * w:first + (i + 1) * w]

        def pa_(name, i=0, w=1, rows_=slice(0, P)):
            return pa[rows_, A_COLS[name][0] + i:A_COLS[name][0] + i + w]

        def pf_(name, i=0):
            return pf[:, bass.ds(F_COLS[name][0] + i, 1)]

        def pb_(name, i=0, w=1, rows_=slice(0, P)):
            return pb[rows_, B_COLS[name][0] + i:B_COLS[name][0] + i + w]

        ident, ones, bd64, eps = cc("ident"), cc("ones"), cc("bd64"), cc("eps")

        x_in, consts_in, packb_in = sem("x_in"), sem("consts_in"), sem("packb_in")
        packa_in, packf_in = sem("packa_in"), sem("packf_in")
        w_in = [sem(f"w_in{i}") for i in range(RING)]
        tile_done = sem("tile_done")
        dve_chain, pool_chain = sem("dve_chain"), sem("pool_chain")
        norm_sq, norm_sum, norm_std, norm_out = (sem(f"norm_{n}") for n in ("sq", "sum", "std", "out"))
        conv_ready = sem("conv_ready")
        silu_ready = sem("silu_ready")
        sqk_ready = sem("sqk_ready")
        proj_evac = sem("proj_evac")
        ba_done = sem("ba_done")
        sp_act, sp_dve = sem("sp_act"), sem("sp_dve")
        beta_ready = sem("beta_ready")
        decay_ready = sem("decay_ready")
        rows_ready = sem("rows_ready")
        l2_sum, l2_std, qk_ready = sem("l2_sum"), sem("l2_std"), sem("qk_ready")
        rope_rot, rope_used, rope_done = sem("rope_rot"), sem("rope_used"), sem("rope_done")
        cols_done, cols_ready = sem("cols_done"), sem("cols_ready")
        bc_done, bc_act, bc_dve = sem("bc_done"), sem("bc_act"), sem("bc_dve")
        gam_ready, gb_ready, kbg_ready = sem("gam_ready"), sem("gb_ready"), sem("kbg_ready")
        gram_done, gram_used = sem("gram_done"), sem("gram_used")
        tr_done, tr_dve, tr_act = sem("tr_done"), sem("tr_dve"), sem("tr_act")
        bl_ready = sem("bl_ready")
        lev_x, lev_xs, lev_y, tu_ready = sem("lev_x"), sem("lev_xs"), sem("lev_y"), sem("tu_ready")
        rec_pe, rec_act, rec_dve = sem("rec_pe"), sem("rec_act"), sem("rec_dve")
        on_sum, on_std, mix_a = sem("on_sum"), sem("on_std"), sem("mix_a")
        att_s, att_sm, att_p, att_pn = (sem(f"att_{n}") for n in ("s", "sm", "p", "pn"))
        att_t, att_pt, att_pv, att_o = (sem(f"att_{n}") for n in ("t", "pt", "pv", "o"))
        y_done = sem("y_done")
        ffn_free = sem("ffn_free")
        ffn_chain = sem("ffn_chain")
        glu_ready, gelu_done, hid_done = sem("glu_ready"), sem("gelu_done"), sem("hid_done")
        rows_zero = sem("rows_zero")
        dve_chain2 = sem("dve_chain2")
        lr_done, lr_ready, gz_done, ngb_ready, gc_ready = (sem(f"gla_{n}") for n in ("lr_done", "lr_ready", "gz", "nb", "c"))
        u_evac, cz_zero, cz_ready, cy_ready = sem("u_evac"), sem("cz_zero"), sem("cz_ready"), sem("cy_ready")
        dsq_ready, dn_sum, dn_std, dn_ready = sem("dsq_ready"), sem("dn_sum"), sem("dn_std"), sem("dn_ready")
        lam_ready, lam_sum, lam_exp = sem("lam_ready"), sem("lam_sum"), sem("lam_exp")
        ge_ready, ki_zero, ki_ready = sem("ge_ready"), sem("ki_zero"), sem("ki_ready")
        st_zero, st_done, st_copied = sem("st_zero"), sem("st_done"), sem("st_copied")
        pr_sub, pr_min, pr_exp, pr_q, pr_ready = (sem(f"pr_{n}") for n in ("sub", "min", "exp", "q", "ready"))
        dg_done, dg_ready = sem("dg_done"), sem("dg_ready")
        go_done, go_sq, gn_sum, gn_std, gla_mix = (sem(f"go_{n}") for n in ("done", "sq", "sum", "std", "mix"))
        df_s, df_sm, df_p, df_pn, df_t, df_pt, df_pv, df_o = (
            sem(f"df_{n}") for n in ("s", "sm", "p", "pn", "t", "pt", "pv", "o"))
        do_sum, do_std, diff_mix = sem("do_sum"), sem("do_std"), sem("diff_mix")
        cm_done, cc_ready, csq_ready, cv_done, cv_std, cn_ready, conv_mix = (
            sem(f"conv_{n}") for n in ("mean", "centred", "sq", "var", "std", "norm", "mix"))
        x_added, rt_done, r_sub, r_exp, gates_ready = (sem(f"route_{n}") for n in ("x", "logits", "sub", "exp", "gates"))
        gt_done, gt_ready, gbc_done, gbc_ready = sem("gt_done"), sem("gt_ready"), sem("gbc_done"), sem("gbc_ready")
        ex_act, ex_up, ex_hid, ex_add = (sem(f"ex_{n}") for n in ("act", "up", "hid", "add"))
        out_done = sem("out_done")

        def second_tensor(pe, tile_in, project, project_tokens, sum_squares, transpose, scores):
            def tile2(u):
                tile_in((T2 + u) % RING, (T2 + u) // RING)
                return (T2 + u) % RING

            sum_squares(NORM2)
            pe.wait_ge(norm_out, NORM2 + 1)
            pe.wait_ge(packb_in, 16)
            for k in range(KD):
                mm = t.matmul(bank[5][0:GRANK, 0:S], pb_("wglr", k * GRANK, GRANK), h[:, k, :],
                              start=k == 0, stop=k == KD - 1)
            mm.then_inc(lr_done, 1)
            for u in range(U_WOUT):
                s = tile2(u)
                if u >= 4:
                    if u - 4 in CONV_VALUES:
                        pe.wait_ge(cz_ready, CONV_VALUES.index(u - 4) + 1)
                    else:
                        pe.wait_ge(u_evac, evacuated(u - 4))
                if U_GV <= u < U_DQ or u >= U_DV:
                    project_tokens(s, bank[u % 4])
                else:
                    project(s, bank[u % 4][:, 0:S])
                if u == 2:
                    pe.wait_ge(lr_ready, 1)
                    t.matmul(bank[5][:, S:2 * S], pb_("gatew", 0, P, slice(0, GRANK)), g_lr[0:GRANK, :],
                             start=True, stop=True).then_inc(gz_done, 1)
                if U_DQ + 2 <= u < U_DQ + 10:
                    i = u - U_DQ - 2
                    pe.wait_ge(dsq_ready, i + 1)
                    if i >= 2:
                        pe.wait_ge(dn_std, i - 1)
                    t.matmul(bank[6 + i % 2][:, 0:S], bd64, d_sq[:, i, :], start=True, stop=True).then_inc(dn_sum, 1)
            pe.wait_ge(lam_ready, 1)
            pe.wait_ge(dn_std, 8)
            t.matmul(bank[6][:, 0:2], ones[0:64, :], lam_p[0:64, :], start=True, stop=True).then_inc(lam_sum, 1)

            pe.wait_ge(u_evac, evacuated(U_WOUT - 1))
            pe.wait_ge(ki_ready, 1)
            for i in range(GH):
                ch_ = slice(GDK * i, GDK * i + GDK)
                for jt in range(NT):
                    for b in range(1 + jt * (P // GB), NGB):
                        mm = t.matmul(bank[i][:, jt * S + b * GB:jt * S + (b + 1) * GB],
                                      g_ki[ch_, b - 1, jt * P:(jt + 1) * P], g_qe[ch_, b * GB:(b + 1) * GB],
                                      start=True, stop=True)
                mm.then_inc(st_done, 1)
            for jt in range(NT):
                pe.wait_ge(pr_ready, jt + 1)
                for r in range(GB):
                    mm = t.matmul(bank[4][:, jt * P + r * GH:jt * P + (r + 1) * GH], g_pr[:, r, :], cc("selhead"),
                                  start=True, stop=True)
                mm.then_inc(dg_done, 1)
            pe.wait_ge(dg_ready, 1)
            pe.wait_ge(st_copied, 2 * GH)
            for i in range(GH):
                o_ = bank[5][64 * (i % 2):64 * (i % 2) + 64, i // 2 * S:i // 2 * S + S]
                vals = g_v[:, :, i * GDV:(i + 1) * GDV]
                t.matmul(o_[:, 0:P], vals[:, 0, :], g_st[:, i, 0, 0:P], start=True, stop=True)
                t.matmul(o_[:, P:S], vals[:, 0, :], g_st[:, i, 0, P:S], start=True, stop=False)
                mm = t.matmul(o_[:, P:S], vals[:, 1, :], g_st[:, i, 1, P:S], start=False, stop=True)
            mm.then_inc(go_done, 1)

            pe.wait_ge(dn_ready, 8)
            for i in range(8 + 5):
                if i < 8:
                    if i >= 2:
                        pe.wait_ge(df_sm, i - 1)
                    scores(i, d_raw[:, 0:4, :], d_raw[:, 4:8, :], bank[2 + i % 2]).then_inc(df_s, 1)
                if i == 4:
                    pe.wait_ge(go_sq, 2)
                    for j in range(2):
                        mm = t.matmul(bank[4][:, j * S:(j + 1) * S], bd64, g_sq[:, j, :], start=True, stop=True)
                    mm.then_inc(gn_sum, 1)
                j, odd = divmod(i - 3, 2)
                if 0 <= j < DFH and odd == 0:
                    pe.wait_ge(df_pn, j + 1)
                    if j >= 2:
                        pe.wait_ge(df_pt, j - 1)
                    if j == 0:
                        pe.wait_ge(lam_exp, 1)
                    b = bank[6 + j % 2]
                    transpose(b[:, 0:P], d_prob[:, 2 * j, 0:P])
                    transpose(b[:, P:2 * P], d_prob[:, 2 * j, P:2 * P])
                    transpose(b[:, 2 * P:3 * P], d_prob[:, 2 * j, 2 * P:3 * P]).then_inc(df_t, 1)
                j, odd = divmod(i - 4, 2)
                if 0 <= j < DFH and odd == 0:
                    pe.wait_ge(df_pt, j + 1)
                    if j >= 2:
                        pe.wait_ge(df_o, 2 * j - 2)
                    o_ = bank[j % 2]
                    vals = d_v[:, :, j * P:(j + 1) * P]
                    t.matmul(o_[:, 0:P], vals[:, 0, :], d_pt[:, j % 2, 0:P], start=True, stop=True)
                    t.matmul(o_[:, P:S], vals[:, 0, :], d_pt[:, j % 2, P:2 * P], start=True, stop=False)
                    t.matmul(o_[:, P:S], vals[:, 1, :], d_pt[:, j % 2, 2 * P:3 * P], start=False,
                             stop=True).then_inc(df_pv, 1)
            pe.wait_ge(cy_ready, 1)
            pe.wait_ge(df_sm, 8)
            for j in range(2):
                mm = t.matmul(bank[2][:, j * S:(j + 1) * S], bd64, c_y[:, j, :], start=True, stop=True)
            mm.then_inc(cm_done, 1)
            pe.wait_ge(df_o, 2 * DFH)
            for g in range(2):
                t.matmul(bank[g][:, :], ones, d_osq[:, 2 * g:2 * g + 2, :], start=True, stop=True).then_inc(do_sum, 1)
            pe.wait_ge(csq_ready, 2)
            for j in range(2):
                mm = t.matmul(bank[3][:, j * S:(j + 1) * S], bd64, c_sq[:, j, :], start=True, stop=True)
            mm.then_inc(cv_done, 1)

            pe.wait_ge(gla_mix, 1)
            pe.wait_ge(conv_mix, 2)
            pe.wait_ge(diff_mix, 2)
            for m in range(KD):
                s = tile2(U_WOUT + m)
                if m >= 4:
                    pe.wait_ge(x_added, m - 3)
                for k in range(KD):
                    mm = t.matmul(bank[m % 4][:, 0:S], ring[:, s, k * P:(k + 1) * P], mix[:, k, :],
                                  start=k == 0, stop=k == KD - 1)
                mm.then_inc(tile_done, 1)

            sum_squares(NORM2 + 1)
            pe.wait_ge(norm_out, NORM2 + 2)
            for c in range(NT):
                for k in range(KD):
                    t.matmul(bank[5][:, c * NR:(c + 1) * NR], h[:, k, c * P:(c + 1) * P], pb_("wrt", k * NR, NR),
                             start=k == 0, stop=False)
                mm = t.matmul(bank[5][:, c * NR:(c + 1) * NR], ones[0:1, :], pb_("rbias", 0, NR, slice(0, 1)),
                              start=False, stop=True)
            mm.then_inc(rt_done, 1)

            def expert_up(e, places, rnd):
                for j, s in enumerate(places):
                    tile_in(s, rnd + (1 if s < places[0] else 0))
                    if places[0] == 0:
                        pass
                    elif j < 2:
                        pe.wait_ge(ex_act, 2 * e + j - 1)
                    else:
                        pe.wait_ge(ex_up, 2 * e + j - 3)
                    project(s, bank[j][:, 0:S])

            def expert_down(e, places, rnd):
                pe.wait_ge(ex_hid, 2 * e + 2 + EX_CREDITS)
                for j, s in enumerate(places):
                    tile_in(s, rnd)
                    for m in range(4 * j, 4 * j + 4):
                        if m % 2 == 0:
                            pe.wait_ge(ex_add, 4 * e + m // 2 + 1)
                        for k in range(2):
                            part = (m % 4) * 2 + k
                            mm = t.matmul(bank[4 + m // 2][:, m % 2 * S:m % 2 * S + S], ring[:, s, part * P:(part + 1) * P],
                                          e_hid[:, k, :], start=k == 0, stop=k == 1)
                    mm.then_inc(tile_done, 1)

            first = (T2 + U_EXP) // RING
            expert_up(0, (0, 1, 2, 3), first)
            pe.wait_ge(gates_ready, 1)
            for c in range(NT):
                mm = transpose(bank[4][0:NE, c * P:(c + 1) * P], r_gate[:, c, :])
            mm.then_inc(gt_done, 1)
            pe.wait_ge(gt_ready, 1)
            for i in range(NE // 2):
                if i >= 2:
                    pe.wait_ge(gbc_ready, i - 1)
                for j in range(2):
                    mm = t.matmul(bank[6 + i % 2][:, j * S:(j + 1) * S],
                                  ident[0:NE, 2 * i + j:2 * i + j + 1].to_broadcast([NE, P]), gate_t[0:NE, :],
                                  start=True, stop=True)
                mm.then_inc(gbc_done, 1)
            with pe.Fori(0, NE - 1) as e:
                expert_up(e + 1, (4, 5, 0, 1), first + e)
                expert_down(e, (2, 3), first + e + 1)
            expert_down(NE - 1, (4, 5), first + NE - 1)

        def second_scalar(act, pre_norm, softplus):
            pre_norm(NORM2)
            act.wait_ge(lr_done, 1)
            a.activation(g_lr[0:GRANK, :], bank[5][0:GRANK, 0:S], ACT.Copy).then_inc(lr_ready, 1)
            act.wait_ge(packb_in, 16)
            for u in range(U_WOUT):
                if u in CONV_VALUES:
                    continue
                act.wait_ge(tile_done, T2 + u + 1)
                src = bank[u % 4]
                halves = src[:, 0:S].rearrange("p (c d) -> p c d", c=NT)
                if u < 2:
                    a.activation((g_q, g_k)[u], src[:, 0:S], ACT.Copy, scale=(GDK ** -0.5, 1.0)[u]).then_inc(u_evac, 1)
                elif u < U_GOG:
                    a.activation(c_sg[:, u // 2 - 1, :], src[:, 0:S], ACT.Sigmoid).then_inc(u_evac, 1)
                elif u < U_GV:
                    a.activation(g_og[:, u - U_GOG, :], src[:, 0:S], ACT.Silu).then_inc(u_evac, 1)
                elif u < U_DQ:
                    j = u - U_GV
                    a.activation(g_v[:, :, j * P:(j + 1) * P], halves, ACT.Copy).then_inc(u_evac, 1)
                elif u < U_DV:
                    i = u - U_DQ
                    a.activation(d_sq[:, i, :], src[:, 0:S], ACT.Square).then_inc(dsq_ready, 1)
                    a.activation(d_raw[:, i, :], src[:, 0:S], ACT.Copy).then_inc(u_evac, 1)
                else:
                    j = u - U_DV
                    a.activation(d_v[:, :, j * P:(j + 1) * P], halves, ACT.Copy).then_inc(u_evac, 1)
                if u == U_GOG - 1:
                    act.wait_ge(ngb_ready, 1)
                    softplus(DEPTH, bank[5][:, S:2 * S], (gz_done, 1), ngb, -1.0, g_sp, 0, P)
                if u == U_GV + 1:
                    act.wait_ge(gc_ready, 1)
                    for b in range(1, NGB):
                        end = b * GB - 1
                        a.activation(g_ke[:, b - 1, 0:b * GB], g_c[:, 0:b * GB], ACT.Exp, bias=g_b[:, end:end + 1])
                        ins = a.activation(g_qe[:, b * GB:(b + 1) * GB], g_c[:, b * GB:(b + 1) * GB], ACT.Exp,
                                           bias=g_c[:, end:end + 1], scale=-1.0)
                    ins.then_inc(ge_ready, 1)
                if U_DQ + 2 <= u < U_DQ + 10:
                    i = u - U_DQ - 2
                    act.wait_ge(dn_sum, i + 1)
                    a.activation(d_std[:, i, :], bank[6 + i % 2][:, 0:S], ACT.Sqrt, bias=eps,
                                 scale=1.0 / 64).then_inc(dn_std, 1)
            act.wait_ge(lam_sum, 1)
            a.activation(lam_e[:], bank[6][:, 0:2], ACT.Exp).then_inc(lam_exp, 1)
            act.wait_ge(pr_min, 1)
            a.activation(g_pr[:], g_pr[:], ACT.Exp).then_inc(pr_exp, 1)
            act.wait_ge(st_zero, 1)
            for i in range(GH):
                act.wait_ge(st_done, i + 1)
                a.activation(g_st[:, i, 0, GB:S], bank[i][:, GB:S], ACT.Copy).then_inc(st_copied, 1)
                a.activation(g_st[:, i, 1, P + GB:S], bank[i][:, S + P + GB:2 * S], ACT.Copy).then_inc(st_copied, 1)
            act.wait_ge(pr_min, 2)
            a.activation(g_pr[:], g_pr[:], ACT.Exp).then_inc(pr_exp, 1)
            act.wait_ge(go_done, 1)
            outs = bank[5][:, :].rearrange("p (j s) -> p j s", j=2)
            a.activation(g_sq[:], outs, ACT.Square).then_inc(go_sq, 1)
            a.activation(g_o[:], outs, ACT.Copy).then_inc(go_sq, 1)
            for i in range(8 + 5):
                if i < 8:
                    act.wait_ge(df_sm, i + 1)
                    a.activation(d_prob[:, i, 0:P], d_prob[:, i, 0:P], ACT.Exp, bias=d_max[:, 2 * i:2 * i + 1],
                                 accum_out=d_z[:, 2 * i:2 * i + 1])
                    a.activation(d_prob[:, i, P:3 * P], d_prob[:, i, P:3 * P], ACT.Exp,
                                 bias=d_max[:, 2 * i + 1:2 * i + 2],
                                 accum_out=d_z[:, 2 * i + 1:2 * i + 2]).then_inc(df_p, 1)
                j, odd = divmod(i - 3, 2)
                if 0 <= j < DFH and odd == 0:
                    act.wait_ge(df_t, j + 1)
                    if j >= 2:
                        act.wait_ge(df_pv, j - 1)
                    a.activation(d_pt[:, j % 2, :], bank[6 + j % 2][:, 0:3 * P], ACT.Copy).then_inc(df_pt, 1)
                j, odd = divmod(i - 4, 2)
                if 0 <= j < DFH and odd == 0:
                    act.wait_ge(df_pv, j + 1)
                    a.activation(d_osq[:, j, :], bank[j % 2][:, 0:S], ACT.Square).then_inc(df_o, 1)
                    a.activation(d_o[:, j, :], bank[j % 2][:, 0:S], ACT.Copy).then_inc(df_o, 1)
            act.wait_ge(gn_sum, 1)
            a.activation(g_std[:], bank[4][:, :].rearrange("p (j s) -> p j s", j=2), ACT.Sqrt, bias=eps,
                         scale=1.0 / GDV).then_inc(gn_std, 1)
            for g in range(2):
                act.wait_ge(do_sum, g + 1)
                a.activation(d_ostd[:, 2 * g:2 * g + 2, :], bank[g][:, :].rearrange("p (j s) -> p j s", j=2), ACT.Sqrt,
                             bias=eps, scale=1.0 / P).then_inc(do_std, 1)
            for j in range(2):
                act.wait_ge(cc_ready, j + 1)
                a.activation(c_sq[:, j, :], c_y[:, j, :], ACT.Square).then_inc(csq_ready, 1)
            act.wait_ge(cv_done, 1)
            a.activation(c_std[:], bank[3][:, :].rearrange("p (j s) -> p j s", j=2), ACT.Sqrt, bias=eps,
                         scale=1.0 / 64).then_inc(cv_std, 1)
            for j in range(2):
                act.wait_ge(cn_ready, j + 1)
                a.activation(mix[:, 2 + j, :], c_y[:, j, :], ACT.Silu, bias=pb_("cnb", j),
                             scale=pb_("cng", j)).then_inc(conv_mix, 1)
            act.wait_ge(x_added, KD)
            pre_norm(NORM2 + 1)

            act.wait_ge(r_sub, 1)
            a.activation(r_e[:], r_e[:], ACT.Exp).then_inc(r_exp, 1)
            act.wait_ge(r_sub, 2)
            a.activation(r_e2[:], r_d[:], ACT.Exp).then_inc(r_exp, 1)
            act.wait_ge(gt_done, 1)
            a.activation(gate_t[0:NE, :], bank[4][0:NE, 0:S], ACT.Copy).then_inc(gt_ready, 1)
            for i in range(NE // 2):
                act.wait_ge(gbc_done, i + 1)
                a.activation(gate_bc[:, 2 * i * S:2 * (i + 1) * S], bank[6 + i % 2][:, :], ACT.Copy).then_inc(gbc_ready, 1)

            def expert(e, done):
                for j in range(2):
                    act.wait_ge(tile_done, T2 + U_EXP + done + j + 1)
                    act.wait_ge(ex_hid, 2 * e + j + 1)
                    a.activation(e_act[:, j, :], bank[j][:, 0:S], ACT.Silu).then_inc(ex_act, 1)

            expert(0, 0)
            with act.Fori(1, NE) as e:
                expert(e, e * RING - 2)

        def second_vector(dve, norm_apply, softplus):
            ch = Chain(dve, dve_chain2, 0)
            dve.wait_ge(packb_in, 16)
            v.tensor_scalar(ngb, pb_("glab"), -1.0, None, ALU.mult).then_inc(ngb_ready, 1)
            lam = pb[0:64, B_COLS["lam"][0]:B_COLS["lam"][0] + 4].rearrange("p (a b) -> p a b", b=2)
            v.tensor_tensor(lam_p[0:64, :], lam[:, :, 0], lam[:, :, 1], ALU.mult).then_inc(lam_ready, 1)
            norm_apply(ch, NORM2, lambda k: pb_("mix", k))
            dve.wait_ge(cz_zero, 1)
            for j in range(2):
                dve.wait_ge(u_evac, evacuated(CONV_VALUES[j] + 1))
                dve.wait_ge(tile_done, T2 + CONV_VALUES[j] + 1)
                v.tensor_tensor(c_z[:, j, CW - 1:], bank[CONV_VALUES[j] % 4][:, 0:S], c_sg[:, j, :],
                                ALU.mult).then_inc(cz_ready, 1)
            r = softplus(ch, DEPTH, g_sp, 0, P)
            ch.mark(v.tensor_tensor_scan(r, cc("ones256"), r, 0.0, ALU.mult, ALU.add))
            ch.dep()
            ch.mark(v.tensor_scalar(g_b, r, -1.0 / GTAU, None, ALU.mult))
            v.tensor_scalar(g_c, r, 1.0 / GTAU, None, ALU.mult).then_inc(gc_ready, 1)
            dve.wait_ge(cz_ready, 2)
            for w in range(CW):
                if w:
                    ch.dep()
                for j in range(2):
                    src = c_z[:, j, w:w + S]
                    if w == 0:
                        ins = v.tensor_scalar(c_y[:, j, :], src, pb_("convw", j * CW), pb_("convb", j), ALU.mult, ALU.add)
                    else:
                        ins = v.scalar_tensor_tensor(c_y[:, j, :], src, pb_("convw", j * CW + w), c_y[:, j, :],
                                                     ALU.mult, ALU.add)
                    if w < CW - 1 or j == 0:
                        ch.mark(ins)
            ins.then_inc(cy_ready, 1)
            dve.wait_ge(ge_ready, 1)
            dve.wait_ge(ki_zero, 1)
            for b in range(1, NGB):
                v.tensor_tensor(g_ki[:, b - 1, 0:b * GB], g_ke[:, b - 1, 0:b * GB], g_k[:, 0:b * GB], ALU.mult)
            v.tensor_tensor(g_qe[:, GB:], g_qe[:, GB:], g_q[:, GB:], ALU.mult).then_inc(ki_ready, 1)
            dve.wait_ge(lam_exp, 1)
            ch.mark(v.scalar_tensor_tensor(nlam, lam_e[:, 1:2], -LAMBDA_INIT, lam_e[:, 0:1], ALU.add, ALU.subtract))

            def in_block(jt):
                dve.wait_ge(pr_sub, jt + 1)
                v.tensor_scalar(g_pr[:], g_pr[:], 0.0, None, ALU.min).then_inc(pr_min, 1)

            def in_block_q(jt):
                dve.wait_ge(pr_exp, jt + 1)
                pr = g_pr[:].rearrange("p r (b j) -> p b r j", b=P // GB)
                q_i = g_q[:, jt * P:(jt + 1) * P].rearrange("p (b r) -> p b r", r=GB).unsqueeze(3).to_broadcast([P, P // GB, GB, GB])
                v.tensor_tensor(pr, pr, q_i, ALU.mult).then_inc(pr_q, 1)

            in_block(0)

            def unit(i):
                dve.wait_ge(dn_std, i + 1)
                ch.mark(v.reciprocal(d_std[:, i, :], d_std[:, i, :]))
                ch.dep()
                dve.wait_ge(u_evac, evacuated(U_DQ + i))
                v.scalar_tensor_tensor(d_raw[:, i, :], d_raw[:, i, :], pb_("qn" if i < 4 else "kn"), d_std[:, i, :],
                                       ALU.mult, ALU.mult).then_inc(dn_ready, 1)

            for i in range(8):
                unit(i)
            in_block_q(0)
            in_block(1)
            in_block_q(1)
            dve.wait_ge(st_copied, 2 * GH)
            for jt in range(NT):
                dve.wait_ge(dg_done, NT)
                for b in range(P // GB):
                    ps_ = slice(b * GB, (b + 1) * GB)
                    at = jt * P + b * GB
                    ins = v.tensor_tensor(
                        g_st[ps_, :, jt, at:at + GB],
                        bank[4][ps_, jt * P:(jt + 1) * P].rearrange("p (r i) -> p i r", i=GH),
                        cc("gmask", rows_=ps_).unsqueeze(1).to_broadcast([GB, GH, GB]), ALU.mult)
            ins.then_inc(dg_ready, 1)

            def masked(i):
                dve.wait_ge(df_s, i + 1)
                ch.mark(v.scalar_tensor_tensor(d_prob[:, i, :], bank[2 + i % 2][:, 0:3 * P], 64 ** -0.5,
                                               cc("causal"), ALU.mult, ALU.add))
                ch.dep()
                ch.mark(v.tensor_reduce(d_max[:, 2 * i:2 * i + 1], d_prob[:, i, 0:P], AX_X, ALU.max, negate=True))
                v.tensor_reduce(d_max[:, 2 * i + 1:2 * i + 2], d_prob[:, i, P:3 * P], AX_X, ALU.max,
                                negate=True).then_inc(df_sm, 1)

            def difference(j):
                dve.wait_ge(df_p, 2 * j + 2)
                ch.mark(v.reciprocal(d_rz[:, 4 * j:4 * j + 4], d_z[:, 4 * j:4 * j + 4]))
                ch.dep()
                ch.mark(v.tensor_scalar(d_rz[:, 4 * j + 2:4 * j + 4], d_rz[:, 4 * j + 2:4 * j + 4], nlam, None, ALU.mult))
                parts = (slice(0, P), slice(P, 3 * P))
                for c, part in enumerate(parts):
                    ch.mark(v.tensor_scalar(d_prob[:, 2 * j, part], d_prob[:, 2 * j, part],
                                            d_rz[:, 4 * j + c:4 * j + c + 1], None, ALU.mult))
                ch.dep()
                for c, part in enumerate(parts):
                    ins = v.scalar_tensor_tensor(d_prob[:, 2 * j, part], d_prob[:, 2 * j + 1, part],
                                                 d_rz[:, 4 * j + 2 + c:4 * j + 3 + c], d_prob[:, 2 * j, part],
                                                 ALU.mult, ALU.add)
                ins.then_inc(df_pn, 1)

            for i in range(8 + 2):
                if i < 8:
                    masked(i)
                j, odd = divmod(i - 2, 2)
                if 0 <= j < DFH and odd == 0:
                    difference(j)
            dve.wait_ge(cm_done, 1)
            for j in range(2):
                v.scalar_tensor_tensor(c_y[:, j, :], bank[2][:, j * S:(j + 1) * S], -1.0 / 64, c_y[:, j, :],
                                       ALU.mult, ALU.add).then_inc(cc_ready, 1)
            dve.wait_ge(gn_std, 1)
            dve.wait_ge(go_sq, 2)
            ch.mark(v.reciprocal(g_rs[:], g_std[:]))
            ch.dep()
            ch.mark(v.scalar_tensor_tensor(g_o[:], g_o[:], pb_("glan"), g_rs[:], ALU.mult, ALU.mult))
            ch.dep()
            v.tensor_tensor(mix[:, 0:2, :], g_o[:], g_og[:], ALU.mult).then_inc(gla_mix, 1)
            for g in range(2):
                hs = slice(2 * g, 2 * g + 2)
                dve.wait_ge(do_std, g + 1)
                ch.mark(v.reciprocal(d_ostd[:, hs, :], d_ostd[:, hs, :]))
                ch.dep()
                ch.mark(v.tensor_scalar(d_ostd[:, hs, :], d_ostd[:, hs, :], 1.0 - LAMBDA_INIT, None, ALU.mult))
                ch.dep()
                v.scalar_tensor_tensor(mix[:, 4 + 2 * g:6 + 2 * g, :], d_o[:, hs, :], pb_("subln"), d_ostd[:, hs, :],
                                       ALU.mult, ALU.mult).then_inc(diff_mix, 1)
            dve.wait_ge(cv_std, 1)
            ch.mark(v.reciprocal(c_rs[:], c_std[:]))
            ch.dep()
            for j in range(2):
                v.tensor_tensor(c_y[:, j, :], c_y[:, j, :], c_rs[:, j, :], ALU.mult).then_inc(cn_ready, 1)
            for m in range(KD):
                dve.wait_ge(tile_done, T2 + U_WOUT + m + 1)
                v.tensor_tensor(x[:, m, :], x[:, m, :], bank[m % 4][:, 0:S], ALU.add).then_inc(x_added, 1)
            dve.wait_ge(x_added, KD)
            norm_apply(ch, NORM2 + 1, lambda k: pb_("ffn", k))

            def b4(col, n=4):
                return col.unsqueeze(2).to_broadcast([P, NT, n])

            order = cc("first4").unsqueeze(1).to_broadcast([P, NT, 4])

            def first_max(vals, best, onehot):
                ch.mark(v.tensor_reduce(best, vals, AX_X, ALU.max))
                ch.dep()
                ch.mark(v.tensor_tensor(r_eq[:], vals, b4(best), ALU.is_equal))
                ch.dep()
                ch.mark(v.tensor_tensor(r_w[:], r_eq[:], order, ALU.mult))
                ch.dep()
                ch.mark(v.tensor_reduce(r_m2[:], r_w[:], AX_X, ALU.max))
                ch.dep()
                ch.mark(v.tensor_tensor(onehot, r_w[:], b4(r_m2), ALU.is_equal))
                ch.dep()

            dve.wait_ge(rt_done, 1)
            ch.mark(v.tensor_copy(r_log[:], bank[5][:, 0:NT * NR].rearrange("p (c n) -> p c n", c=NT)))
            ch.dep()
            first_max(r_log[:, :, 0:NG], r_max, r_oh[:])
            v.tensor_tensor(r_e[:], r_log[:, :, 0:NG], b4(r_max), ALU.subtract).then_inc(r_sub, 1)
            by_group = r_log[:, :, NG:NR].rearrange("p c (g e) -> p c g e", g=NG)
            pro = r_pro[:].rearrange("p c (g e) -> p c g e", g=NG)
            for c in range(NT):
                ch.mark(v.tensor_tensor(pro[:, c], by_group[:, c], r_oh[:, c, :].unsqueeze(2).to_broadcast([P, NG, 4]), ALU.mult))
            ch.dep()
            ch.mark(v.tensor_reduce(r_sel[:], r_pro[:].rearrange("p c (g e) -> p c e g", g=NG), AX_X, ALU.add))
            ch.dep()
            first_max(r_sel[:], r_l1, r_o1[:])
            ch.mark(v.scalar_tensor_tensor(r_s2[:], r_o1[:], NEG, r_sel[:], ALU.mult, ALU.add))
            ch.dep()
            first_max(r_s2[:], r_l2, r_o2[:])
            v.tensor_tensor(r_d, r_l2, r_l1, ALU.subtract).then_inc(r_sub, 1)
            dve.wait_ge(r_exp, 1)
            ch.mark(v.tensor_reduce(r_sum, r_e[:], AX_X, ALU.add))
            ch.dep()
            ch.mark(v.reciprocal(r_pg, r_sum))
            dve.wait_ge(r_exp, 2)
            ch.mark(v.tensor_scalar(r_u, r_e2, 1.0, None, ALU.add))
            ch.dep()
            ch.mark(v.reciprocal(r_w1, r_u))
            ch.dep()
            ch.mark(v.tensor_tensor(r_w1, r_w1, r_pg, ALU.mult))
            ch.dep()
            ch.mark(v.tensor_tensor(r_w2, r_w1, r_e2, ALU.mult))
            ch.dep()
            ch.mark(v.tensor_tensor(r_t1[:], r_o1[:], b4(r_w1), ALU.mult))
            ch.mark(v.tensor_tensor(r_t2[:], r_o2[:], b4(r_w2), ALU.mult))
            ch.dep()
            ch.mark(v.tensor_tensor(r_t1[:], r_t1[:], r_t2[:], ALU.add))
            ch.dep()
            gates = r_gate[:].rearrange("p c (g e) -> p c g e", g=NG)
            for c in range(NT):
                ins = v.tensor_tensor(gates[:, c], r_oh[:, c, :].unsqueeze(2).to_broadcast([P, NG, 4]),
                                      r_t1[:, c, :].unsqueeze(1).to_broadcast([P, NG, 4]), ALU.mult)
            ins.then_inc(gates_ready, 1)
            dve.wait_ge(gbc_ready, NE // 2)

            def expert_gate(e, done):
                for j in range(2):
                    dve.wait_ge(tile_done, T2 + U_EXP + done + 2 + j + 1)
                    dve.wait_ge(ex_hid, 2 * e + j + 1)
                    v.tensor_tensor(e_up[:, j, :], bank[2 + j][:, 0:S], gate_bc[:, bass.ds(e * S, S)],
                                    ALU.mult).then_inc(ex_up, 1)

            def expert_add(e, done):
                for b in range(4):
                    dve.wait_ge(tile_done, T2 + U_EXP + done + b // 2 + 1)
                    ins = v.tensor_tensor(x[:, 2 * b:2 * b + 2, :], x[:, 2 * b:2 * b + 2, :],
                                          bank[4 + b][:, :].rearrange("p (j s) -> p j s", j=2), ALU.add)
                    ins.then_inc(ex_add, 1)

            expert_gate(0, 0)
            with dve.Fori(0, NE - 1) as e:
                expert_gate(e + 1, (e + 1) * RING - 2)
                expert_add(e, e * RING + 8)
            expert_add(NE - 1, NE * RING - 2)

        def second_pool(pool):
            pool.wait_ge(norm_out, NORM2)
            pl.memset(g_ki[:], 0.0).then_inc(ki_zero, 1)
            pl.memset(c_z[:, :, 0:CW - 1], 0.0).then_inc(cz_zero, 1)
            pl.memset(g_st[:], 0.0).then_inc(st_zero, 1)
            for jt in range(NT):
                nb = P // GB
                pr = g_pr[:].rearrange("p r (b j) -> p b r j", b=nb)
                here = slice(jt * P, (jt + 1) * P)
                b_i = g_b[:, here].rearrange("p (b r) -> p b r", r=GB).unsqueeze(3).to_broadcast([P, nb, GB, GB])
                b_j = g_b[:, here].rearrange("p (b j) -> p b j", j=GB).unsqueeze(2).to_broadcast([P, nb, GB, GB])
                k_j = g_k[:, here].rearrange("p (b j) -> p b j", j=GB).unsqueeze(2).to_broadcast([P, nb, GB, GB])
                pool.wait_ge(gc_ready, 1)
                if jt:
                    pool.wait_ge(dg_done, jt)
                pl.tensor_tensor(pr, b_i, b_j, ALU.subtract).then_inc(pr_sub, 1)
                pool.wait_ge(pr_q, jt + 1)
                pl.tensor_tensor(pr, pr, k_j, ALU.mult).then_inc(pr_ready, 1)
            pool.wait_ge(x_added, KD)
            for j in range(EX_CREDITS):
                pl.memset(credit[:, j:j + 1], 0.0).then_inc(ex_hid, 1)
            for j in range(4):
                pl.memset(credit[:, 2 + j:3 + j], 0.0).then_inc(ex_add, 1)

            def expert(e):
                for j in range(2):
                    pool.wait_ge(tile_done, T2 + U_EXP + e * RING + 4)
                    pool.wait_ge(ex_act, 2 * e + j + 1)
                    pool.wait_ge(ex_up, 2 * e + j + 1)
                    pl.tensor_tensor(e_hid[:, j, :], e_act[:, j, :], e_up[:, j, :], ALU.mult).then_inc(ex_hid, 1)

            with pool.Fori(0, NE) as e:
                expert(e)

        block = ctx.enter_context(nc.Block())

        @block.sync
        def _(sp):
            sp.dma_start(x[:], xt).then_inc(x_in, 16)
            sp.dma_start(cst[:], consts).then_inc(consts_in, 16)
            for s in range(RING):
                sp.dma_start(ring[:, s, :], wtiles[s]).then_inc(w_in[s], 16)
            sp.dma_start(pb[:], packb).then_inc(packb_in, 16)
            with sp.Fori(1, ALL_TILES // RING) as r:
                for s in range(RING):
                    sp.wait_ge(tile_done, (r - 1) * RING + s + 1)
                    sp.dma_start(ring[:, s, :], wtiles[bass.ds(r * RING + s, 1)].rearrange("o p n -> (o p) n")
                                 ).then_inc(w_in[s], 16)
            sp.wait_ge(ex_add, 4 * NE + 4)
            sp.dma_start(out, x[:]).then_inc(out_done, 16)
            sp.wait_ge(out_done, 16)

        @block.tensor
        def _(pe):
            def tile_in(s, rnd):
                pe.wait_ge(w_in[s], 16 * rnd + 16)

            def project(s, out_):
                for k in range(KD):
                    mm = t.matmul(out_, ring[:, s, k * P:(k + 1) * P], h[:, k, :], start=k == 0, stop=k == KD - 1)
                mm.then_inc(tile_done, 1)

            def project_tokens(s, out_bank):
                for c in range(NT):
                    for k in range(KD):
                        mm = t.matmul(out_bank[:, c * P:(c + 1) * P], h[:, k, c * P:(c + 1) * P],
                                      ring[:, s, k * P:(k + 1) * P], start=k == 0, stop=k == KD - 1)
                mm.then_inc(tile_done, 1)

            def sum_squares(i):
                for k in range(KD):
                    pe.wait_ge(norm_sq, i * KD + k + 1)
                    mm = t.matmul(bank[4][:, 0:S], ones, sq[:, k, :], start=k == 0, stop=k == KD - 1)
                mm.then_inc(norm_sum, 1)

            def transpose(out_, in_):
                return t.transpose(out_, in_, ident)

            def scores(i, q, k, b):
                lo, j = 64 * (i % 2), i // 2
                t.matmul(b[:, 0:P], q[lo:lo + 64, j, 0:P], k[lo:lo + 64, j, 0:P], start=True, stop=True)
                return t.matmul(b[:, P:3 * P], q[lo:lo + 64, j, P:S], k[lo:lo + 64, j, :], start=True, stop=True)

            pe.wait_ge(consts_in, 16)

            def layer(l):
                sum_squares(l * 4)
                pe.wait_ge(norm_out, l * 4 + 1)
                pe.wait_ge(packa_in, l * 16 + 16)
                for n in range(T_WOUT):
                    tile_in(n % RING, l * LAYER_ROUNDS + n // RING)
                    if 4 <= n < T_Z + 4:
                        pe.wait_ge(conv_ready, l * 12 + n - 3)
                    elif n >= T_Z + 4:
                        pe.wait_ge(proj_evac, l * 16 + n - T_Z - 3)
                    if n < T_BV:
                        project(n % RING, bank[n % 4][:, 0:S])
                    else:
                        project_tokens(n % RING, bank[n % 4])
                    if n == T_Z - 1:
                        for k in range(KD):
                            mm = t.matmul(bank[4][0:64, S:2 * S], pa_("wba", k * 64, 64), h[:, k, :],
                                          start=k == 0, stop=k == KD - 1)
                        mm.then_inc(ba_done, 1)
                    if T_BQ <= n < T_BQ + 8:
                        i = n - T_BQ
                        pe.wait_ge(sqk_ready, l * 8 + i + 1)
                        if i >= 2:
                            pe.wait_ge(l2_std, l * 8 + i - 1)
                        t.matmul(bank[6 + i % 2][:, 0:S], ones, sqk[:, i, :], start=True, stop=True).then_inc(l2_sum, 1)
                    if T_BQ + 2 <= n < T_BQ + 10:
                        j = n - T_BQ - 2
                        pe.wait_ge(proj_evac, l * 16 + 4 + j + 1)
                        if j >= 2:
                            pe.wait_ge(rope_used, l * 8 + j - 1)
                        t.matmul(bank[4 + j % 2][:, 0:S], cc("rot"), raw[:, j, :],
                                 start=True, stop=True).then_inc(rope_rot, 1)

                pe.wait_ge(rows_ready, l + 1)
                pe.wait_ge(rope_used, l * 8 + 8)
                for c in range(NT):
                    mm = t.matmul(bank[4][:, S + 64 * c:S + 64 * c + 64], rows[0:64, c * P:(c + 1) * P],
                                  ident[0:64, 0:64], start=True, stop=True)
                mm.then_inc(cols_done, 1)
                pe.wait_ge(proj_evac, l * 16 + 16)
                pe.wait_ge(l2_std, l * 8 + 8)
                pe.wait_ge(qk_ready, l * 8 + 8)
                for i in range(DNH):
                    if i >= 2:
                        pe.wait_ge(bc_act, l * 4 + i - 1)
                        pe.wait_ge(bc_dve, l * 4 + i - 1)
                    t.matmul(bank[i % 2][:, 0:S], ident[0:64, 32 + i:33 + i].to_broadcast([64, P]), rows[0:64, :],
                             start=True, stop=True)
                    t.matmul(bank[i % 2][:, S:2 * S], ident[0:64, i:i + 1].to_broadcast([64, P]), rows[0:64, :],
                             start=True, stop=True).then_inc(bc_done, 1)
                    if i >= 2:
                        pe.wait_ge(tr_dve, l * 4 + i - 1)
                        pe.wait_ge(tr_act, l * 4 + i - 1)
                    pe.wait_ge(silu_ready, l * 12 + 8 + i + 1)
                    transpose(bank[6 + i % 2][:, 0:P], qkvs[:, 8 + i, 0:P])
                    transpose(bank[6 + i % 2][:, P:2 * P], qkvs[:, 8 + i, P:S])
                    transpose(bank[6 + i % 2][:, 2 * P:3 * P], qkn[:, 4 + i, 0:P]).then_inc(tr_done, 1)
                    if i >= 2:
                        pe.wait_ge(gram_used, l * 4 + i - 1)
                    for c in range(NT):
                        keys = qkn[:, 4 + i, c * P:(c + 1) * P]
                        t.matmul(bank[2 + i % 2][:, c * S:c * S + P], keys, keys, start=True, stop=True)
                        mm = t.matmul(bank[2 + i % 2][:, c * S + P:c * S + 2 * P], keys, qkn[:, i, c * P:(c + 1) * P],
                                      start=True, stop=True)
                    mm.then_inc(gram_done, 1)

                pe.wait_ge(bc_act, l * 4 + 4)
                pe.wait_ge(bc_dve, l * 4 + 4)
                pe.wait_ge(bl_ready, l * LEVELS + 1)
                for g in range(2):
                    for u in range(4):
                        mm = t.matmul(bank[g][:, u * P:(u + 1) * P], bl[:, 0, 4 * g + u, :], ident, start=True, stop=True)
                    mm.then_inc(lev_x, 1)
                pe.wait_ge(gram_used, l * 4 + 4)
                pe.wait_ge(tr_dve, l * 4 + 4)
                pe.wait_ge(tr_act, l * 4 + 4)
                for lev in range(1, LEVELS):
                    pe.wait_ge(bl_ready, l * LEVELS + lev + 1)
                    for g in range(2):
                        pe.wait_ge(tu_ready, l * 2 * LEVELS + 2 * (lev - 1) + g + 1)
                        for u in range(4 * g, 4 * g + 4):
                            mm = t.matmul(bank[6 + g][:, u % 4 * P:u % 4 * P + P], bl[:, lev % 2, u, :], tinv[:, u, :],
                                          start=True, stop=True)
                        mm.then_inc(lev_x, 1)
                    for g in range(2):
                        pe.wait_ge(lev_xs, l * 2 * (LEVELS - 1) + 2 * (lev - 1) + g + 1)
                        for u in range(4 * g, 4 * g + 4):
                            if lev < LEVELS - 1:
                                t.matmul(bank[g][:, u % 4 * P:u % 4 * P + P], uinv[:, u, :], xs[:, u, :],
                                         start=True, stop=True)
                            mm = t.matmul(bank[2 + g][:, u % 4 * P:u % 4 * P + P], xs[:, u, :], uinv[:, u, :],
                                          start=True, stop=True)
                        mm.then_inc(lev_y, 1)

                pe.wait_ge(tu_ready, l * 2 * LEVELS + 2 * LEVELS)
                for i in range(DNH):
                    mm = t.matmul(bank[6][:, i * P:(i + 1) * P], uinv[:, 2 * i, :], vb[:, 2 * i, :], start=True, stop=True)
                mm.then_inc(rec_pe, 1)
                pe.wait_ge(rec_act, l * 7 + 1)
                pe.wait_ge(rope_used, l * 8 + 8)
                for i in range(DNH):
                    mm = t.matmul(bank[7][:, i * P:(i + 1) * P], kd[:, i, :], vnew[:, 0, i, :], start=True, stop=True)
                mm.then_inc(rec_pe, 1)
                for i in range(DNH):
                    mm = t.matmul(bank[5][:, i * P:(i + 1) * P], vnew[:, 0, i, :], qkt[:, 2 * i, :], start=True, stop=True)
                mm.then_inc(rec_pe, 1)
                pe.wait_ge(rec_act, l * 7 + 2)
                pe.wait_ge(kbg_ready, l * 4 + 4)
                for i in range(DNH):
                    mm = t.matmul(bank[6][:, i * P:(i + 1) * P], kbg[:, i, :], st1[:, i, :], start=True, stop=True)
                mm.then_inc(rec_pe, 1)
                pe.wait_ge(rec_dve, l + 1)
                for i in range(DNH):
                    mm = t.matmul(bank[7][:, i * P:(i + 1) * P], uinv[:, 2 * i + 1, :], resid[:, i, :], start=True, stop=True)
                mm.then_inc(rec_pe, 1)
                pe.wait_ge(rec_act, l * 7 + 5)
                for i in range(DNH):
                    t.matmul(bank[6][:, i * P:(i + 1) * P], st1[:, i, :], qg[:, i, :], start=True, stop=False)
                    mm = t.matmul(bank[6][:, i * P:(i + 1) * P], vnew[:, 1, i, :], qkt[:, 2 * i + 1, :],
                                  start=False, stop=True)
                mm.then_inc(rec_pe, 1)

                pe.wait_ge(rope_done, l * 8 + 8)
                for i in range(SWAH + 3):
                    if i < SWAH:
                        if i >= 2:
                            pe.wait_ge(att_sm, l * 8 + i - 1)
                        scores(i, raw[:, 0:4, :], raw[:, 4:8, :], bank[2 + i % 2]).then_inc(att_s, 1)
                    if i == 1:
                        pe.wait_ge(rec_act, l * 7 + 7)
                        for g in range(2):
                            t.matmul(bank[g][:, :], ones, sq[:, 2 * g:2 * g + 2, :], start=True, stop=True).then_inc(on_sum, 1)
                    j = i - 2
                    if 0 <= j < SWAH:
                        pe.wait_ge(att_pn, l * 8 + j + 1)
                        if j >= 2:
                            pe.wait_ge(att_pt, l * 8 + j - 1)
                        b = bank[6 + j % 2]
                        transpose(b[:, 0:P], prob[:, j, 0:P])
                        transpose(b[:, P:2 * P], prob[:, j, P:2 * P])
                        transpose(b[:, 2 * P:3 * P], prob[:, j, 2 * P:3 * P]).then_inc(att_t, 1)
                    j = i - 3
                    if 0 <= j < SWAH:
                        pe.wait_ge(att_pt, l * 8 + j + 1)
                        if j == 0:
                            pe.wait_ge(on_std, l * 2 + 2)
                        if j >= 4 and j % 2 == 0:
                            pe.wait_ge(att_o, l * 4 + j // 2 - 1)
                        o_ = bank[j // 2 % 2][64 * (j % 2):64 * (j % 2) + 64, :]
                        vals = vtok[:, :, j * 64:(j + 1) * 64]
                        t.matmul(o_[:, 0:P], vals[:, 0, :], pt[:, j % 2, 0:P], start=True, stop=True)
                        t.matmul(o_[:, P:S], vals[:, 0, :], pt[:, j % 2, P:2 * P], start=True, stop=False)
                        t.matmul(o_[:, P:S], vals[:, 1, :], pt[:, j % 2, 2 * P:3 * P], start=False,
                                 stop=True).then_inc(att_pv, 1)

                pe.wait_ge(mix_a, l + 1)
                pe.wait_ge(att_o, l * 4 + 4)
                for m in range(KD):
                    n = T_WOUT + m
                    tile_in(n % RING, l * LAYER_ROUNDS + n // RING)
                    if m >= 4:
                        pe.wait_ge(y_done, l * 16 + m - 3)
                    for k in range(KD):
                        mm = t.matmul(bank[m % 4][:, 0:S], ring[:, n % RING, k * P:(k + 1) * P], mix[:, k, :],
                                      start=k == 0, stop=k == KD - 1)
                    mm.then_inc(tile_done, 1)
                sum_squares(l * 4 + 1)

                sum_squares(l * 4 + 2)

                def pair(p, q, rnd):
                    pe.wait_ge(norm_out, l * 4 + 3)
                    pe.wait_ge(ffn_free, l * NP_FF + p + 1)
                    tile_in(2 * q, rnd)
                    project(2 * q, bank[2 * q][:, 0:S])
                    tile_in(2 * q + 1, rnd)
                    project(2 * q + 1, bank[2 * q + 1][:, 0:S])

                with pe.Fori(0, FFN_LOOPS) as i:
                    for q in range(PAIRS):
                        pair(i * PAIRS + q, q, l * LAYER_ROUNDS + T_UP // RING + i)
                for q in range(NP_FF - FFN_LOOPS * PAIRS):
                    pair(FFN_LOOPS * PAIRS + q, q, l * LAYER_ROUNDS + T_UP // RING + FFN_LOOPS)
                for m in range(KD):
                    if m == 0:
                        pe.wait_ge(ffn_free, l * NP_FF + NP_FF + CREDITS)
                    if m >= 4:
                        pe.wait_ge(y_done, l * 16 + 8 + m - 3)
                    for k in range(NP_FF):
                        n, part = T_DOWN + (m * NP_FF + k) // 8, (m * NP_FF + k) % 8
                        if part == 0 or k == 0:
                            tile_in(n % RING, l * LAYER_ROUNDS + n // RING)
                        if m == 0:
                            pe.wait_ge(hid_done, l * NP_FF + k + 1 + CREDITS)
                        mm = t.matmul(bank[m % 4][:, 0:S], ring[:, n % RING, part * P:(part + 1) * P],
                                      hid[:, k * S:(k + 1) * S], start=k == 0, stop=k == NP_FF - 1)
                        if part == 7:
                            mm.then_inc(tile_done, 1)
                sum_squares(l * 4 + 3)

            with pe.Fori(0, DEPTH) as l:
                layer(l)
            second_tensor(pe, tile_in, project, project_tokens, sum_squares, transpose, scores)

        @block.scalar
        def _(act):
            def square(i, k, src):
                a.activation(sq[:, k, :], src, ACT.Square).then_inc(norm_sq, 1)

            def norm_root(i):
                act.wait_ge(norm_sum, i + 1)
                a.activation(std[:], bank[4][:, 0:S], ACT.Sqrt, bias=eps, scale=1.0 / D).then_inc(norm_std, 1)

            def pre_norm(i):
                for k in range(KD):
                    square(i, k, x[:, k, :])
                norm_root(i)

            def post_norm(i, done):
                for m in range(KD):
                    act.wait_ge(y_done, done + m + 1)
                    square(i, m, y[:, m, :])
                norm_root(i)

            def softplus(l, src, ready, bias, scale, sp, lo, hi):
                act.wait_ge(ready[0], ready[1])
                a.activation(sp[lo:hi, 0, :], src, ACT.Identity, bias=bias, scale=scale).then_inc(sp_act, 1)
                act.wait_ge(sp_dve, l * 2 + 1)
                a.activation(sp[lo:hi, 2, :], sp[lo:hi, 1, :], ACT.Exp, scale=-1.0).then_inc(sp_act, 1)
                act.wait_ge(sp_dve, l * 2 + 2)
                a.activation(sp[lo:hi, 4, :], sp[lo:hi, 3, :], ACT.Ln).then_inc(sp_act, 1)

            act.wait_ge(x_in, 16)
            act.wait_ge(consts_in, 16)

            def layer(l):
                pre_norm(l * 4)
                for n in range(12):
                    act.wait_ge(conv_ready, l * 12 + n + 1)
                    a.activation(qkvs[:, n, :], qkvc[:, n, :], ACT.Silu).then_inc(silu_ready, 1)
                    if n < 8:
                        act.wait_ge(silu_ready, l * 12 + n + 1)
                        a.activation(sqk[:, n, :], qkvs[:, n, :], ACT.Square).then_inc(sqk_ready, 1)
                act.wait_ge(packa_in, l * 16 + 16)
                softplus(l, bank[4][32:36, S:2 * S], (ba_done, l + 1), pa_("dt", rows_=slice(32, 36)), 1.0, spt, 32, 36)
                a.activation(cols[32:36, 1, 0:1], pa_("alog", rows_=slice(32, 36)), ACT.Exp).then_inc(decay_ready, 1)
                act.wait_ge(rows_zero, 1)
                a.activation(rows[0:4, :], bank[4][0:4, S:2 * S], ACT.Sigmoid).then_inc(beta_ready, 1)
                for n in range(T_Z, T_WOUT):
                    act.wait_ge(tile_done, l * LAYER_TILES + n + 1)
                    src = bank[n % 4]
                    if n < T_BQ:
                        a.activation(zs[:, n - T_Z, :], src[:, 0:S], ACT.Silu).then_inc(proj_evac, 1)
                    elif n < T_BV:
                        a.activation(raw[:, n - T_BQ, :], src[:, 0:S], ACT.Copy).then_inc(proj_evac, 1)
                    else:
                        j = n - T_BV
                        a.activation(vtok[:, :, j * P:(j + 1) * P], src[:, 0:S].rearrange("p (c d) -> p c d", c=NT),
                                     ACT.Copy).then_inc(proj_evac, 1)
                    if T_BQ <= n < T_BQ + 8:
                        i = n - T_BQ
                        act.wait_ge(l2_sum, l * 8 + i + 1)
                        a.activation(rin[:, i, :], bank[6 + i % 2][:, 0:S], ACT.Sqrt, bias=eps).then_inc(l2_std, 1)

                for i in range(DNH):
                    act.wait_ge(bc_done, l * 4 + i + 1)
                    a.activation(eg1[:, i, :], bank[i % 2][:, P:S], ACT.Exp)
                    a.activation(bbc[:, i, :], bank[i % 2][:, S:2 * S], ACT.Copy).then_inc(bc_act, 1)
                    act.wait_ge(bc_dve, l * 4 + i + 1)
                    a.activation(gam[:, i, :], gam[:, i, :], ACT.Exp).then_inc(gam_ready, 1)
                    act.wait_ge(tr_dve, l * 4 + i + 1)
                    act.wait_ge(gam_ready, l * 4 + i + 1)
                    a.activation(kd[:, i, :], bank[6 + i % 2][:, 2 * P:3 * P], ACT.Copy,
                                 scale=gam[:, i, P - 1:P]).then_inc(tr_act, 1)
                for lev in range(1, LEVELS):
                    for g in range(2):
                        act.wait_ge(lev_x, l * 2 * LEVELS + 2 * lev + g + 1)
                        a.activation(xs[:, 4 * g:4 * g + 4, :], bank[6 + g][:, :].rearrange("p (u k) -> p u k", u=4),
                                     ACT.Copy).then_inc(lev_xs, 1)

                def heads(b):
                    return b[:, :].rearrange("p (i k) -> p i k", i=DNH)

                act.wait_ge(rec_pe, l * 6 + 1)
                a.activation(vnew[:, 0], heads(bank[6]), ACT.Copy).then_inc(rec_act, 1)
                act.wait_ge(rec_pe, l * 6 + 2)
                a.activation(st1[:], heads(bank[7]), ACT.Copy).then_inc(rec_act, 1)
                act.wait_ge(rec_pe, l * 6 + 3)
                a.activation(ot[:, :, 0:P], heads(bank[5]), ACT.Copy).then_inc(rec_act, 1)
                a.activation(sq[:, 0:4, 0:P], heads(bank[5]), ACT.Square).then_inc(rec_act, 1)
                act.wait_ge(rec_pe, l * 6 + 5)
                a.activation(vnew[:, 1], heads(bank[7]), ACT.Copy).then_inc(rec_act, 1)
                act.wait_ge(rec_pe, l * 6 + 6)
                a.activation(ot[:, :, P:S], heads(bank[6]), ACT.Copy).then_inc(rec_act, 1)
                a.activation(sq[:, 0:4, P:S], heads(bank[6]), ACT.Square).then_inc(rec_act, 1)
                for g in range(2):
                    act.wait_ge(on_sum, l * 2 + g + 1)
                    a.activation(rin[:, 2 * g:2 * g + 2, :], bank[g][:, :].rearrange("p (i s) -> p i s", i=2),
                                 ACT.Sqrt, bias=eps, scale=1.0 / P).then_inc(on_std, 1)

                for i in range(SWAH + 3):
                    if i < SWAH:
                        act.wait_ge(att_sm, l * 8 + i + 1)
                        a.activation(prob[:, i, 0:P], prob[:, i, 0:P], ACT.Exp, bias=att_max[:, 2 * i:2 * i + 1],
                                     accum_out=att_z[:, 2 * i:2 * i + 1])
                        a.activation(prob[:, i, P:3 * P], prob[:, i, P:3 * P], ACT.Exp,
                                     bias=att_max[:, 2 * i + 1:2 * i + 2],
                                     accum_out=att_z[:, 2 * i + 1:2 * i + 2]).then_inc(att_p, 1)
                    j = i - 2
                    if 0 <= j < SWAH:
                        act.wait_ge(att_t, l * 8 + j + 1)
                        if j >= 2:
                            act.wait_ge(att_pv, l * 8 + j - 1)
                        a.activation(pt[:, j % 2, :], bank[6 + j % 2][:, 0:3 * P], ACT.Copy).then_inc(att_pt, 1)
                    j = i - 3
                    if j % 2 == 1 and 0 <= j < SWAH:
                        act.wait_ge(att_pv, l * 8 + j + 1)
                        a.activation(mix[:, 4 + j // 2, :], bank[j // 2 % 2][:, 0:S], ACT.Copy).then_inc(att_o, 1)

                post_norm(l * 4 + 1, l * 16)

                act.wait_ge(norm_out, l * 4 + 2)
                pre_norm(l * 4 + 2)

                def gelu(p, q):
                    act.wait_ge(glu_ready, l * NP_FF + p + 1)
                    act.wait_ge(hid_done, l * NP_FF + p + 1)
                    a.activation(glu_a[:, q, :], glu_g[:, q, :], ACT.Gelu_apprx_tanh).then_inc(gelu_done, 1)

                with act.Fori(0, FFN_LOOPS) as i:
                    for q in range(PAIRS):
                        gelu(i * PAIRS + q, q)
                for q in range(NP_FF - FFN_LOOPS * PAIRS):
                    gelu(FFN_LOOPS * PAIRS + q, q)
                post_norm(l * 4 + 3, l * 16 + 8)
                act.wait_ge(norm_out, l * 4 + 4)

            with act.Fori(0, DEPTH) as l:
                layer(l)
            second_scalar(act, pre_norm, softplus)

        @block.vector
        def _(dve):
            def norm_apply(ch, i, gain):
                dve.wait_ge(norm_std, i + 1)
                ch.mark(v.reciprocal(rstd[:], std[:]))
                ch.dep()
                for k in range(KD):
                    ins = v.scalar_tensor_tensor(h[:, k, :], x[:, k, :], gain(k), rstd[:], ALU.mult, ALU.mult)
                ins.then_inc(norm_out, 1)

            def norm_add(ch, i, gain):
                dve.wait_ge(norm_std, i + 1)
                ch.mark(v.reciprocal(rstd[:], std[:]))
                ch.dep()
                for k in range(KD):
                    ch.mark(v.scalar_tensor_tensor(y[:, k, :], y[:, k, :], gain(k), rstd[:], ALU.mult, ALU.mult))
                ch.dep()
                v.tensor_tensor(x[:], x[:], y[:], ALU.add).then_inc(norm_out, 1)

            def take_y(l, half, done):
                for m in range(KD):
                    dve.wait_ge(tile_done, done(m))
                    v.tensor_copy(y[:, m, :], bank[m % 4][:, 0:S]).then_inc(y_done, 1)

            def softplus(ch, l, sp, lo, hi):
                z, ab, e, u, ln, r = (sp[lo:hi, j, :] for j in range(6))
                dve.wait_ge(sp_act, l * 3 + 1)
                v.scalar_tensor_tensor(ab, z, -1.0, z, ALU.mult, ALU.max).then_inc(sp_dve, 1)
                dve.wait_ge(sp_act, l * 3 + 2)
                v.tensor_scalar(u, e, 1.0, None, ALU.add).then_inc(sp_dve, 1)
                dve.wait_ge(sp_dve, l * 2 + 2)
                ch.mark(v.scalar_tensor_tensor(ab, u, -1.0, e, ALU.add, ALU.subtract))
                ch.mark(v.reciprocal(r, u))
                ch.dep()
                ch.mark(v.tensor_tensor(ab, ab, r, ALU.mult))
                ch.dep()
                dve.wait_ge(sp_act, l * 3 + 3)
                ch.mark(v.scalar_tensor_tensor(r, z, 0.0, ln, ALU.max, ALU.add))
                ch.dep()
                ch.mark(v.tensor_tensor(r, r, ab, ALU.subtract))
                ch.dep()
                return r

            dve.wait_ge(x_in, 16)
            dve.wait_ge(consts_in, 16)

            def layer(l):
                ch = Chain(dve, dve_chain, l * DVE_LINKS)
                dve.wait_ge(packa_in, l * 16 + 16)
                norm_apply(ch, l * 4, lambda k: pa_("pre", k))

                for n in range(12):
                    dve.wait_ge(tile_done, l * LAYER_TILES + n + 1)
                    src, dst = bank[n % 4], qkvc[:, n, :]
                    ch.mark(v.tensor_scalar(dst, src[:, 0:S], pa_("conv", n * CONV + CONV - 1), None, ALU.mult))
                    for j in range(1, CONV):
                        ch.dep()
                        ins = v.scalar_tensor_tensor(dst[:, j:], src[:, 0:S - j], pa_("conv", n * CONV + CONV - 1 - j),
                                                     dst[:, j:], ALU.mult, ALU.add)
                        if j < CONV - 1:
                            ch.mark(ins)
                    ins.then_inc(conv_ready, 1)

                r = softplus(ch, l, spt, 32, 36)
                dve.wait_ge(decay_ready, l + 1)
                ch.mark(v.tensor_scalar(r, r, cols[32:36, 1, 0:1], -1.0, ALU.mult, ALU.mult))
                ch.dep()
                dve.wait_ge(beta_ready, l + 1)
                dve.wait_ge(rows_zero, 1)
                for c in range(NT):
                    ins = v.tensor_tensor_scan(rows[32:36, c * P:(c + 1) * P], cc("ones", rows_=slice(32, 36)),
                                               r[:, c * P:(c + 1) * P], 0.0, ALU.mult, ALU.add)
                ins.then_inc(rows_ready, 1)

                for i in range(8):
                    dve.wait_ge(l2_std, l * 8 + i + 1)
                    ch.mark(v.reciprocal(rin[:, i, :], rin[:, i, :]))
                    ch.dep()
                    v.scalar_tensor_tensor(qkn[:, i, :], qkvs[:, i, :], float(P) ** -0.5 if i < 4 else 1.0,
                                           rin[:, i, :], ALU.mult, ALU.mult).then_inc(qk_ready, 1)
                    dve.wait_ge(rope_rot, l * 8 + i + 1)
                    v.tensor_tensor(ropet[:, i, :], bank[4 + i % 2][:, 0:S], cc("sin"),
                                    ALU.mult).then_inc(rope_used, 1)
                    ch.mark(v.tensor_tensor(raw[:, i, :], raw[:, i, :], cc("cos"), ALU.mult))
                    ch.dep()
                    dve.wait_ge(rope_used, l * 8 + i + 1)
                    v.tensor_tensor(raw[:, i, :], raw[:, i, :], ropet[:, i, :], ALU.add).then_inc(rope_done, 1)

                dve.wait_ge(cols_done, l + 1)
                v.tensor_copy(cols[:], bank[4][:, S:S + 128].rearrange("p (c k) -> p c k", c=NT)).then_inc(cols_ready, 1)
                dve.wait_ge(cols_ready, l + 1)
                for i in range(DNH):
                    dve.wait_ge(bc_act, l * 4 + i + 1)
                    for c in range(NT):
                        ins = v.scalar_tensor_tensor(gam[:, i, c * P:(c + 1) * P], bank[i % 2][:, c * P:(c + 1) * P],
                                                     cols[:, c, 32 + i:33 + i], cc("decmask"), ALU.subtract, ALU.add)
                    ins.then_inc(bc_dve, 1)
                    dve.wait_ge(tr_done, l * 4 + i + 1)
                    for c in range(NT):
                        ins = v.tensor_scalar(vb[:, 2 * i + c, :], bank[6 + i % 2][:, c * P:(c + 1) * P],
                                              cols[:, c, i:i + 1], None, ALU.mult)
                    ins.then_inc(tr_dve, 1)
                    dve.wait_ge(gram_done, l * 4 + i + 1)
                    dve.wait_ge(gam_ready, l * 4 + i + 1)
                    dve.wait_ge(gb_ready, l * 4 + i + 1)
                    pair = bank[2 + i % 2][:, :].rearrange("p (c w k) -> p c w k", c=NT, w=2)
                    v.tensor_tensor(qkt[:, 2 * i:2 * i + 2, :], pair[:, :, 1, :],
                                    gam[:, i, :].rearrange("p (c k) -> p c k", c=NT), ALU.mult)
                    v.tensor_tensor(bp[:, 2 * i:2 * i + 2, :], pair[:, :, 0, :],
                                    bbc[:, i, :].rearrange("p (c k) -> p c k", c=NT), ALU.mult).then_inc(gram_used, 1)

                for lev in range(LEVELS):
                    for g in range(2):
                        us = slice(4 * g, 4 * g + 4)
                        t_ps = bank[g][:, :].rearrange("p (u k) -> p u k", u=4)
                        u_ps = bank[2 + g][:, :].rearrange("p (u k) -> p u k", u=4)
                        if lev == 0:
                            eye = ident.unsqueeze(1).to_broadcast([P, 4, P])
                            dve.wait_ge(bl_ready, l * LEVELS + 1)
                            v.tensor_tensor(uinv[:, us, :], eye, bl[:, 0, us, :], ALU.subtract)
                            dve.wait_ge(lev_x, l * 2 * LEVELS + g + 1)
                            v.tensor_tensor(tinv[:, us, :], eye, t_ps, ALU.subtract).then_inc(tu_ready, 1)
                        else:
                            dve.wait_ge(lev_y, l * 2 * (LEVELS - 1) + 2 * (lev - 1) + g + 1)
                            dve.wait_ge(tu_ready, l * 2 * LEVELS + 2 * (lev - 1) + g + 1)
                            if lev < LEVELS - 1:
                                v.tensor_tensor(tinv[:, us, :], tinv[:, us, :], t_ps, ALU.subtract)
                            v.tensor_tensor(uinv[:, us, :], uinv[:, us, :], u_ps, ALU.subtract).then_inc(tu_ready, 1)

                dve.wait_ge(rec_pe, l * 6 + 4)
                v.tensor_tensor(resid[:], vb[:].rearrange("p (i c) k -> p i c k", c=NT)[:, :, 1, :],
                                bank[6][:, :].rearrange("p (i k) -> p i k", i=DNH), ALU.subtract).then_inc(rec_dve, 1)

                def masked(i):
                    dve.wait_ge(att_s, l * 8 + i + 1)
                    ch.mark(v.scalar_tensor_tensor(prob[:, i, :], bank[2 + i % 2][:, 0:3 * P], SWAD ** -0.5,
                                                   cc("dilmask"), ALU.mult, ALU.add))
                    ch.dep()
                    ch.mark(v.tensor_reduce(att_max[:, 2 * i:2 * i + 1], prob[:, i, 0:P], AX_X, ALU.max, negate=True))
                    v.tensor_reduce(att_max[:, 2 * i + 1:2 * i + 2], prob[:, i, P:3 * P], AX_X, ALU.max,
                                    negate=True).then_inc(att_sm, 1)

                def out_norm(g):
                    dve.wait_ge(on_std, l * 2 + g + 1)
                    hs = slice(2 * g, 2 * g + 2)
                    ch.mark(v.reciprocal(rin[:, hs, :], rin[:, hs, :]))
                    ch.dep()
                    ch.mark(v.scalar_tensor_tensor(ot[:, hs, :], ot[:, hs, :], pa_("onorm"), rin[:, hs, :],
                                                   ALU.mult, ALU.mult))
                    ch.dep()
                    ins = v.tensor_tensor(mix[:, hs, :], ot[:, hs, :], zs[:, hs, :], ALU.mult)
                    if g == 1:
                        ins.then_inc(mix_a, 1)

                for i in range(SWAH + 1):
                    if i < SWAH:
                        masked(i)
                    j = i - 1
                    if j >= 0:
                        dve.wait_ge(att_p, l * 8 + j + 1)
                        ch.mark(v.reciprocal(att_rz[:, 2 * j:2 * j + 2], att_z[:, 2 * j:2 * j + 2]))
                        ch.dep()
                        v.tensor_scalar(prob[:, j, 0:P], prob[:, j, 0:P], att_rz[:, 2 * j:2 * j + 1], None, ALU.mult)
                        v.tensor_scalar(prob[:, j, P:3 * P], prob[:, j, P:3 * P], att_rz[:, 2 * j + 1:2 * j + 2], None,
                                        ALU.mult).then_inc(att_pn, 1)
                    if i in (2, 3):
                        out_norm(i - 2)

                take_y(l, 0, lambda m: l * LAYER_TILES + T_WOUT + m + 1)
                dve.wait_ge(y_done, l * 16 + 8)
                norm_add(ch, l * 4 + 1, lambda k: pa_("post", k))
                dve.wait_ge(packf_in, l * 16 + 16)
                dve.wait_ge(norm_out, l * 4 + 2)
                norm_apply(ch, l * 4 + 2, lambda k: pf_("pre", k))

                def glu(p, q):
                    done = l * LAYER_TILES + T_UP + 2 * p
                    start = (l * NP_FF + p) * FFN_LINKS
                    both = ((bank[2 * q], glu_g[:, q, :], 0), (bank[2 * q + 1], glu_v[:, q, :], 1))
                    dve.wait_ge(gelu_done, l * NP_FF + p + 1)
                    dve.wait_ge(hid_done, l * NP_FF + p + 1)
                    for src, dst, w in both:
                        dve.wait_ge(tile_done, done + w + 1)
                        v.tensor_scalar(dst, src[:, 0:S], pf_("conv", p * 6 + w * 3 + 2), pf_("bias", p * 2 + w),
                                        ALU.mult, ALU.add).then_inc(ffn_chain, 1)
                    for j in range(1, FCONV):
                        for src, dst, w in both:
                            dve.wait_ge(ffn_chain, start + 2 * (j - 1) + w + 1)
                            ins = v.scalar_tensor_tensor(dst[:, j:], src[:, 0:S - j], pf_("conv", p * 6 + w * 3 + 2 - j),
                                                         dst[:, j:], ALU.mult, ALU.add)
                            if j < FCONV - 1:
                                ins.then_inc(ffn_chain, 1)
                            elif w == 0:
                                ins.then_inc(glu_ready, 1)
                            else:
                                ins.then_inc(ffn_free, 1)

                with dve.Fori(0, FFN_LOOPS) as i:
                    for q in range(PAIRS):
                        glu(i * PAIRS + q, q)
                for q in range(NP_FF - FFN_LOOPS * PAIRS):
                    glu(FFN_LOOPS * PAIRS + q, q)
                take_y(l, 1, lambda m: l * LAYER_TILES + T_DOWN + ((m + 1) * NP_FF + 7) // 8)
                dve.wait_ge(y_done, l * 16 + 16)
                norm_add(ch, l * 4 + 3, lambda k: pf_("post", k))
                dve.wait_ge(norm_out, l * 4 + 4)
                assert ch.n == DVE_LINKS, ("DVE_LINKS", ch.n)

            with dve.Fori(0, DEPTH) as l:
                layer(l)
            second_vector(dve, norm_apply, softplus)

        @block.gpsimd
        def _(pool):
            pool.dma_start(pa[:], packa[0]).then_inc(packa_in, 16)
            pool.dma_start(pf[:], packf[0]).then_inc(packf_in, 16)
            pl.memset(rows[:], 0.0).then_inc(rows_zero, 1)
            pool.wait_ge(rows_zero, 1)
            for q in range(PAIRS):
                pl.memset(credit[:, 3 * q:3 * q + 1], 0.0).then_inc(hid_done, 1)
                pl.memset(credit[:, 3 * q + 1:3 * q + 2], 0.0).then_inc(ffn_free, 1)
                pl.memset(credit[:, 3 * q + 2:3 * q + 3], 0.0).then_inc(gelu_done, 1)

            def layer(l):
                ch = Chain(pool, pool_chain, l * POOL_LINKS)
                for i in range(DNH):
                    pool.wait_ge(bc_act, l * 4 + i + 1)
                    pool.wait_ge(qk_ready, l * 8 + 8)
                    pl.tensor_tensor(qg[:, i, :], qkn[:, i, P:S], eg1[:, i, :], ALU.mult)
                    ch.mark(pl.tensor_tensor(kbg[:, i, :], qkn[:, 4 + i, P:S], eg1[:, i, :], ALU.mult))
                    ch.dep()
                    pl.tensor_tensor(kbg[:, i, :], kbg[:, i, :], bbc[:, i, P:S], ALU.mult).then_inc(kbg_ready, 1)
                    pool.wait_ge(gam_ready, l * 4 + i + 1)
                    pool.wait_ge(kbg_ready, l * 4 + i + 1)
                    pl.tensor_tensor(bbc[:, i, :], bbc[:, i, :], gam[:, i, :], ALU.mult).then_inc(gb_ready, 1)
                pool.wait_ge(gram_used, l * 4 + 4)
                for lev in range(LEVELS):
                    if lev >= 2:
                        pool.wait_ge(lev_x, l * 2 * LEVELS + 2 * (lev - 1))
                        pool.wait_ge(tu_ready, l * 2 * LEVELS + 2 * (lev - 1))
                    pl.tensor_tensor(bl[:, lev % 2], bp[:], cc("level", lev, P).unsqueeze(1).to_broadcast([P, 8, P]),
                                     ALU.mult).then_inc(bl_ready, 1)

                def product(p, q):
                    pool.wait_ge(gelu_done, l * NP_FF + p + 1 + CREDITS)
                    pool.wait_ge(ffn_free, l * NP_FF + p + 1 + CREDITS)
                    pl.tensor_tensor(hid[:, bass.ds(p * S, S)], glu_a[:, q, :], glu_v[:, q, :], ALU.mult).then_inc(hid_done, 1)

                pool.wait_ge(norm_out, l * 4 + 2)
                pool.dma_start(pa[:], packa[bass.ds(l + 1, 1)].rearrange("o p n -> (o p) n")).then_inc(packa_in, 16)
                with pool.Fori(0, FFN_LOOPS) as i:
                    for q in range(PAIRS):
                        product(i * PAIRS + q, q)
                for q in range(NP_FF - FFN_LOOPS * PAIRS):
                    product(FFN_LOOPS * PAIRS + q, q)
                pool.wait_ge(norm_out, l * 4 + 4)
                pool.dma_start(pf[:], packf[bass.ds(l + 1, 1)].rearrange("o p n -> (o p) n")).then_inc(packf_in, 16)
                assert ch.n == POOL_LINKS, ("POOL_LINKS", ch.n)

            with pool.Fori(0, DEPTH) as l:
                layer(l)
            second_pool(pool)


def shape_constants():
    c = np.zeros((P, C_W), np.float32)

    def put(name, value):
        lo, hi = C_COLS[name]
        value = np.asarray(value, np.float32)
        c[:value.shape[0], lo:hi] = value

    i = np.arange(P)
    put("ident", np.eye(P))
    put("ones", np.ones((P, P)))
    put("ones256", np.ones((P, S)))
    put("bd64", i[:, None] // 64 == i[None, :] // 64)
    half, d = ROPE_DIM // 2, i % SWAD
    rot = np.zeros((P, P))
    for o in range(P):
        if d[o] < half:
            rot[o + half, o] = -1.0
        elif d[o] < ROPE_DIM:
            rot[o - half, o] = 1.0
    put("rot", rot)
    freq = np.float32(ROPE_THETA) ** (-np.arange(0, ROPE_DIM, 2, dtype=np.float32) / np.float32(ROPE_DIM))
    angle = np.arange(S, dtype=np.float32)[None, :] * freq[:, None]
    cos, sin = np.ones((P, S), np.float32), np.zeros((P, S), np.float32)
    for o in range(P):
        if d[o] < ROPE_DIM:
            cos[o], sin[o] = np.cos(angle[d[o] % half]), np.sin(angle[d[o] % half])
    put("cos", cos)
    put("sin", sin)
    put("decmask", np.where(i[None, :] >= i[:, None], 0.0, NEG))
    levels = []
    for lev in range(LEVELS):
        b = 2 ** lev
        same = i[:, None] // (2 * b) == i[None, :] // (2 * b)
        levels.append(same & (i[:, None] % (2 * b) < b) & (i[None, :] % (2 * b) >= b))
    put("level", np.concatenate(levels, axis=1))
    times = np.zeros((S, S))
    dist = np.arange(S)[:, None] - np.arange(S)[None, :]
    for window, dil in DIL:
        times += (dist >= 0) & (dist <= window) & (dist % dil == 0)
    logs = np.where(times > 0, np.log(np.maximum(times, 1)), NEG)
    put("dilmask", np.concatenate([logs[0:P, 0:P], logs[P:S, :]], axis=1))
    causal = np.where(dist >= 0, 0.0, NEG)
    put("causal", np.concatenate([causal[0:P, 0:P], causal[P:S, :]], axis=1))
    put("eps", np.full((P, 1), EPS))
    put("gmask", np.arange(GB)[None, :] >= i[:, None] % GB)
    put("selhead", i[:, None] // GDK == np.arange(GH)[None, :])
    put("first4", np.tile([4.0, 3.0, 2.0, 1.0], (P, 1)))
    return c


def kernel(**inputs):
    import concourse.bacc as bacc
    from concourse.bass_utils import run_bass_kernel_spmd

    w = {k: np.asarray(a) for k, a in inputs.items()}

    def tiles(m):
        k, n = m.shape
        return m.reshape(k // P, P, n // P, P).transpose(2, 1, 0, 3).reshape(n // P, P, k)

    def blocks(m, order):
        b = np.stack([m[r * P:(r + 1) * P, c * P:(c + 1) * P] for r, c in order])
        return b.reshape(-1, 8, P, P).transpose(0, 2, 1, 3).reshape(-1, P, 8 * P)

    def cols(v):
        return v.reshape(-1, P).T

    parts = []
    packa = np.zeros((DEPTH + 1, P, A_W), np.float32)
    packf = np.zeros((DEPTH + 1, P, F_W), np.float32)
    packb = np.zeros((P, B_W), np.float32)

    def put(pack, table, name, value):
        lo, hi = table[name]
        value = value.reshape(value.shape[0], -1)
        assert value.shape[1] == hi - lo, name
        pack[:value.shape[0], lo:hi] = value

    for l in range(DEPTH):
        wi = w["w_in"][l]
        small = 4 * DNH * P
        parts.append(tiles(wi[:, :small]))
        parts.append(tiles(wi[:, small + 2 * DNH:]))
        parts.append(tiles(w["w_out"][l]))
        up = tiles(w["ffn_up"][l])
        parts.append(np.stack([up[:NP_FF], up[NP_FF:]], 1).reshape(2 * NP_FF, P, KD * P))
        parts.append(blocks(w["ffn_down"][l], [(k, m) for m in range(KD) for k in range(NP_FF)]))
        put(packa[l], A_COLS, "pre", cols(w["pre_mix_norm"][l]))
        put(packa[l], A_COLS, "post", cols(w["post_mix_norm"][l]))
        put(packa[l], A_COLS, "conv", w["dn_conv"][l].reshape(CONV, 12, P).transpose(2, 1, 0))
        put(packa[l], A_COLS, "onorm", w["dn_out_norm"][l].reshape(P, 1))
        lo = A_COLS["alog"][0]
        packa[l, 32:32 + DNH, lo] = w["dn_a_log"][l]
        lo = A_COLS["dt"][0]
        packa[l, 32:32 + DNH, lo] = w["dn_dt_bias"][l]
        ba = np.zeros((P, KD, 64), np.float32)
        ba[:, :, 0:DNH] = wi[:, small:small + DNH].reshape(KD, P, DNH).transpose(1, 0, 2)
        ba[:, :, 32:32 + DNH] = wi[:, small + DNH:small + 2 * DNH].reshape(KD, P, DNH).transpose(1, 0, 2)
        put(packa[l], A_COLS, "wba", ba)
        put(packf[l], F_COLS, "pre", cols(w["pre_ffn_norm"][l]))
        put(packf[l], F_COLS, "post", cols(w["post_ffn_norm"][l]))
        put(packf[l], F_COLS, "conv", w["ffn_conv"][l].reshape(FCONV, 2, NP_FF, P).transpose(3, 2, 1, 0))
        put(packf[l], F_COLS, "bias", w["ffn_conv_bias"][l].reshape(2, NP_FF, P).transpose(2, 1, 0))

    w2 = w["w_in_2"][0]
    edges = np.cumsum([GH * GDK, GH * GDK, GH * GDV, GRANK, GH * GDV, 512, 512, 512, 512])
    gq, gk, gv, glr, gog, cu, dq, dk, dv = np.split(w2, edges[:-1], axis=1)
    ct = tiles(cu)
    parts += [tiles(gq), tiles(gk), ct[[0, 2, 1, 3]], tiles(gog), tiles(gv), tiles(dq), tiles(dk), tiles(dv),
              tiles(w["w_out_2"][0])]
    ups, downs = [], []
    for e in range(NE):
        ups.append(np.concatenate([tiles(w["expert_w_gate_2"][0, e]), tiles(w["expert_w_up_2"][0, e])]))
        downs.append(blocks(w["expert_w_down_2"][0, e], [(k, m) for m in range(KD) for k in range(2)]))
    parts.append(ups[0])
    for e in range(NE - 1):
        parts += [ups[e + 1], downs[e]]
    parts.append(downs[-1])
    wtiles = np.concatenate(parts)
    assert wtiles.shape == (ALL_TILES, P, KD * P)

    put(packb, B_COLS, "mix", cols(w["mix_norm_g_2"][0]))
    put(packb, B_COLS, "ffn", cols(w["ffn_norm_g_2"][0]))
    put(packb, B_COLS, "wglr", glr.reshape(KD, P, GRANK).transpose(1, 0, 2))
    router = np.concatenate([w["router_group_w_2"][0], w["router_expert_w_2"][0]], axis=1)
    put(packb, B_COLS, "wrt", router.reshape(KD, P, NR).transpose(1, 0, 2))
    put(packb, B_COLS, "rbias", np.concatenate([w["router_group_b_2"][0], w["router_expert_b_2"][0]]).reshape(1, NR))
    put(packb, B_COLS, "glab", w["gla_gate_b_2"][0].reshape(P, 1))
    put(packb, B_COLS, "gatew", w["gla_gate_w_2"][0])
    put(packb, B_COLS, "convw", w["conv_w_2"][0].reshape(CW, 2, P).transpose(2, 1, 0))
    for name, key in (("convb", "conv_b_2"), ("cng", "conv_norm_g_2"), ("cnb", "conv_norm_b_2")):
        put(packb, B_COLS, name, cols(w[key][0]))
    for name, key in (("glan", "gla_norm_g_2"), ("qn", "diff_qnorm_g_2"), ("kn", "diff_knorm_g_2")):
        put(packb, B_COLS, name, np.tile(w[key][0], 2).reshape(P, 1))
    put(packb, B_COLS, "subln", w["diff_subln_g_2"][0].reshape(P, 1))
    put(packb, B_COLS, "lam", np.stack([w[f"diff_{n}_2"][0] for n in ("lq1", "lk1", "lq2", "lk2")], axis=1))

    arrays = {
        "xt": np.ascontiguousarray(w["x"][0].T.reshape(KD, P, S).transpose(1, 0, 2)),
        "wtiles": wtiles, "consts": shape_constants(), "packa": packa, "packf": packf, "packb": packb,
    }
    nc = bacc.Bacc("TRN2", target_bir_lowering=False, num_devices=1)
    args = [nc.dram_tensor(name, arr.shape, F32, kind="ExternalInput").ap() for name, arr in arrays.items()]
    out = nc.dram_tensor("out", (P, KD, S), F32, kind="ExternalOutput").ap()
    block_program(nc, *args, out)
    got = run_bass_kernel_spmd(nc, [arrays], core_ids=[0]).results[0]["out"]
    return got.transpose(1, 0, 2).reshape(1, D, S).transpose(0, 2, 1)
```

```python
from contextlib import ExitStack

import concourse.bass as bass
import numpy as np
from concourse import mybir

ALU = mybir.AluOpType
ACT = mybir.ActivationFunctionType
AX_X = mybir.AxisListType.X
F32 = mybir.dt.float32
F32R = mybir.dt.float32r

P = 128
S = 256
NT = S // P
D = 1024
KD = D // P
DEPTH = 2
EPS = 1e-6
NEG = -1e30

DNH, CONV = 4, 4
FF = 2816
NP_FF = FF // P
FCONV = 3
SWAH, SWAD = 8, 64
DIL = ((128, 1), (512, 4), (2048, 16))
ROPE_THETA, ROPE_DIM = 500000.0, 16
LEVELS = 7

GH, GDK, GDV, GRANK, GTAU = 4, 32, 64, 16, 16.0
GB = 32
NGB = S // GB
CW = 31
DFH = 4
LAMBDA_INIT = 0.2
NG, NEG_E, NE = 4, 4, 16
NR = NG + NE

RING = 6
SLOTS = 3
T_Z, T_BQ, T_BV, T_WOUT, T_UP = 12, 16, 24, 28, 36
DOWN_LAG = 2
LAYER_TILES = T_UP + 3 * NP_FF
T2 = DEPTH * LAYER_TILES
U_CONV, U_GOG, U_GV, U_DQ, U_DV, U_WOUT, U_EXP = 2, 6, 8, 10, 18, 22, 30
ALL_TILES = T2 + U_EXP + NE * RING
assert RING % SLOTS == 0 and LAYER_TILES % RING == 0 and (T2 + U_EXP) % RING == 0 and T_UP % RING == 0
PAIRS = 2
PEEL = 2 * DOWN_LAG
GLU_LOOPS = (NP_FF - PEEL) // PAIRS
assert (NP_FF - PEEL) % PAIRS == 0 and SLOTS == 3
CREDITS = PAIRS
MIX2_ORDER = (0, 1, 4, 5, 6, 7, 2, 3)
MIX_ORDER = (4, 5, 6, 7, 0, 1, 2, 3)
EX_CREDITS = 2
NORM2 = DEPTH * 4
U_PAIRS = 12
CONV_VALUES = (U_CONV, U_CONV + 2)


def evacuated(u):
    return sum(i not in CONV_VALUES for i in range(u + 1))


def columns(*widths):
    at, out = 0, {}
    for name, w in widths:
        out[name] = (at, at + w)
        at += w
    return out, at


C_COLS, C_W = columns(
    ("ident", P), ("ones", P), ("bd64", P), ("rot", P), ("cos", S), ("sin", S), ("decmask", P),
    ("level", LEVELS * P), ("dilmask", 3 * P), ("causal", 3 * P), ("eps", 1), ("gmask", GB),
    ("selhead", GH), ("first4", 4), ("ones256", S))
A_COLS, A_W = columns(
    ("pre", KD), ("conv", 12 * CONV), ("onorm", 1), ("alog", 1), ("dt", 1), ("post", KD), ("wba", KD * 64))
F_COLS, F_W = columns(("pre", KD), ("conv", NP_FF * 2 * FCONV), ("bias", NP_FF * 2), ("post", KD))
B_COLS, B_W = columns(
    ("mix", KD), ("ffn", KD), ("wglr", KD * GRANK), ("wrt", KD * NR), ("glab", 1), ("glan", 1),
    ("convw", 2 * CW), ("convb", 2), ("cng", 2), ("cnb", 2), ("qn", 1), ("kn", 1), ("lam", 4),
    ("subln", 1), ("gatew", P), ("rbias", NR))

DVE_LINKS, POOL_LINKS = 94, 4
FFN_LINKS = 2


class Chain:

    def __init__(self, engine, sem, start):
        self.engine, self.sem, self.start, self.n = engine, sem, start, 0

    def mark(self, ins):
        self.n += 1
        ins.then_inc(self.sem, 1)

    def dep(self):
        self.engine.wait_ge(self.sem, self.start + self.n)

    def dep_before(self, back):
        self.engine.wait_ge(self.sem, self.start + self.n - back)


class Arena:

    def __init__(self, region, width):
        self.region, self.width, self.at = region, width, 0

    def take(self, *shape):
        n = int(np.prod(shape))
        assert self.at + n <= self.width, (self.at, n, self.width)
        v = self.region[:, self.at:self.at + n]
        self.at += n
        names = " ".join("abcd"[:len(shape)])
        sizes = {k: s for k, s in zip("abcd", shape)}
        return v if len(shape) == 1 else v.rearrange(f"p ({names}) -> p {names}", **sizes)


def block_program(nc, xt, wtiles, consts, packa, packf, packb, out):
    v, a, pl, t = nc.vector, nc.scalar, nc.gpsimd, nc.tensor
    ctx = ExitStack()
    with ctx:
        def sb(name, *shape):
            return ctx.enter_context(nc.sbuf_tensor(name, [P, *shape], F32))

        def sem(name):
            return ctx.enter_context(nc.semaphore(name))

        x = sb("x", KD, S)
        h = sb("h", KD, S)
        sq = sb("sq", KD, S)
        y = sb("y", KD, S)
        ring = sb("ring", SLOTS, 1024)

        def split(name, *shape):
            return [ctx.enter_context(nc.sbuf_tensor(f"{name}_{part}", [P, *shape], F32R)) for part in ("hi", "lo")]

        w_hi, w_lo = split("w", SLOTS, 1024)
        act_hi, act_lo = split("act", KD, S)
        cst = sb("cst", C_W)
        pa = sb("pa", A_W)
        pf = sb("pf", F_W)
        pb = sb("pb", B_W)
        std = sb("std", S)
        rstd = sb("rstd", S)
        mix = sb("mix", KD, S)
        ARENA = 22400
        credit = sb("credit", 24)
        region = sb("region", ARENA)
        hid_hi, hid_lo = split("hid", 2, S)

        ar = Arena(region, ARENA)
        qkvc = ar.take(12, S)
        qkvs = ar.take(12, S)
        sqk, ropet, raw, rin8 = sq, y, h, mix
        zs = ar.take(DNH, S)
        vtok = ar.take(NT, 512)
        rows = ar.take(S)
        cols = ar.take(NT, 64)
        rin = ar.take(4, S)
        gam = ar.take(DNH, S)
        bbc = ar.take(DNH, S)
        spt = region[:, ar.at - 8 * S:ar.at - 2 * S].rearrange("p (j s) -> p j s", j=6)
        eg1 = ar.take(DNH, P)
        kbg = ar.take(DNH, P)
        qg = ar.take(DNH, P)
        bp = ar.take(DNH * NT, P)
        qkt = ar.take(DNH * NT, P)
        vb = ar.take(DNH * NT, P)
        kd = ar.take(DNH, P)
        uinv = ar.take(DNH * NT, P)
        vnew = ar.take(2, DNH, P)
        st1 = ar.take(DNH, P)
        resid = ar.take(DNH, P)
        ot = ar.take(DNH, S)
        att_max = ar.take(16)
        att_z = ar.take(16)
        att_rz = ar.take(16)
        pt = ar.take(2, 3 * P)
        prob = region[:, 0:8 * 3 * P].rearrange("p (i k) -> p i k", i=8)
        qkn = qkvc[:, 0:8, :]
        tinv, xs = (sq[:, 4 * i:4 * i + 4, :].rearrange("p a (u k) -> p (a u) k", k=P) for i in range(2))
        bl = y[:].rearrange("p (w a) (u k) -> p w (a u) k", w=2, k=P)

        ar = Arena(region, ARENA)
        glu_g = ar.take(PAIRS, S)
        glu_v = ar.take(PAIRS, S)
        glu_a = ar.take(PAIRS, S)
        glu_p = ar.take(PAIRS, S)

        ar = Arena(region, ARENA)
        g_q = ar.take(S)
        g_k = ar.take(S)
        g_og = ar.take(2, S)
        g_v = ar.take(NT, S)
        g_lr = ar.take(S)
        g_c = ar.take(S)
        g_b = ar.take(S)
        g_ki = ar.take(NGB - 1, S)
        g_ke = ar.take(NGB - 1, S)
        g_qe = ar.take(S)
        g_pr = ar.take(GB, P)
        g_st = ar.take(GH, NT, S)
        g_o = ar.take(2, S)
        g_sq = ar.take(2, S)
        g_std = ar.take(2, S)
        g_rs = ar.take(2, S)
        c_sg = ar.take(2, S)
        c_z = ar.take(2, S + CW - 1)
        c_y = ar.take(2, S)
        c_sq = ar.take(2, S)
        c_std = ar.take(2, S)
        c_rs = ar.take(2, S)
        d_raw, d_sq, d_std = h, sq, y
        d_v = ar.take(NT, 512)
        d_prob = ar.take(8, 3 * P)
        g_sp = region[:, ar.at - 24 * P:ar.at - 12 * P].rearrange("p (j s) -> p j s", j=6)
        d_max = ar.take(16)
        d_z = ar.take(16)
        d_rz = ar.take(16)
        d_pt = ar.take(2, 3 * P)
        d_o, d_osq, d_ostd = y[:, 0:4, :], sq[:, 0:4, :], sq[:, 4:8, :]
        lam_p = ar.take(2)
        lam_e = ar.take(2)
        nlam = ar.take(1)
        ngb = ar.take(1)
        ar = Arena(region, ARENA)
        r_log = ar.take(NT, NR)
        r_max = ar.take(NT)
        r_eq = ar.take(NT, 4)
        r_w = ar.take(NT, 4)
        r_m2 = ar.take(NT)
        r_oh = ar.take(NT, 4)
        r_e = ar.take(NT, 4)
        r_sum = ar.take(NT)
        r_pg = ar.take(NT)
        r_pro = ar.take(NT, 16)
        r_sel = ar.take(NT, 4)
        r_l1 = ar.take(NT)
        r_o1 = ar.take(NT, 4)
        r_s2 = ar.take(NT, 4)
        r_l2 = ar.take(NT)
        r_o2 = ar.take(NT, 4)
        r_d = ar.take(NT)
        r_e2 = ar.take(NT)
        r_u = ar.take(NT)
        r_w1 = ar.take(NT)
        r_w2 = ar.take(NT)
        r_t1 = ar.take(NT, 4)
        r_t2 = ar.take(NT, 4)
        r_gate = ar.take(NT, NE)
        gate_t = ar.take(S)
        gate_bc = ar.take(NE * S)
        e_act = ar.take(2, S)
        e_up = ar.take(2, S)
        e_prod = ar.take(2, S)

        bank = [ctx.enter_context(nc.psum_tensor(f"bank{i}", [P, 512], F32)) for i in range(8)]

        def cc(name, i=0, w=None, rows_=slice(0, P)):
            first, end = C_COLS[name]
            w = end - first if w is None else w
            return cst[rows_, first + i * w:first + (i + 1) * w]

        def pa_(name, i=0, w=1, rows_=slice(0, P)):
            return pa[rows_, A_COLS[name][0] + i:A_COLS[name][0] + i + w]

        def pf_(name, i=0):
            return pf[:, bass.ds(F_COLS[name][0] + i, 1)]

        def pb_(name, i=0, w=1, rows_=slice(0, P)):
            return pb[rows_, B_COLS[name][0] + i:B_COLS[name][0] + i + w]

        ident, ones, bd64, eps = cc("ident"), cc("ones"), cc("bd64"), cc("eps")

        x_in, consts_in, packb_in = sem("x_in"), sem("consts_in"), sem("packb_in")
        packa_in, packf_in = sem("packa_in"), sem("packf_in")
        w_in = [sem(f"w_in{i}") for i in range(SLOTS)]
        hi_ready, lo_ready = sem("hi_ready"), sem("lo_ready")
        tile_done = sem("tile_done")
        dve_chain, pool_chain = sem("dve_chain"), sem("pool_chain")
        norm_sq, norm_sum, norm_std = (sem(f"norm_{n}") for n in ("sq", "sum", "std"))
        h_ready, h_hi, h_lo = (sem(f"h_{n}") for n in ("ready", "hi", "lo"))
        x_ready = sem("x_ready")
        mix_ready, mix_hi, mix_lo = (sem(f"mix_{n}") for n in ("ready", "hi", "lo"))
        conv_ready = sem("conv_ready")
        silu_ready = sem("silu_ready")
        sqk_ready = sem("sqk_ready")
        proj_evac = sem("proj_evac")
        ba_done = sem("ba_done")
        sp_act, sp_dve = sem("sp_act"), sem("sp_dve")
        beta_ready = sem("beta_ready")
        decay_ready = sem("decay_ready")
        rows_ready = sem("rows_ready")
        l2_sum, l2_std, qk_ready = sem("l2_sum"), sem("l2_std"), sem("qk_ready")
        rope_rot, rope_used, rope_done = sem("rope_rot"), sem("rope_used"), sem("rope_done")
        cols_done, cols_ready = sem("cols_done"), sem("cols_ready")
        bc_done, bc_act, bc_dve = sem("bc_done"), sem("bc_act"), sem("bc_dve")
        gam_ready, gb_ready, kbg_ready = sem("gam_ready"), sem("gb_ready"), sem("kbg_ready")
        gram_done, gram_used = sem("gram_done"), sem("gram_used")
        tr_done, tr_dve, tr_act = sem("tr_done"), sem("tr_dve"), sem("tr_act")
        bl_ready = sem("bl_ready")
        lev_x, lev_xs, lev_y, tu_ready = sem("lev_x"), sem("lev_xs"), sem("lev_y"), sem("tu_ready")
        rec_pe, rec_act, rec_dve = sem("rec_pe"), sem("rec_act"), sem("rec_dve")
        on_sum, on_std = sem("on_sum"), sem("on_std")
        att_s, att_sm, att_p, att_pn = (sem(f"att_{n}") for n in ("s", "sm", "p", "pn"))
        att_t, att_pt, att_pv, att_o = (sem(f"att_{n}") for n in ("t", "pt", "pv", "o"))
        y_done = sem("y_done")
        ffn_free = sem("ffn_free")
        ffn_chain = sem("ffn_chain")
        glu_first = sem("glu_first")
        glu_ready, gelu_done, hid_done = sem("glu_ready"), sem("gelu_done"), sem("hid_done")
        prod_done, hi_done = sem("prod_done"), sem("hi_done")
        conv_first = sem("conv_first")
        rows_zero = sem("rows_zero")
        dve_chain2 = sem("dve_chain2")
        lr_done, lr_ready, gz_done, ngb_ready, gc_ready = (sem(f"gla_{n}") for n in ("lr_done", "lr_ready", "gz", "nb", "c"))
        u_evac, cz_zero, cz_ready, cy_ready = sem("u_evac"), sem("cz_zero"), sem("cz_ready"), sem("cy_ready")
        dsq_ready, dn_sum, dn_std, dn_ready = sem("dsq_ready"), sem("dn_sum"), sem("dn_std"), sem("dn_ready")
        lam_ready, lam_sum, lam_exp = sem("lam_ready"), sem("lam_sum"), sem("lam_exp")
        ge_ready, ki_zero, ki_ready = sem("ge_ready"), sem("ki_zero"), sem("ki_ready")
        st_zero, st_done, st_copied = sem("st_zero"), sem("st_done"), sem("st_copied")
        pr_sub, pr_min, pr_exp, pr_q, pr_ready = (sem(f"pr_{n}") for n in ("sub", "min", "exp", "q", "ready"))
        dg_done, dg_ready = sem("dg_done"), sem("dg_ready")
        go_done, go_sq, gn_sum, gn_std, gla_mix = (sem(f"go_{n}") for n in ("done", "sq", "sum", "std", "mix"))
        df_s, df_sm, df_p, df_pn, df_t, df_pt, df_pv, df_o = (
            sem(f"df_{n}") for n in ("s", "sm", "p", "pn", "t", "pt", "pv", "o"))
        do_sum, do_std, diff_mix = sem("do_sum"), sem("do_std"), sem("diff_mix")
        cm_done, cc_ready, csq_ready, cv_done, cv_std, cn_ready, conv_mix = (
            sem(f"conv_{n}") for n in ("mean", "centred", "sq", "var", "std", "norm", "mix"))
        x_added, rt_done, r_sub, r_exp, gates_ready = (sem(f"route_{n}") for n in ("x", "logits", "sub", "exp", "gates"))
        gt_done, gt_ready, gbc_done, gbc_ready = sem("gt_done"), sem("gt_ready"), sem("gbc_done"), sem("gbc_ready")
        ex_act, ex_up, ex_prod, ex_hi, ex_hid, ex_add = (sem(f"ex_{n}") for n in ("act", "up", "prod", "hi", "hid", "add"))
        out_done = sem("out_done")

        def second_tensor(pe, tile_in, product, wblock, project, project_tokens, sum_squares, transpose, scores):
            sum_squares(NORM2)
            pe.wait_ge(packb_in, 16)
            for k in range(KD):
                pe.wait_ge(h_ready, DEPTH * 16 + k + 1)
                mm = t.matmul(bank[5][0:GRANK, 0:S], pb_("wglr", k * GRANK, GRANK), h[:, k, :],
                              start=k == 0, stop=k == KD - 1)
            mm.then_inc(lr_done, 1)
            for u in range(U_WOUT):
                n = T2 + u
                if u >= 4:
                    if u - 4 in CONV_VALUES:
                        pe.wait_ge(cz_ready, CONV_VALUES.index(u - 4) + 1)
                    else:
                        pe.wait_ge(u_evac, evacuated(u - 4))
                if U_GV <= u < U_DQ or u >= U_DV:
                    project_tokens(n, n % SLOTS, bank[u % 4])
                else:
                    project(n, n % SLOTS, bank[u % 4][:, 0:S], (h_lo, DEPTH * 16) if u == 0 else None)
                if u == 2:
                    pe.wait_ge(lr_ready, 1)
                    t.matmul(bank[5][:, S:2 * S], pb_("gatew", 0, P, slice(0, GRANK)), g_lr[0:GRANK, :],
                             start=True, stop=True).then_inc(gz_done, 1)
                if U_DQ + 2 <= u < U_DQ + 10:
                    i = u - U_DQ - 2
                    pe.wait_ge(dsq_ready, i + 1)
                    if i >= 2:
                        pe.wait_ge(dn_std, i - 1)
                    t.matmul(bank[6 + i % 2][:, 0:S], bd64, d_sq[:, i, :], start=True, stop=True).then_inc(dn_sum, 1)
            pe.wait_ge(lam_ready, 1)
            pe.wait_ge(dn_std, 8)
            t.matmul(bank[6][:, 0:2], ones[0:64, :], lam_p[0:64, :], start=True, stop=True).then_inc(lam_sum, 1)

            pe.wait_ge(u_evac, evacuated(U_WOUT - 1))
            pe.wait_ge(ki_ready, 1)
            for i in range(GH):
                ch_ = slice(GDK * i, GDK * i + GDK)
                for jt in range(NT):
                    for b in range(1 + jt * (P // GB), NGB):
                        mm = t.matmul(bank[i][:, jt * S + b * GB:jt * S + (b + 1) * GB],
                                      g_ki[ch_, b - 1, jt * P:(jt + 1) * P], g_qe[ch_, b * GB:(b + 1) * GB],
                                      start=True, stop=True)
                mm.then_inc(st_done, 1)
            for jt in range(NT):
                pe.wait_ge(pr_ready, jt + 1)
                for r in range(GB):
                    mm = t.matmul(bank[4][:, jt * P + r * GH:jt * P + (r + 1) * GH], g_pr[:, r, :], cc("selhead"),
                                  start=True, stop=True)
                mm.then_inc(dg_done, 1)
            pe.wait_ge(dg_ready, 1)
            pe.wait_ge(st_copied, 2 * GH)
            for i in range(GH):
                o_ = bank[5][64 * (i % 2):64 * (i % 2) + 64, i // 2 * S:i // 2 * S + S]
                vals = g_v[:, :, i * GDV:(i + 1) * GDV]
                t.matmul(o_[:, 0:P], vals[:, 0, :], g_st[:, i, 0, 0:P], start=True, stop=True)
                t.matmul(o_[:, P:S], vals[:, 0, :], g_st[:, i, 0, P:S], start=True, stop=False)
                mm = t.matmul(o_[:, P:S], vals[:, 1, :], g_st[:, i, 1, P:S], start=False, stop=True)
            mm.then_inc(go_done, 1)

            pe.wait_ge(dn_ready, 8)
            for i in range(8 + 5):
                if i < 8:
                    if i >= 2:
                        pe.wait_ge(df_sm, i - 1)
                    scores(i, d_raw[:, 0:4, :], d_raw[:, 4:8, :], bank[2 + i % 2]).then_inc(df_s, 1)
                if i == 4:
                    pe.wait_ge(go_sq, 2)
                    for j in range(2):
                        mm = t.matmul(bank[4][:, j * S:(j + 1) * S], bd64, g_sq[:, j, :], start=True, stop=True)
                    mm.then_inc(gn_sum, 1)
                j, odd = divmod(i - 3, 2)
                if 0 <= j < DFH and odd == 0:
                    pe.wait_ge(df_pn, j + 1)
                    if j >= 2:
                        pe.wait_ge(df_pt, j - 1)
                    if j == 0:
                        pe.wait_ge(lam_exp, 1)
                    b = bank[6 + j % 2]
                    transpose(b[:, 0:P], d_prob[:, 2 * j, 0:P])
                    transpose(b[:, P:2 * P], d_prob[:, 2 * j, P:2 * P])
                    transpose(b[:, 2 * P:3 * P], d_prob[:, 2 * j, 2 * P:3 * P]).then_inc(df_t, 1)
                j, odd = divmod(i - 4, 2)
                if 0 <= j < DFH and odd == 0:
                    pe.wait_ge(df_pt, j + 1)
                    if j >= 2:
                        pe.wait_ge(df_o, 2 * j - 2)
                    o_ = bank[j % 2]
                    vals = d_v[:, :, j * P:(j + 1) * P]
                    t.matmul(o_[:, 0:P], vals[:, 0, :], d_pt[:, j % 2, 0:P], start=True, stop=True)
                    t.matmul(o_[:, P:S], vals[:, 0, :], d_pt[:, j % 2, P:2 * P], start=True, stop=False)
                    t.matmul(o_[:, P:S], vals[:, 1, :], d_pt[:, j % 2, 2 * P:3 * P], start=False,
                             stop=True).then_inc(df_pv, 1)
            pe.wait_ge(cy_ready, 1)
            pe.wait_ge(df_sm, 8)
            for j in range(2):
                mm = t.matmul(bank[2][:, j * S:(j + 1) * S], bd64, c_y[:, j, :], start=True, stop=True)
            mm.then_inc(cm_done, 1)
            pe.wait_ge(df_o, 2 * DFH)
            for g in range(2):
                t.matmul(bank[g][:, :], ones, d_osq[:, 2 * g:2 * g + 2, :], start=True, stop=True).then_inc(do_sum, 1)
            pe.wait_ge(csq_ready, 2)
            for j in range(2):
                mm = t.matmul(bank[3][:, j * S:(j + 1) * S], bd64, c_sq[:, j, :], start=True, stop=True)
            mm.then_inc(cv_done, 1)

            for m in range(KD):
                n = T2 + U_WOUT + m
                tile_in(n)
                if m >= 4:
                    pe.wait_ge(x_added, m - 3)
                for i, k in enumerate(MIX2_ORDER):
                    if m == 0:
                        pe.wait_ge(mix_lo, DEPTH * KD + i + 1)
                    mm = product(bank[4 + m % 4][:, 0:S], wblock(n % SLOTS, k), (act_hi[:, k, :], act_lo[:, k, :]),
                                 i == 0, i == KD - 1)
                mm.then_inc(tile_done, 1)

            sum_squares(NORM2 + 1)
            pe.wait_ge(h_ready, DEPTH * 16 + 16)
            for c in range(NT):
                for k in range(KD):
                    t.matmul(bank[5][:, c * NR:(c + 1) * NR], h[:, k, c * P:(c + 1) * P], pb_("wrt", k * NR, NR),
                             start=k == 0, stop=False)
                mm = t.matmul(bank[5][:, c * NR:(c + 1) * NR], ones[0:1, :], pb_("rbias", 0, NR, slice(0, 1)),
                              start=False, stop=True)
            mm.then_inc(rt_done, 1)

            def expert_up(n, e, slots):
                for j, s in enumerate(slots):
                    if j < 2:
                        pe.wait_ge(ex_act, 2 * e + j - 1)
                    else:
                        pe.wait_ge(ex_up, 2 * e + j - 3)
                    project(n + j, s, bank[j][:, 0:S])

            def expert_down(n, e, slots):
                pe.wait_ge(ex_hid, 2 * e + 2 + EX_CREDITS)
                for j, s in enumerate(slots):
                    tile_in(n + j)
                    for m in range(4 * j, 4 * j + 4):
                        if m % 2 == 0:
                            pe.wait_ge(ex_add, 4 * e + m // 2 + 1)
                        for k in range(2):
                            mm = product(bank[4 + m // 2][:, m % 2 * S:m % 2 * S + S], wblock(s, (m % 4) * 2 + k),
                                         (hid_hi[:, k, :], hid_lo[:, k, :]), k == 0, k == 1)
                    mm.then_inc(tile_done, 1)

            first = T2 + U_EXP
            for j in range(4):
                project(first + j, j % SLOTS, bank[j][:, 0:S], (h_lo, DEPTH * 16 + 8) if j == 0 else None)
            pe.wait_ge(gates_ready, 1)
            for c in range(NT):
                mm = transpose(bank[4][0:NE, c * P:(c + 1) * P], r_gate[:, c, :])
            mm.then_inc(gt_done, 1)
            pe.wait_ge(gt_ready, 1)
            for i in range(NE // 2):
                if i >= 2:
                    pe.wait_ge(gbc_ready, i - 1)
                for j in range(2):
                    mm = t.matmul(bank[6 + i % 2][:, j * S:(j + 1) * S],
                                  ident[0:NE, 2 * i + j:2 * i + j + 1].to_broadcast([NE, P]), gate_t[0:NE, :],
                                  start=True, stop=True)
                mm.then_inc(gbc_done, 1)
            with pe.Fori(0, NE - 1) as e:
                expert_up(e * RING + (first + 4), e + 1, (1, 2, 0, 1))
                expert_down(e * RING + (first + 8), e, (2, 0))
            expert_down(first + NE * RING - 2, NE - 1, (1, 2))

        def second_scalar(act, pre_norm, softplus, refill_hi):
            def refill(u):
                refill_hi(T2 // SLOTS, u)

            def mix_part(k):
                a.activation(act_hi[:, k, :], mix[:, k, :], ACT.Copy).then_inc(mix_hi, 1)

            pre_norm(NORM2, x_ready, DEPTH * 16, DEPTH * 16)
            act.wait_ge(lr_done, 1)
            a.activation(g_lr[0:GRANK, :], bank[5][0:GRANK, 0:S], ACT.Copy).then_inc(lr_ready, 1)
            act.wait_ge(packb_in, 16)
            for u in range(U_WOUT):
                src = bank[u % 4]
                halves = src[:, 0:S].rearrange("p (c d) -> p c d", c=NT)
                act.wait_ge(tile_done, T2 + u + 1)
                if u < 2:
                    a.activation((g_q, g_k)[u], src[:, 0:S], ACT.Copy, scale=(GDK ** -0.5, 1.0)[u]).then_inc(u_evac, 1)
                elif u in CONV_VALUES:
                    pass
                elif u < U_GOG:
                    a.activation(c_sg[:, u // 2 - 1, :], src[:, 0:S], ACT.Sigmoid).then_inc(u_evac, 1)
                elif u < U_GV:
                    a.activation(g_og[:, u - U_GOG, :], src[:, 0:S], ACT.Silu).then_inc(u_evac, 1)
                elif u < U_DQ:
                    j = u - U_GV
                    a.activation(g_v[:, :, j * P:(j + 1) * P], halves, ACT.Copy).then_inc(u_evac, 1)
                elif u < U_DV:
                    i = u - U_DQ
                    a.activation(d_sq[:, i, :], src[:, 0:S], ACT.Square).then_inc(dsq_ready, 1)
                    a.activation(d_raw[:, i, :], src[:, 0:S], ACT.Copy).then_inc(u_evac, 1)
                else:
                    j = u - U_DV
                    a.activation(d_v[:, :, j * P:(j + 1) * P], halves, ACT.Copy).then_inc(u_evac, 1)
                if U_GOG - 1 <= u < U_GOG + 2:
                    if u == U_GOG - 1:
                        act.wait_ge(gz_done, 1)
                        act.wait_ge(ngb_ready, 1)
                    softplus(u - U_GOG + 1, DEPTH, bank[5][:, S:2 * S], ngb, -1.0, g_sp, 0, P)
                refill(u)
                if U_GV <= u < U_GV + 4:
                    if u == U_GV:
                        act.wait_ge(gc_ready, 1)
                    for b in range(1 + 2 * (u - U_GV), min(NGB, 3 + 2 * (u - U_GV))):
                        end = b * GB - 1
                        a.activation(g_ke[:, b - 1, 0:b * GB], g_c[:, 0:b * GB], ACT.Exp, bias=g_b[:, end:end + 1])
                        ins = a.activation(g_qe[:, b * GB:(b + 1) * GB], g_c[:, b * GB:(b + 1) * GB], ACT.Exp,
                                           bias=g_c[:, end:end + 1], scale=-1.0)
                        if b == NGB - 1:
                            ins.then_inc(ge_ready, 1)
                if U_DQ + 2 <= u < U_DQ + 10:
                    i = u - U_DQ - 2
                    act.wait_ge(dn_sum, i + 1)
                    a.activation(d_std[:, i, :], bank[6 + i % 2][:, 0:S], ACT.Sqrt, bias=eps,
                                 scale=1.0 / 64).then_inc(dn_std, 1)
                if u == U_PAIRS + 1:
                    act.wait_ge(pr_min, 1)
                    a.activation(g_pr[:], g_pr[:], ACT.Exp).then_inc(pr_exp, 1)
            act.wait_ge(lam_sum, 1)
            a.activation(lam_e[:], bank[6][:, 0:2], ACT.Exp).then_inc(lam_exp, 1)
            act.wait_ge(st_zero, 1)
            for i in range(GH):
                act.wait_ge(st_done, i + 1)
                a.activation(g_st[:, i, 0, GB:S], bank[i][:, GB:S], ACT.Copy).then_inc(st_copied, 1)
                a.activation(g_st[:, i, 1, P + GB:S], bank[i][:, S + P + GB:2 * S], ACT.Copy).then_inc(st_copied, 1)
            act.wait_ge(pr_min, 2)
            a.activation(g_pr[:], g_pr[:], ACT.Exp).then_inc(pr_exp, 1)
            act.wait_ge(go_done, 1)
            outs = bank[5][:, :].rearrange("p (j s) -> p j s", j=2)
            a.activation(g_sq[:], outs, ACT.Square).then_inc(go_sq, 1)
            a.activation(g_o[:], outs, ACT.Copy).then_inc(go_sq, 1)
            for i in range(8 + 5):
                if i < 8:
                    act.wait_ge(df_sm, i + 1)
                    a.activation(d_prob[:, i, 0:P], d_prob[:, i, 0:P], ACT.Exp, bias=d_max[:, 2 * i:2 * i + 1],
                                 accum_out=d_z[:, 2 * i:2 * i + 1])
                    a.activation(d_prob[:, i, P:3 * P], d_prob[:, i, P:3 * P], ACT.Exp,
                                 bias=d_max[:, 2 * i + 1:2 * i + 2],
                                 accum_out=d_z[:, 2 * i + 1:2 * i + 2]).then_inc(df_p, 1)
                j, odd = divmod(i - 3, 2)
                if 0 <= j < DFH and odd == 0:
                    act.wait_ge(df_t, j + 1)
                    if j >= 2:
                        act.wait_ge(df_pv, j - 1)
                    a.activation(d_pt[:, j % 2, :], bank[6 + j % 2][:, 0:3 * P], ACT.Copy).then_inc(df_pt, 1)
                j, odd = divmod(i - 4, 2)
                if 0 <= j < DFH and odd == 0:
                    act.wait_ge(df_pv, j + 1)
                    a.activation(d_osq[:, j, :], bank[j % 2][:, 0:S], ACT.Square).then_inc(df_o, 1)
                    a.activation(d_o[:, j, :], bank[j % 2][:, 0:S], ACT.Copy).then_inc(df_o, 1)
            act.wait_ge(gn_sum, 1)
            a.activation(g_std[:], bank[4][:, :].rearrange("p (j s) -> p j s", j=2), ACT.Sqrt, bias=eps,
                         scale=1.0 / GDV).then_inc(gn_std, 1)
            for g in range(2):
                act.wait_ge(do_sum, g + 1)
                a.activation(d_ostd[:, 2 * g:2 * g + 2, :], bank[g][:, :].rearrange("p (j s) -> p j s", j=2), ACT.Sqrt,
                             bias=eps, scale=1.0 / P).then_inc(do_std, 1)
            act.wait_ge(gla_mix, 1)
            for k in range(2):
                mix_part(k)
            for j in range(2):
                act.wait_ge(cc_ready, j + 1)
                a.activation(c_sq[:, j, :], c_y[:, j, :], ACT.Square).then_inc(csq_ready, 1)
            for g in range(2):
                act.wait_ge(diff_mix, g + 1)
                for k in range(4 + 2 * g, 6 + 2 * g):
                    mix_part(k)
            act.wait_ge(cv_done, 1)
            a.activation(c_std[:], bank[3][:, :].rearrange("p (j s) -> p j s", j=2), ACT.Sqrt, bias=eps,
                         scale=1.0 / 64).then_inc(cv_std, 1)
            for j in range(2):
                act.wait_ge(cn_ready, j + 1)
                a.activation(mix[:, 2 + j, :], c_y[:, j, :], ACT.Silu, bias=pb_("cnb", j),
                             scale=pb_("cng", j)).then_inc(conv_mix, 1)
            for j in range(2):
                act.wait_ge(conv_mix, j + 1)
                mix_part(2 + j)
            for m in range(KD):
                refill(U_WOUT + m)
            pre_norm(NORM2 + 1, x_added, 0, DEPTH * 16 + 8)

            first = (T2 + U_EXP) // SLOTS

            def gate(r, at, e, j):
                act.wait_ge(tile_done, r * SLOTS + at + j + 1)
                act.wait_ge(ex_hid, 2 * e + j + 1)
                a.activation(e_act[:, j, :], bank[j][:, 0:S], ACT.Silu).then_inc(ex_act, 1)

            act.wait_ge(r_sub, 1)
            a.activation(r_e[:], r_e[:], ACT.Exp).then_inc(r_exp, 1)
            gate(first, 0, 0, 0)
            refill_hi(first, 0)
            act.wait_ge(r_sub, 2)
            a.activation(r_e2[:], r_d[:], ACT.Exp).then_inc(r_exp, 1)
            gate(first, 0, 0, 1)
            for j in range(1, 4):
                refill_hi(first, j)
            act.wait_ge(gt_done, 1)
            a.activation(gate_t[0:NE, :], bank[4][0:NE, 0:S], ACT.Copy).then_inc(gt_ready, 1)
            for i in range(NE // 2):
                act.wait_ge(gbc_done, i + 1)
                a.activation(gate_bc[:, 2 * i * S:2 * (i + 1) * S], bank[6 + i % 2][:, :], ACT.Copy).then_inc(gbc_ready, 1)

            def expert(e, refills):
                r = e * (RING // SLOTS) + first
                for j in range(refills):
                    if j < 2:
                        gate(r, 4, e + 1, j)
                    refill_hi(r, 4 + j)

            with act.Fori(0, NE - 2) as e:
                expert(e, RING)
            expert(NE - 2, RING - 1)

        def second_vector(dve, norm_apply, softplus, refill_lo, part_lo):
            def refill(u):
                refill_lo(T2 // SLOTS, u)

            ch = Chain(dve, dve_chain2, 0)
            dve.wait_ge(packb_in, 16)
            v.tensor_scalar(ngb, pb_("glab"), -1.0, None, ALU.mult).then_inc(ngb_ready, 1)
            lam = pb[0:64, B_COLS["lam"][0]:B_COLS["lam"][0] + 4].rearrange("p (a b) -> p a b", b=2)
            v.tensor_tensor(lam_p[0:64, :], lam[:, :, 0], lam[:, :, 1], ALU.mult).then_inc(lam_ready, 1)
            norm_apply(ch, NORM2, lambda k: pb_("mix", k), DEPTH * 16)

            def conv_value(j):
                dve.wait_ge(cz_zero, 1)
                dve.wait_ge(u_evac, evacuated(CONV_VALUES[j] + 1))
                dve.wait_ge(tile_done, T2 + CONV_VALUES[j] + 1)
                v.tensor_tensor(c_z[:, j, CW - 1:], bank[CONV_VALUES[j] % 4][:, 0:S], c_sg[:, j, :],
                                ALU.mult).then_inc(cz_ready, 1)

            def log_decays():
                r = softplus(2, ch, DEPTH, g_sp, 0, P)
                ch.mark(v.tensor_tensor_scan(r, cc("ones256"), r, 0.0, ALU.mult, ALU.add))
                ch.dep()
                ch.mark(v.tensor_scalar(g_b, r, -1.0 / GTAU, None, ALU.mult))
                v.tensor_scalar(g_c, r, 1.0 / GTAU, None, ALU.mult).then_inc(gc_ready, 1)

            def taps(first, end):
                if first == 0:
                    dve.wait_ge(cz_ready, 2)
                for w in range(first, end):
                    if w:
                        ch.dep()
                    for j in range(2):
                        src = c_z[:, j, w:w + S]
                        if w == 0:
                            ins = v.tensor_scalar(c_y[:, j, :], src, pb_("convw", j * CW), pb_("convb", j), ALU.mult, ALU.add)
                        else:
                            ins = v.scalar_tensor_tensor(c_y[:, j, :], src, pb_("convw", j * CW + w), c_y[:, j, :],
                                                         ALU.mult, ALU.add)
                        if w < CW - 1 or j == 0:
                            ch.mark(ins)
                if end == CW:
                    ins.then_inc(cy_ready, 1)

            def between_blocks():
                dve.wait_ge(ge_ready, 1)
                dve.wait_ge(ki_zero, 1)
                for b in range(1, NGB):
                    v.tensor_tensor(g_ki[:, b - 1, 0:b * GB], g_ke[:, b - 1, 0:b * GB], g_k[:, 0:b * GB], ALU.mult)
                v.tensor_tensor(g_qe[:, GB:], g_qe[:, GB:], g_q[:, GB:], ALU.mult).then_inc(ki_ready, 1)

            def in_block(jt):
                dve.wait_ge(pr_sub, jt + 1)
                v.tensor_scalar(g_pr[:], g_pr[:], 0.0, None, ALU.min).then_inc(pr_min, 1)

            def in_block_q(jt):
                dve.wait_ge(pr_exp, jt + 1)
                pr = g_pr[:].rearrange("p r (b j) -> p b r j", b=P // GB)
                q_i = g_q[:, jt * P:(jt + 1) * P].rearrange("p (b r) -> p b r", r=GB).unsqueeze(3).to_broadcast([P, P // GB, GB, GB])
                v.tensor_tensor(pr, pr, q_i, ALU.mult).then_inc(pr_q, 1)

            def unit(i):
                dve.wait_ge(dn_std, i + 1)
                ch.mark(v.reciprocal(d_std[:, i, :], d_std[:, i, :]))
                ch.dep()
                dve.wait_ge(u_evac, evacuated(U_DQ + i))
                v.scalar_tensor_tensor(d_raw[:, i, :], d_raw[:, i, :], pb_("qn" if i < 4 else "kn"), d_std[:, i, :],
                                       ALU.mult, ALU.mult).then_inc(dn_ready, 1)

            tap = 0
            for u in range(U_WOUT):
                if u in CONV_VALUES:
                    pass
                elif u - 1 in CONV_VALUES:
                    conv_value(CONV_VALUES.index(u - 1))
                if U_GOG - 1 <= u < U_GOG + 1:
                    softplus(u - U_GOG + 1, ch, DEPTH, g_sp, 0, P)
                if u == U_GOG + 1:
                    log_decays()
                if U_GOG <= u < U_PAIRS:
                    taps(tap, tap + 3)
                    tap += 3
                if u == U_PAIRS:
                    between_blocks()
                    in_block(0)
                if U_DQ + 3 <= u < U_DQ + 11:
                    unit(u - U_DQ - 3)
                refill(u)
            dve.wait_ge(lam_exp, 1)
            ch.mark(v.scalar_tensor_tensor(nlam, lam_e[:, 1:2], -LAMBDA_INIT, lam_e[:, 0:1], ALU.add, ALU.subtract))
            in_block_q(0)
            taps(tap, CW)
            in_block(1)
            in_block_q(1)
            dve.wait_ge(st_copied, 2 * GH)
            for jt in range(NT):
                dve.wait_ge(dg_done, NT)
                for b in range(P // GB):
                    ps_ = slice(b * GB, (b + 1) * GB)
                    at = jt * P + b * GB
                    ins = v.tensor_tensor(
                        g_st[ps_, :, jt, at:at + GB],
                        bank[4][ps_, jt * P:(jt + 1) * P].rearrange("p (r i) -> p i r", i=GH),
                        cc("gmask", rows_=ps_).unsqueeze(1).to_broadcast([GB, GH, GB]), ALU.mult)
            ins.then_inc(dg_ready, 1)

            def masked(i):
                dve.wait_ge(df_s, i + 1)
                ch.mark(v.scalar_tensor_tensor(d_prob[:, i, :], bank[2 + i % 2][:, 0:3 * P], 64 ** -0.5,
                                               cc("causal"), ALU.mult, ALU.add))
                ch.dep()
                ch.mark(v.tensor_reduce(d_max[:, 2 * i:2 * i + 1], d_prob[:, i, 0:P], AX_X, ALU.max, negate=True))
                v.tensor_reduce(d_max[:, 2 * i + 1:2 * i + 2], d_prob[:, i, P:3 * P], AX_X, ALU.max,
                                negate=True).then_inc(df_sm, 1)

            def difference(j):
                dve.wait_ge(df_p, 2 * j + 2)
                ch.mark(v.reciprocal(d_rz[:, 4 * j:4 * j + 4], d_z[:, 4 * j:4 * j + 4]))
                ch.dep()
                ch.mark(v.tensor_scalar(d_rz[:, 4 * j + 2:4 * j + 4], d_rz[:, 4 * j + 2:4 * j + 4], nlam, None, ALU.mult))
                parts = (slice(0, P), slice(P, 3 * P))
                for c, part in enumerate(parts):
                    ch.mark(v.tensor_scalar(d_prob[:, 2 * j, part], d_prob[:, 2 * j, part],
                                            d_rz[:, 4 * j + c:4 * j + c + 1], None, ALU.mult))
                ch.dep()
                for c, part in enumerate(parts):
                    ins = v.scalar_tensor_tensor(d_prob[:, 2 * j, part], d_prob[:, 2 * j + 1, part],
                                                 d_rz[:, 4 * j + 2 + c:4 * j + 3 + c], d_prob[:, 2 * j, part],
                                                 ALU.mult, ALU.add)
                ins.then_inc(df_pn, 1)

            for i in range(8 + 2):
                if i < 8:
                    masked(i)
                j, odd = divmod(i - 2, 2)
                if 0 <= j < DFH and odd == 0:
                    difference(j)
            dve.wait_ge(cm_done, 1)
            for j in range(2):
                v.scalar_tensor_tensor(c_y[:, j, :], bank[2][:, j * S:(j + 1) * S], -1.0 / 64, c_y[:, j, :],
                                       ALU.mult, ALU.add).then_inc(cc_ready, 1)
            dve.wait_ge(gn_std, 1)
            dve.wait_ge(go_sq, 2)
            ch.mark(v.reciprocal(g_rs[:], g_std[:]))
            ch.dep()
            ch.mark(v.scalar_tensor_tensor(g_o[:], g_o[:], pb_("glan"), g_rs[:], ALU.mult, ALU.mult))
            ch.dep()
            v.tensor_tensor(mix[:, 0:2, :], g_o[:], g_og[:], ALU.mult).then_inc(gla_mix, 1)
            for g in range(2):
                hs = slice(2 * g, 2 * g + 2)
                dve.wait_ge(do_std, g + 1)
                ch.mark(v.reciprocal(d_ostd[:, hs, :], d_ostd[:, hs, :]))
                ch.dep()
                ch.mark(v.tensor_scalar(d_ostd[:, hs, :], d_ostd[:, hs, :], 1.0 - LAMBDA_INIT, None, ALU.mult))
                ch.dep()
                v.scalar_tensor_tensor(mix[:, 4 + 2 * g:6 + 2 * g, :], d_o[:, hs, :], pb_("subln"), d_ostd[:, hs, :],
                                       ALU.mult, ALU.mult).then_inc(diff_mix, 1)
            for i, k in enumerate(MIX2_ORDER[:6]):
                part_lo(k, mix, mix_hi, DEPTH * 4 + i + 1, mix_lo)
            dve.wait_ge(cv_std, 1)
            ch.mark(v.reciprocal(c_rs[:], c_std[:]))
            ch.dep()
            for j in range(2):
                v.tensor_tensor(c_y[:, j, :], c_y[:, j, :], c_rs[:, j, :], ALU.mult).then_inc(cn_ready, 1)
            for i, k in enumerate(MIX2_ORDER[6:]):
                part_lo(k, mix, mix_hi, DEPTH * 4 + 6 + i + 1, mix_lo)
            for m in range(KD):
                dve.wait_ge(tile_done, T2 + U_WOUT + m + 1)
                v.tensor_tensor(x[:, m, :], x[:, m, :], bank[4 + m % 4][:, 0:S], ALU.add).then_inc(x_added, 1)
                refill(U_WOUT + m)
            dve.wait_ge(x_added, KD)
            norm_apply(ch, NORM2 + 1, lambda k: pb_("ffn", k), DEPTH * 16 + 8)

            def b4(col, n=4):
                return col.unsqueeze(2).to_broadcast([P, NT, n])

            order = cc("first4").unsqueeze(1).to_broadcast([P, NT, 4])

            def first_max(vals, best, onehot):
                ch.mark(v.tensor_reduce(best, vals, AX_X, ALU.max))
                ch.dep()
                ch.mark(v.tensor_tensor(r_eq[:], vals, b4(best), ALU.is_equal))
                ch.dep()
                ch.mark(v.tensor_tensor(r_w[:], r_eq[:], order, ALU.mult))
                ch.dep()
                ch.mark(v.tensor_reduce(r_m2[:], r_w[:], AX_X, ALU.max))
                ch.dep()
                ch.mark(v.tensor_tensor(onehot, r_w[:], b4(r_m2), ALU.is_equal))
                ch.dep()

            dve.wait_ge(rt_done, 1)
            ch.mark(v.tensor_copy(r_log[:], bank[5][:, 0:NT * NR].rearrange("p (c n) -> p c n", c=NT)))
            ch.dep()
            first_max(r_log[:, :, 0:NG], r_max, r_oh[:])
            v.tensor_tensor(r_e[:], r_log[:, :, 0:NG], b4(r_max), ALU.subtract).then_inc(r_sub, 1)
            first = (T2 + U_EXP) // SLOTS
            refill_lo(first, 0)
            by_group = r_log[:, :, NG:NR].rearrange("p c (g e) -> p c g e", g=NG)
            pro = r_pro[:].rearrange("p c (g e) -> p c g e", g=NG)
            for c in range(NT):
                ch.mark(v.tensor_tensor(pro[:, c], by_group[:, c], r_oh[:, c, :].unsqueeze(2).to_broadcast([P, NG, 4]), ALU.mult))
            ch.dep()
            ch.mark(v.tensor_reduce(r_sel[:], r_pro[:].rearrange("p c (g e) -> p c e g", g=NG), AX_X, ALU.add))
            ch.dep()
            first_max(r_sel[:], r_l1, r_o1[:])
            ch.mark(v.scalar_tensor_tensor(r_s2[:], r_o1[:], NEG, r_sel[:], ALU.mult, ALU.add))
            ch.dep()
            first_max(r_s2[:], r_l2, r_o2[:])
            v.tensor_tensor(r_d, r_l2, r_l1, ALU.subtract).then_inc(r_sub, 1)
            dve.wait_ge(r_exp, 1)
            ch.mark(v.tensor_reduce(r_sum, r_e[:], AX_X, ALU.add))
            ch.dep()
            ch.mark(v.reciprocal(r_pg, r_sum))
            dve.wait_ge(r_exp, 2)
            ch.mark(v.tensor_scalar(r_u, r_e2, 1.0, None, ALU.add))
            ch.dep()
            ch.mark(v.reciprocal(r_w1, r_u))
            ch.dep()
            ch.mark(v.tensor_tensor(r_w1, r_w1, r_pg, ALU.mult))
            ch.dep()
            ch.mark(v.tensor_tensor(r_w2, r_w1, r_e2, ALU.mult))
            ch.dep()
            ch.mark(v.tensor_tensor(r_t1[:], r_o1[:], b4(r_w1), ALU.mult))
            ch.mark(v.tensor_tensor(r_t2[:], r_o2[:], b4(r_w2), ALU.mult))
            ch.dep()
            ch.mark(v.tensor_tensor(r_t1[:], r_t1[:], r_t2[:], ALU.add))
            ch.dep()
            gates = r_gate[:].rearrange("p c (g e) -> p c g e", g=NG)
            for c in range(NT):
                ins = v.tensor_tensor(gates[:, c], r_oh[:, c, :].unsqueeze(2).to_broadcast([P, NG, 4]),
                                      r_t1[:, c, :].unsqueeze(1).to_broadcast([P, NG, 4]), ALU.mult)
            ins.then_inc(gates_ready, 1)
            for j in range(1, 4):
                refill_lo(first, j)
            dve.wait_ge(gbc_ready, NE // 2)

            def expert_gate(r, at, e, j):
                dve.wait_ge(tile_done, r * SLOTS + at + 2 + j + 1)
                dve.wait_ge(ex_hid, 2 * e + j + 1)
                v.tensor_tensor(e_up[:, j, :], bank[2 + j][:, 0:S], gate_bc[:, bass.ds(e * S, S)],
                                ALU.mult).then_inc(ex_up, 1)

            def expert_hi(e):
                for j in range(2):
                    dve.wait_ge(ex_act, 2 * e + j + 1)
                    dve.wait_ge(ex_up, 2 * e + j + 1)
                    v.tensor_tensor(hid_hi[:, j, :], e_act[:, j, :], e_up[:, j, :], ALU.mult).then_inc(ex_hi, 1)

            def expert_add(r, at, j):
                dve.wait_ge(tile_done, r * SLOTS + at + j + 1)
                for b in range(2 * j, 2 * j + 2):
                    v.tensor_tensor(x[:, 2 * b:2 * b + 2, :], x[:, 2 * b:2 * b + 2, :],
                                    bank[4 + b][:, :].rearrange("p (j s) -> p j s", j=2), ALU.add).then_inc(ex_add, 1)

            def expert(e, refills):
                r = e * (RING // SLOTS) + first
                for j in range(RING):
                    if 2 <= j < 4:
                        expert_gate(r, 4, e + 1, j - 2)
                    if j >= 4:
                        expert_add(r, 8, j - 4)
                    if j < refills:
                        refill_lo(r, 4 + j)
                expert_hi(e + 1)

            for j in range(2):
                expert_gate(first, 0, 0, j)
            expert_hi(0)
            with dve.Fori(0, NE - 2) as e:
                expert(e, RING)
            expert(NE - 2, RING - 1)
            for j in range(2):
                expert_add(first + (NE - 1) * (RING // SLOTS), 4, j)

        def second_pool(pool):
            pool.wait_ge(x_ready, DEPTH * 16 + 8)
            pl.memset(g_ki[:], 0.0).then_inc(ki_zero, 1)
            pl.memset(c_z[:, :, 0:CW - 1], 0.0).then_inc(cz_zero, 1)
            pl.memset(g_st[:], 0.0).then_inc(st_zero, 1)
            for jt in range(NT):
                nb = P // GB
                pr = g_pr[:].rearrange("p r (b j) -> p b r j", b=nb)
                here = slice(jt * P, (jt + 1) * P)
                b_i = g_b[:, here].rearrange("p (b r) -> p b r", r=GB).unsqueeze(3).to_broadcast([P, nb, GB, GB])
                b_j = g_b[:, here].rearrange("p (b j) -> p b j", j=GB).unsqueeze(2).to_broadcast([P, nb, GB, GB])
                k_j = g_k[:, here].rearrange("p (b j) -> p b j", j=GB).unsqueeze(2).to_broadcast([P, nb, GB, GB])
                pool.wait_ge(gc_ready, 1)
                if jt:
                    pool.wait_ge(dg_done, jt)
                pl.tensor_tensor(pr, b_i, b_j, ALU.subtract).then_inc(pr_sub, 1)
                pool.wait_ge(pr_q, jt + 1)
                pl.tensor_tensor(pr, pr, k_j, ALU.mult).then_inc(pr_ready, 1)
            pool.wait_ge(x_added, KD)
            for j in range(EX_CREDITS):
                pl.memset(credit[:, j:j + 1], 0.0).then_inc(ex_hid, 1)
            for j in range(4):
                pl.memset(credit[:, 2 + j:3 + j], 0.0).then_inc(ex_add, 1)

            def expert(e):
                for j in range(2):
                    pool.wait_ge(ex_act, 2 * e + j + 1)
                    pool.wait_ge(ex_up, 2 * e + j + 1)
                    pool.wait_ge(ex_hid, 2 * e + j + 1)
                    pl.tensor_tensor(e_prod[:, j, :], e_act[:, j, :], e_up[:, j, :], ALU.mult).then_inc(ex_prod, 1)
                    pool.wait_ge(ex_prod, 2 * e + j + 1)
                    pool.wait_ge(ex_hi, 2 * e + j + 1)
                    pl.tensor_tensor(hid_lo[:, j, :], e_prod[:, j, :], hid_hi[:, j, :].bitcast(F32),
                                     ALU.subtract).then_inc(ex_hid, 1)

            with pool.Fori(0, NE) as e:
                expert(e)

        block = ctx.enter_context(nc.Block())

        @block.sync
        def _(sp):
            sp.dma_start(x[:], xt).then_inc(x_in, 16)
            sp.dma_start(cst[:], consts).then_inc(consts_in, 16)
            for s in range(SLOTS):
                sp.dma_start(ring[:, s, :], wtiles[s]).then_inc(w_in[s], 16)
            sp.dma_start(pb[:], packb).then_inc(packb_in, 16)
            for n in range(SLOTS, RING):
                sp.wait_ge(lo_ready, n - SLOTS + 1)
                sp.dma_start(ring[:, n % SLOTS, :], wtiles[n]).then_inc(w_in[n % SLOTS], 16)
            with sp.Fori(1, ALL_TILES // RING) as r:
                for s in range(RING):
                    sp.wait_ge(lo_ready, r * RING + s - SLOTS + 1)
                    sp.dma_start(ring[:, s % SLOTS, :], wtiles[bass.ds(r * RING + s, 1)].rearrange("o p n -> (o p) n")
                                 ).then_inc(w_in[s % SLOTS], 16)
            sp.wait_ge(ex_add, 4 * NE + 4)
            sp.dma_start(out, x[:]).then_inc(out_done, 16)
            sp.wait_ge(out_done, 16)

        @block.tensor
        def _(pe):
            def tile_in(n):
                pe.wait_ge(lo_ready, n + 1)

            def product(out_, w_part, x_parts, first, last):
                (wh, wl), (xh, xl) = w_part, x_parts
                t.matmul(out_, wh, xh, start=first, stop=False)
                t.matmul(out_, wh, xl, start=False, stop=False)
                return t.matmul(out_, wl, xh, start=False, stop=last)

            def wblock(s, k):
                return w_hi[:, s, k * P:(k + 1) * P], w_lo[:, s, k * P:(k + 1) * P]

            def project(n, s, out_, ready=None):
                tile_in(n)
                for k in range(KD):
                    if ready is not None:
                        pe.wait_ge(ready[0], ready[1] + k + 1)
                    mm = product(out_, wblock(s, k), (act_hi[:, k, :], act_lo[:, k, :]), k == 0, k == KD - 1)
                mm.then_inc(tile_done, 1)

            def project_tokens(n, s, out_bank):
                tile_in(n)
                for c in range(NT):
                    for k in range(KD):
                        here = slice(c * P, (c + 1) * P)
                        mm = product(out_bank[:, here], (act_hi[:, k, here], act_lo[:, k, here]), wblock(s, k),
                                     k == 0, k == KD - 1)
                mm.then_inc(tile_done, 1)

            def sum_squares(i):
                for k in range(KD):
                    pe.wait_ge(norm_sq, i * KD + k + 1)
                    mm = t.matmul(bank[0][:, 0:S], ones, sq[:, k, :], start=k == 0, stop=k == KD - 1)
                mm.then_inc(norm_sum, 1)

            def transpose(out_, in_):
                return t.transpose(out_, in_, ident)

            def scores(i, q, k, b):
                lo, j = 64 * (i % 2), i // 2
                t.matmul(b[:, 0:P], q[lo:lo + 64, j, 0:P], k[lo:lo + 64, j, 0:P], start=True, stop=True)
                return t.matmul(b[:, P:3 * P], q[lo:lo + 64, j, P:S], k[lo:lo + 64, j, :], start=True, stop=True)

            pe.wait_ge(consts_in, 16)

            def layer(l):
                sum_squares(l * 4)
                pe.wait_ge(packa_in, l * 16 + 16)
                for n in range(T_WOUT):
                    if 4 <= n < T_Z + 4:
                        pe.wait_ge(conv_ready, l * 12 + n - 3)
                    elif n >= T_Z + 4:
                        pe.wait_ge(proj_evac, l * 16 + n - T_Z - 3)
                    if n < T_BV:
                        project(l * LAYER_TILES + n, n % SLOTS, bank[n % 4][:, 0:S], (h_lo, l * 16) if n == 0 else None)
                    else:
                        project_tokens(l * LAYER_TILES + n, n % SLOTS, bank[n % 4])
                    if n == T_Z - 1:
                        for k in range(KD):
                            mm = t.matmul(bank[4][0:64, S:2 * S], pa_("wba", k * 64, 64), h[:, k, :],
                                          start=k == 0, stop=k == KD - 1)
                        mm.then_inc(ba_done, 1)
                    if T_BQ <= n < T_BQ + 8:
                        i = n - T_BQ
                        pe.wait_ge(sqk_ready, l * 8 + i + 1)
                        if i >= 2:
                            pe.wait_ge(l2_std, l * 8 + i - 1)
                        t.matmul(bank[6 + i % 2][:, 0:S], ones, sqk[:, i, :], start=True, stop=True).then_inc(l2_sum, 1)
                    if T_BQ + 2 <= n < T_BQ + 10:
                        j = n - T_BQ - 2
                        pe.wait_ge(proj_evac, l * 16 + 4 + j + 1)
                        if j >= 2:
                            pe.wait_ge(rope_used, l * 8 + j - 1)
                        t.matmul(bank[4 + j % 2][:, 0:S], cc("rot"), raw[:, j, :],
                                 start=True, stop=True).then_inc(rope_rot, 1)

                pe.wait_ge(rows_ready, l + 1)
                pe.wait_ge(rope_used, l * 8 + 8)
                for c in range(NT):
                    mm = t.matmul(bank[4][:, S + 64 * c:S + 64 * c + 64], rows[0:64, c * P:(c + 1) * P],
                                  ident[0:64, 0:64], start=True, stop=True)
                mm.then_inc(cols_done, 1)
                pe.wait_ge(proj_evac, l * 16 + 16)
                pe.wait_ge(l2_std, l * 8 + 8)
                pe.wait_ge(qk_ready, l * 8 + 8)
                for i in range(DNH):
                    if i >= 2:
                        pe.wait_ge(bc_act, l * 4 + i - 1)
                        pe.wait_ge(bc_dve, l * 4 + i - 1)
                    t.matmul(bank[i % 2][:, 0:S], ident[0:64, 32 + i:33 + i].to_broadcast([64, P]), rows[0:64, :],
                             start=True, stop=True)
                    t.matmul(bank[i % 2][:, S:2 * S], ident[0:64, i:i + 1].to_broadcast([64, P]), rows[0:64, :],
                             start=True, stop=True).then_inc(bc_done, 1)
                    if i >= 2:
                        pe.wait_ge(tr_dve, l * 4 + i - 1)
                        pe.wait_ge(tr_act, l * 4 + i - 1)
                    pe.wait_ge(silu_ready, l * 12 + 8 + i + 1)
                    transpose(bank[6 + i % 2][:, 0:P], qkvs[:, 8 + i, 0:P])
                    transpose(bank[6 + i % 2][:, P:2 * P], qkvs[:, 8 + i, P:S])
                    transpose(bank[6 + i % 2][:, 2 * P:3 * P], qkn[:, 4 + i, 0:P]).then_inc(tr_done, 1)
                    if i >= 2:
                        pe.wait_ge(gram_used, l * 4 + i - 1)
                    for c in range(NT):
                        keys = qkn[:, 4 + i, c * P:(c + 1) * P]
                        t.matmul(bank[2 + i % 2][:, c * S:c * S + P], keys, keys, start=True, stop=True)
                        mm = t.matmul(bank[2 + i % 2][:, c * S + P:c * S + 2 * P], keys, qkn[:, i, c * P:(c + 1) * P],
                                      start=True, stop=True)
                    mm.then_inc(gram_done, 1)

                def attend(i):
                    if i == 0:
                        pe.wait_ge(rope_done, l * 8 + 8)
                        pe.wait_ge(gram_used, l * 4 + 4)
                    if i < SWAH:
                        if i >= 2:
                            pe.wait_ge(att_sm, l * 8 + i - 1)
                        scores(i, raw[:, 0:4, :], raw[:, 4:8, :], bank[2 + i % 2]).then_inc(att_s, 1)
                    j = i - 2
                    if 0 <= j < SWAH:
                        pe.wait_ge(att_pn, l * 8 + j + 1)
                        if j >= 1:
                            pe.wait_ge(att_pt, l * 8 + j)
                        transpose(bank[4][:, 0:P], prob[:, j, 0:P])
                        transpose(bank[4][:, P:2 * P], prob[:, j, P:2 * P])
                        transpose(bank[4][:, 2 * P:3 * P], prob[:, j, 2 * P:3 * P]).then_inc(att_t, 1)
                    j = i - 3
                    if 0 <= j < SWAH:
                        pe.wait_ge(att_pt, l * 8 + j + 1)
                        if j >= 2 and j % 2 == 0:
                            pe.wait_ge(att_o, l * 8 + j)
                        o_ = bank[5][64 * (j % 2):64 * (j % 2) + 64, :]
                        vals = vtok[:, :, j * 64:(j + 1) * 64]
                        t.matmul(o_[:, 0:P], vals[:, 0, :], pt[:, j % 2, 0:P], start=True, stop=True)
                        t.matmul(o_[:, P:S], vals[:, 0, :], pt[:, j % 2, P:2 * P], start=True, stop=False)
                        t.matmul(o_[:, P:S], vals[:, 1, :], pt[:, j % 2, 2 * P:3 * P], start=False,
                                 stop=True).then_inc(att_pv, 1)

                pe.wait_ge(bc_act, l * 4 + 4)
                pe.wait_ge(bc_dve, l * 4 + 4)
                pe.wait_ge(bl_ready, l * LEVELS + 1)
                for g in range(2):
                    for u in range(4):
                        mm = t.matmul(bank[g][:, u * P:(u + 1) * P], bl[:, 0, 4 * g + u, :], ident, start=True, stop=True)
                    mm.then_inc(lev_x, 1)
                pe.wait_ge(tr_dve, l * 4 + 4)
                pe.wait_ge(tr_act, l * 4 + 4)
                for lev in range(1, LEVELS):
                    pe.wait_ge(bl_ready, l * LEVELS + lev + 1)
                    for g in range(2):
                        pe.wait_ge(tu_ready, l * 2 * LEVELS + 2 * (lev - 1) + g + 1)
                        for u in range(4 * g, 4 * g + 4):
                            mm = t.matmul(bank[6 + g][:, u % 4 * P:u % 4 * P + P], bl[:, lev % 2, u, :], tinv[:, u, :],
                                          start=True, stop=True)
                        mm.then_inc(lev_x, 1)
                    attend(lev - 1)
                    for g in range(2):
                        pe.wait_ge(lev_xs, l * 2 * (LEVELS - 1) + 2 * (lev - 1) + g + 1)
                        for u in range(4 * g, 4 * g + 4):
                            if lev < LEVELS - 1:
                                t.matmul(bank[g][:, u % 4 * P:u % 4 * P + P], uinv[:, u, :], xs[:, u, :],
                                         start=True, stop=True)
                            mm = t.matmul(bank[6 + g][:, u % 4 * P:u % 4 * P + P], xs[:, u, :], uinv[:, u, :],
                                          start=True, stop=True)
                        mm.then_inc(lev_y, 1)

                attend(LEVELS - 1)
                pe.wait_ge(tu_ready, l * 2 * LEVELS + 2 * LEVELS)
                for i in range(DNH):
                    mm = t.matmul(bank[6][:, i * P:(i + 1) * P], uinv[:, 2 * i, :], vb[:, 2 * i, :], start=True, stop=True)
                mm.then_inc(rec_pe, 1)
                attend(LEVELS)
                pe.wait_ge(rec_act, l * 7 + 1)
                for i in range(DNH):
                    mm = t.matmul(bank[7][:, i * P:(i + 1) * P], kd[:, i, :], vnew[:, 0, i, :], start=True, stop=True)
                mm.then_inc(rec_pe, 1)
                for i in range(DNH):
                    mm = t.matmul(bank[0][:, i * P:(i + 1) * P], vnew[:, 0, i, :], qkt[:, 2 * i, :], start=True, stop=True)
                mm.then_inc(rec_pe, 1)
                attend(LEVELS + 1)
                pe.wait_ge(rec_act, l * 7 + 2)
                pe.wait_ge(kbg_ready, l * 4 + 4)
                for i in range(DNH):
                    mm = t.matmul(bank[6][:, i * P:(i + 1) * P], kbg[:, i, :], st1[:, i, :], start=True, stop=True)
                mm.then_inc(rec_pe, 1)
                attend(LEVELS + 2)
                pe.wait_ge(rec_dve, l + 1)
                for i in range(DNH):
                    mm = t.matmul(bank[7][:, i * P:(i + 1) * P], uinv[:, 2 * i + 1, :], resid[:, i, :], start=True, stop=True)
                mm.then_inc(rec_pe, 1)
                attend(LEVELS + 3)
                pe.wait_ge(rec_act, l * 7 + 5)
                for i in range(DNH):
                    t.matmul(bank[6][:, i * P:(i + 1) * P], st1[:, i, :], qg[:, i, :], start=True, stop=False)
                    mm = t.matmul(bank[6][:, i * P:(i + 1) * P], vnew[:, 1, i, :], qkt[:, 2 * i + 1, :],
                                  start=False, stop=True)
                mm.then_inc(rec_pe, 1)
                pe.wait_ge(rec_act, l * 7 + 7)
                for g in range(2):
                    t.matmul(bank[g][:, :], ones, sq[:, 2 * g:2 * g + 2, :], start=True, stop=True).then_inc(on_sum, 1)

                pe.wait_ge(att_sm, l * 8 + 8)
                for m in range(KD):
                    n = T_WOUT + m
                    tile_in(l * LAYER_TILES + n)
                    if m >= 4:
                        pe.wait_ge(y_done, l * 16 + m - 3)
                    for i, k in enumerate(MIX_ORDER):
                        if m == 0:
                            pe.wait_ge(mix_lo, l * KD + i + 1)
                        mm = product(bank[4 + m % 4][:, 0:S], wblock(n % SLOTS, k), (act_hi[:, k, :], act_lo[:, k, :]),
                                     i == 0, i == KD - 1)
                    mm.then_inc(tile_done, 1)
                sum_squares(l * 4 + 1)

                sum_squares(l * 4 + 2)

                def step(r, k, p, q, up=True, down=True, start=False, stop=False, ready=None):
                    if up:
                        pe.wait_ge(ffn_free, l * NP_FF + p + 1)
                        for w in range(2):
                            project(r * SLOTS + (k + w), (k + w) % SLOTS, bank[2 * q + w][:, 0:S],
                                    ready if w == 0 else None)
                        k = k + 2
                    if down:
                        tile_in(r * SLOTS + k)
                        pe.wait_ge(hid_done, l * NP_FF + p + 1)
                        for m in range(KD):
                            mm = product(bank[4 + m // 2][:, m % 2 * S:m % 2 * S + S], wblock(k % SLOTS, m),
                                         (hid_hi[:, q, :], hid_lo[:, q, :]), start and m % 2 == 0,
                                         stop and m % 2 == 1)
                        mm.then_inc(tile_done, 1)

                r0 = l * (LAYER_TILES // SLOTS) + T_UP // SLOTS
                for p in range(DOWN_LAG):
                    step(r0, 2 * p, p, p % PAIRS, down=False, ready=(h_lo, l * 16 + 8) if p == 0 else None)
                for p in range(DOWN_LAG, PEEL):
                    step(r0 + (p - 1), 1, p, p % PAIRS, start=p == DOWN_LAG)
                with pe.Fori(0, GLU_LOOPS) as i:
                    for q in range(PAIRS):
                        step(r0 + i * PAIRS + (q + PEEL - 1), 1, i * PAIRS + (q + PEEL), q)
                for p in range(NP_FF, NP_FF + DOWN_LAG):
                    step(r0 + (NP_FF - 1), 1 + p - NP_FF, p, p % PAIRS, up=False, stop=p == NP_FF + DOWN_LAG - 1)
                sum_squares(l * 4 + 3)

            with pe.Fori(0, DEPTH) as l:
                layer(l)
            second_tensor(pe, tile_in, product, wblock, project, project_tokens, sum_squares, transpose, scores)

        @block.scalar
        def _(act):
            def make_hi(n, s, loads):
                act.wait_ge(w_in[s], loads * 16)
                a.activation(w_hi[:, s, :], ring[:, s, :], ACT.Copy).then_inc(hi_ready, 1)

            def refill_hi(r, k):
                act.wait_ge(tile_done, r * SLOTS + k + 1)
                make_hi(r * SLOTS + k + SLOTS, k % SLOTS, r + (k // SLOTS + 2))

            def square(i, k, src):
                a.activation(sq[:, k, :], src, ACT.Square).then_inc(norm_sq, 1)

            def norm_root(i):
                act.wait_ge(norm_sum, i + 1)
                a.activation(std[:], bank[0][:, 0:S], ACT.Sqrt, bias=eps, scale=1.0 / D).then_inc(norm_std, 1)

            def pre_norm(i, x_parts, first, at):
                for k in range(KD):
                    act.wait_ge(x_parts, first + k + 1)
                    square(i, k, x[:, k, :])
                norm_root(i)
                for k in range(KD):
                    act.wait_ge(h_ready, at + k + 1)
                    a.activation(act_hi[:, k, :], h[:, k, :], ACT.Copy).then_inc(h_hi, 1)

            def post_square(i, m, done):
                act.wait_ge(y_done, done + m + 1)
                square(i, m, y[:, m, :])

            def softplus(step, l, src, bias, scale, sp, lo, hi):
                if step == 0:
                    a.activation(sp[lo:hi, 0, :], src, ACT.Identity, bias=bias, scale=scale).then_inc(sp_act, 1)
                elif step == 1:
                    act.wait_ge(sp_dve, l * 2 + 1)
                    a.activation(sp[lo:hi, 2, :], sp[lo:hi, 1, :], ACT.Exp, scale=-1.0).then_inc(sp_act, 1)
                else:
                    act.wait_ge(sp_dve, l * 2 + 2)
                    a.activation(sp[lo:hi, 4, :], sp[lo:hi, 3, :], ACT.Ln).then_inc(sp_act, 1)

            act.wait_ge(consts_in, 16)
            for n in range(SLOTS):
                make_hi(n, n, 1)

            def layer(l):
                def refill(n):
                    refill_hi(l * (LAYER_TILES // SLOTS), n)

                pre_norm(l * 4, x_ready, l * 16, l * 16)
                act.wait_ge(packa_in, l * 16 + 16)

                def silu(n):
                    act.wait_ge(conv_ready, l * 12 + n + 1)
                    a.activation(qkvs[:, n, :], qkvc[:, n, :], ACT.Silu).then_inc(silu_ready, 1)
                    if n < 8:
                        act.wait_ge(silu_ready, l * 12 + n + 1)
                        a.activation(sqk[:, n, :], qkvs[:, n, :], ACT.Square).then_inc(sqk_ready, 1)

                for n in range(T_Z):
                    act.wait_ge(tile_done, l * LAYER_TILES + n + 1)
                    a.activation(qkvc[:, n, :], bank[n % 4][:, 0:S], ACT.Copy,
                                 scale=pa_("conv", n * CONV + CONV - 1)).then_inc(conv_first, 1)
                    refill(n)
                    if n >= 1:
                        silu(n - 1)
                for n in range(T_Z, T_WOUT):
                    act.wait_ge(tile_done, l * LAYER_TILES + n + 1)
                    src = bank[n % 4]
                    if n < T_BQ:
                        a.activation(zs[:, n - T_Z, :], src[:, 0:S], ACT.Silu).then_inc(proj_evac, 1)
                    elif n < T_BV:
                        a.activation(raw[:, n - T_BQ, :], src[:, 0:S], ACT.Copy).then_inc(proj_evac, 1)
                    else:
                        j = n - T_BV
                        a.activation(vtok[:, :, j * P:(j + 1) * P], src[:, 0:S].rearrange("p (c d) -> p c d", c=NT),
                                     ACT.Copy).then_inc(proj_evac, 1)
                    if n == T_Z:
                        silu(T_Z - 1)
                        act.wait_ge(ba_done, l + 1)
                        act.wait_ge(rows_zero, 1)
                        a.activation(rows[0:4, :], bank[4][0:4, S:2 * S], ACT.Sigmoid).then_inc(beta_ready, 1)
                        a.activation(cols[32:36, 1, 0:1], pa_("alog", rows_=slice(32, 36)), ACT.Exp).then_inc(decay_ready, 1)
                    if T_Z <= n < T_Z + 3:
                        softplus(n - T_Z, l, bank[4][32:36, S:2 * S], pa_("dt", rows_=slice(32, 36)), 1.0, spt, 32, 36)
                    refill(n)
                    if T_BQ <= n < T_BQ + 8:
                        i = n - T_BQ
                        act.wait_ge(l2_sum, l * 8 + i + 1)
                        a.activation(rin8[:, i, :], bank[6 + i % 2][:, 0:S], ACT.Sqrt, bias=eps).then_inc(l2_std, 1)

                for i in range(DNH):
                    act.wait_ge(bc_done, l * 4 + i + 1)
                    a.activation(eg1[:, i, :], bank[i % 2][:, P:S], ACT.Exp)
                    a.activation(bbc[:, i, :], bank[i % 2][:, S:2 * S], ACT.Copy).then_inc(bc_act, 1)
                    act.wait_ge(bc_dve, l * 4 + i + 1)
                    a.activation(gam[:, i, :], gam[:, i, :], ACT.Exp).then_inc(gam_ready, 1)
                    act.wait_ge(tr_dve, l * 4 + i + 1)
                    act.wait_ge(gam_ready, l * 4 + i + 1)
                    a.activation(kd[:, i, :], bank[6 + i % 2][:, 2 * P:3 * P], ACT.Copy,
                                 scale=gam[:, i, P - 1:P]).then_inc(tr_act, 1)

                def attend(i):
                    if i < SWAH:
                        act.wait_ge(att_sm, l * 8 + i + 1)
                        a.activation(prob[:, i, 0:P], prob[:, i, 0:P], ACT.Exp, bias=att_max[:, 2 * i:2 * i + 1],
                                     accum_out=att_z[:, 2 * i:2 * i + 1])
                        a.activation(prob[:, i, P:3 * P], prob[:, i, P:3 * P], ACT.Exp,
                                     bias=att_max[:, 2 * i + 1:2 * i + 2],
                                     accum_out=att_z[:, 2 * i + 1:2 * i + 2]).then_inc(att_p, 1)
                    j = i - 2
                    if 0 <= j < SWAH:
                        act.wait_ge(att_t, l * 8 + j + 1)
                        if j >= 2:
                            act.wait_ge(att_pv, l * 8 + j - 1)
                        a.activation(pt[:, j % 2, :], bank[4][:, 0:3 * P], ACT.Copy).then_inc(att_pt, 1)
                    j = i - 3
                    if j % 2 == 1 and 0 <= j < SWAH:
                        act.wait_ge(att_pv, l * 8 + j + 1)
                        a.activation(mix[:, 4 + j // 2, :], bank[5][:, 0:S], ACT.Copy).then_inc(att_o, 1)
                        a.activation(act_hi[:, 4 + j // 2, :], bank[5][:, 0:S], ACT.Copy).then_inc(att_o, 1)

                for lev in range(1, LEVELS):
                    for g in range(2):
                        act.wait_ge(lev_x, l * 2 * LEVELS + 2 * lev + g + 1)
                        a.activation(xs[:, 4 * g:4 * g + 4, :], bank[6 + g][:, :].rearrange("p (u k) -> p u k", u=4),
                                     ACT.Copy).then_inc(lev_xs, 1)
                    attend(lev - 1)

                def heads(b):
                    return b[:, :].rearrange("p (i k) -> p i k", i=DNH)

                attend(LEVELS - 1)
                act.wait_ge(rec_pe, l * 6 + 1)
                a.activation(vnew[:, 0], heads(bank[6]), ACT.Copy).then_inc(rec_act, 1)
                attend(LEVELS)
                act.wait_ge(rec_pe, l * 6 + 2)
                a.activation(st1[:], heads(bank[7]), ACT.Copy).then_inc(rec_act, 1)
                act.wait_ge(rec_pe, l * 6 + 3)
                a.activation(ot[:, :, 0:P], heads(bank[0]), ACT.Copy).then_inc(rec_act, 1)
                a.activation(sq[:, 0:4, 0:P], heads(bank[0]), ACT.Square).then_inc(rec_act, 1)
                attend(LEVELS + 1)
                attend(LEVELS + 2)
                act.wait_ge(rec_pe, l * 6 + 5)
                a.activation(vnew[:, 1], heads(bank[7]), ACT.Copy).then_inc(rec_act, 1)
                attend(LEVELS + 3)
                act.wait_ge(rec_pe, l * 6 + 6)
                a.activation(ot[:, :, P:S], heads(bank[6]), ACT.Copy).then_inc(rec_act, 1)
                a.activation(sq[:, 0:4, P:S], heads(bank[6]), ACT.Square).then_inc(rec_act, 1)
                for g in range(2):
                    act.wait_ge(on_sum, l * 2 + g + 1)
                    a.activation(rin[:, 2 * g:2 * g + 2, :], bank[g][:, :].rearrange("p (i s) -> p i s", i=2),
                                 ACT.Sqrt, bias=eps, scale=1.0 / P).then_inc(on_std, 1)
                for k in range(DNH):
                    act.wait_ge(mix_ready, l * 4 + k + 1)
                    a.activation(act_hi[:, k, :], mix[:, k, :], ACT.Copy).then_inc(mix_hi, 1)

                for m in range(KD):
                    refill(T_WOUT + m)
                    if m >= 1:
                        post_square(l * 4 + 1, m - 1, l * 16)
                post_square(l * 4 + 1, KD - 1, l * 16)
                norm_root(l * 4 + 1)
                pre_norm(l * 4 + 2, x_ready, l * 16 + 8, l * 16 + 8)
                act.wait_ge(packf_in, l * 16 + 16)

                def step(r, k, p, q, up=True, down=True):
                    if up:
                        act.wait_ge(gelu_done, l * NP_FF + p + 1)
                        act.wait_ge(hid_done, l * NP_FF + p + 1)
                        for w, dst in enumerate((glu_g, glu_v)):
                            act.wait_ge(tile_done, r * SLOTS + (k + w + 1))
                            a.activation(dst[:, q, :], bank[2 * q + w][:, 0:S], ACT.Identity,
                                         scale=pf_("conv", p * 6 + w * 3 + 2), bias=pf_("bias", p * 2 + w)).then_inc(glu_first, 1)
                            refill_hi(r, k + w)
                        act.wait_ge(glu_ready, l * NP_FF + p + 1)
                        a.activation(glu_a[:, q, :], glu_g[:, q, :], ACT.Gelu_apprx_tanh).then_inc(gelu_done, 1)
                        k = k + 2
                    if down:
                        refill_hi(r, k)

                r0 = l * (LAYER_TILES // SLOTS) + T_UP // SLOTS
                for p in range(DOWN_LAG):
                    step(r0, 2 * p, p, p % PAIRS, down=False)
                for p in range(DOWN_LAG, PEEL):
                    step(r0 + (p - 1), 1, p, p % PAIRS)
                with act.Fori(0, GLU_LOOPS) as i:
                    for q in range(PAIRS):
                        step(r0 + i * PAIRS + (q + PEEL - 1), 1, i * PAIRS + (q + PEEL), q)
                for p in range(NP_FF, NP_FF + DOWN_LAG):
                    step(r0 + (NP_FF - 1), 1 + p - NP_FF, p, p % PAIRS, up=False)
                for m in range(KD):
                    post_square(l * 4 + 3, m, l * 16 + 8)
                norm_root(l * 4 + 3)

            with act.Fori(0, DEPTH) as l:
                layer(l)
            second_scalar(act, pre_norm, softplus, refill_hi)

        @block.vector
        def _(dve):
            def make_lo(n, s):
                dve.wait_ge(hi_ready, n + 1)
                v.tensor_tensor(w_lo[:, s, :], ring[:, s, :], w_hi[:, s, :].bitcast(F32), ALU.subtract).then_inc(lo_ready, 1)

            def refill_lo(r, k):
                make_lo(r * SLOTS + k + SLOTS, k % SLOTS)

            def part_lo(k, src, hi, made, done):
                dve.wait_ge(hi, made)
                v.tensor_tensor(act_lo[:, k, :], src[:, k, :], act_hi[:, k, :].bitcast(F32), ALU.subtract).then_inc(done, 1)

            def norm_apply(ch, i, gain, at):
                dve.wait_ge(norm_std, i + 1)
                ch.mark(v.reciprocal(rstd[:], std[:]))
                ch.dep()
                for k in range(KD + 2):
                    if k < KD:
                        v.scalar_tensor_tensor(h[:, k, :], x[:, k, :], gain(k), rstd[:], ALU.mult,
                                               ALU.mult).then_inc(h_ready, 1)
                    if k >= 2:
                        part_lo(k - 2, h, h_hi, at + k - 1, h_lo)

            def norm_add(ch, i, gain):
                dve.wait_ge(norm_std, i + 1)
                ch.mark(v.reciprocal(rstd[:], std[:]))
                ch.dep()
                for k in range(KD):
                    ch.mark(v.scalar_tensor_tensor(y[:, k, :], y[:, k, :], gain(k), rstd[:], ALU.mult, ALU.mult))
                    if k >= 1:
                        ch.dep_before(1)
                        v.tensor_tensor(x[:, k - 1, :], x[:, k - 1, :], y[:, k - 1, :], ALU.add).then_inc(x_ready, 1)
                ch.dep()
                v.tensor_tensor(x[:, KD - 1, :], x[:, KD - 1, :], y[:, KD - 1, :], ALU.add).then_inc(x_ready, 1)

            def softplus(step, ch, l, sp, lo, hi):
                z, ab, e, u, ln, r = (sp[lo:hi, j, :] for j in range(6))
                if step == 0:
                    dve.wait_ge(sp_act, l * 3 + 1)
                    v.scalar_tensor_tensor(ab, z, -1.0, z, ALU.mult, ALU.max).then_inc(sp_dve, 1)
                elif step == 1:
                    dve.wait_ge(sp_act, l * 3 + 2)
                    v.tensor_scalar(u, e, 1.0, None, ALU.add).then_inc(sp_dve, 1)
                else:
                    dve.wait_ge(sp_dve, l * 2 + 2)
                    ch.mark(v.scalar_tensor_tensor(ab, u, -1.0, e, ALU.add, ALU.subtract))
                    ch.mark(v.reciprocal(r, u))
                    ch.dep()
                    ch.mark(v.tensor_tensor(ab, ab, r, ALU.mult))
                    ch.dep()
                    dve.wait_ge(sp_act, l * 3 + 3)
                    ch.mark(v.scalar_tensor_tensor(r, z, 0.0, ln, ALU.max, ALU.add))
                    ch.dep()
                    ch.mark(v.tensor_tensor(r, r, ab, ALU.subtract))
                    ch.dep()
                return r

            dve.wait_ge(x_in, 16)
            dve.wait_ge(consts_in, 16)
            for k in range(KD):
                v.memset(credit[:, 9 + k:10 + k], 0.0).then_inc(x_ready, 1)
            for n in range(SLOTS):
                make_lo(n, n)

            def layer(l):
                ch = Chain(dve, dve_chain, l * DVE_LINKS)

                def refill(n):
                    refill_lo(l * (LAYER_TILES // SLOTS), n)

                dve.wait_ge(packa_in, l * 16 + 16)
                norm_apply(ch, l * 4, lambda k: pa_("pre", k), l * 16)

                for n in range(T_Z):
                    src, dst = bank[n % 4], qkvc[:, n, :]
                    dve.wait_ge(conv_first, l * 12 + n + 1)
                    for j in range(1, CONV):
                        if j > 1:
                            ch.dep()
                        ins = v.scalar_tensor_tensor(dst[:, j:], src[:, 0:S - j], pa_("conv", n * CONV + CONV - 1 - j),
                                                     dst[:, j:], ALU.mult, ALU.add)
                        if j < CONV - 1:
                            ch.mark(ins)
                    ins.then_inc(conv_ready, 1)
                    refill(n)

                def decays():
                    r = softplus(2, ch, l, spt, 32, 36)
                    dve.wait_ge(decay_ready, l + 1)
                    ch.mark(v.tensor_scalar(r, r, cols[32:36, 1, 0:1], -1.0, ALU.mult, ALU.mult))
                    ch.dep()
                    dve.wait_ge(beta_ready, l + 1)
                    dve.wait_ge(rows_zero, 1)
                    for c in range(NT):
                        ins = v.tensor_tensor_scan(rows[32:36, c * P:(c + 1) * P], cc("ones", rows_=slice(32, 36)),
                                                   r[:, c * P:(c + 1) * P], 0.0, ALU.mult, ALU.add)
                    ins.then_inc(rows_ready, 1)

                for n in range(T_Z, T_WOUT):
                    if n < T_Z + 2:
                        softplus(n - T_Z, ch, l, spt, 32, 36)
                    if n == T_Z + 2:
                        decays()
                    i = n - T_BQ - 1
                    if 0 <= i < 8:
                        dve.wait_ge(l2_std, l * 8 + i + 1)
                        ch.mark(v.reciprocal(rin8[:, i, :], rin8[:, i, :]))
                        ch.dep()
                        v.scalar_tensor_tensor(qkn[:, i, :], qkvs[:, i, :], float(P) ** -0.5 if i < 4 else 1.0,
                                               rin8[:, i, :], ALU.mult, ALU.mult).then_inc(qk_ready, 1)
                    j = n - T_BQ - 3
                    if 0 <= j < 8:
                        dve.wait_ge(rope_rot, l * 8 + j + 1)
                        v.tensor_tensor(ropet[:, j, :], bank[4 + j % 2][:, 0:S], cc("sin"),
                                        ALU.mult).then_inc(rope_used, 1)
                        ch.mark(v.tensor_tensor(raw[:, j, :], raw[:, j, :], cc("cos"), ALU.mult))
                        ch.dep()
                        dve.wait_ge(rope_used, l * 8 + j + 1)
                        v.tensor_tensor(raw[:, j, :], raw[:, j, :], ropet[:, j, :], ALU.add).then_inc(rope_done, 1)
                    refill(n)

                dve.wait_ge(cols_done, l + 1)
                v.tensor_copy(cols[:], bank[4][:, S:S + 128].rearrange("p (c k) -> p c k", c=NT)).then_inc(cols_ready, 1)
                dve.wait_ge(cols_ready, l + 1)
                for i in range(DNH):
                    dve.wait_ge(bc_act, l * 4 + i + 1)
                    for c in range(NT):
                        ins = v.scalar_tensor_tensor(gam[:, i, c * P:(c + 1) * P], bank[i % 2][:, c * P:(c + 1) * P],
                                                     cols[:, c, 32 + i:33 + i], cc("decmask"), ALU.subtract, ALU.add)
                    ins.then_inc(bc_dve, 1)
                    dve.wait_ge(tr_done, l * 4 + i + 1)
                    for c in range(NT):
                        ins = v.tensor_scalar(vb[:, 2 * i + c, :], bank[6 + i % 2][:, c * P:(c + 1) * P],
                                              cols[:, c, i:i + 1], None, ALU.mult)
                    ins.then_inc(tr_dve, 1)
                    dve.wait_ge(gram_done, l * 4 + i + 1)
                    dve.wait_ge(gam_ready, l * 4 + i + 1)
                    dve.wait_ge(gb_ready, l * 4 + i + 1)
                    pair = bank[2 + i % 2][:, :].rearrange("p (c w k) -> p c w k", c=NT, w=2)
                    v.tensor_tensor(qkt[:, 2 * i:2 * i + 2, :], pair[:, :, 1, :],
                                    gam[:, i, :].rearrange("p (c k) -> p c k", c=NT), ALU.mult)
                    v.tensor_tensor(bp[:, 2 * i:2 * i + 2, :], pair[:, :, 0, :],
                                    bbc[:, i, :].rearrange("p (c k) -> p c k", c=NT), ALU.mult).then_inc(gram_used, 1)

                def attend(i):
                    if i < SWAH:
                        dve.wait_ge(att_s, l * 8 + i + 1)
                        ch.mark(v.scalar_tensor_tensor(prob[:, i, :], bank[2 + i % 2][:, 0:3 * P], SWAD ** -0.5,
                                                       cc("dilmask"), ALU.mult, ALU.add))
                        ch.dep()
                        ch.mark(v.tensor_reduce(att_max[:, 2 * i:2 * i + 1], prob[:, i, 0:P], AX_X, ALU.max, negate=True))
                        v.tensor_reduce(att_max[:, 2 * i + 1:2 * i + 2], prob[:, i, P:3 * P], AX_X, ALU.max,
                                        negate=True).then_inc(att_sm, 1)
                    j = i - 1
                    if 0 <= j < SWAH:
                        dve.wait_ge(att_p, l * 8 + j + 1)
                        ch.mark(v.reciprocal(att_rz[:, 2 * j:2 * j + 2], att_z[:, 2 * j:2 * j + 2]))
                        ch.dep()
                        v.tensor_scalar(prob[:, j, 0:P], prob[:, j, 0:P], att_rz[:, 2 * j:2 * j + 1], None, ALU.mult)
                        v.tensor_scalar(prob[:, j, P:3 * P], prob[:, j, P:3 * P], att_rz[:, 2 * j + 1:2 * j + 2], None,
                                        ALU.mult).then_inc(att_pn, 1)

                for lev in range(LEVELS):
                    if lev >= 1:
                        attend(lev - 1)
                    for g in range(2):
                        us = slice(4 * g, 4 * g + 4)
                        t_ps = bank[g][:, :].rearrange("p (u k) -> p u k", u=4)
                        u_ps = bank[6 + g][:, :].rearrange("p (u k) -> p u k", u=4)
                        if lev == 0:
                            eye = ident.unsqueeze(1).to_broadcast([P, 4, P])
                            dve.wait_ge(bl_ready, l * LEVELS + 1)
                            v.tensor_tensor(uinv[:, us, :], eye, bl[:, 0, us, :], ALU.subtract)
                            dve.wait_ge(lev_x, l * 2 * LEVELS + g + 1)
                            v.tensor_tensor(tinv[:, us, :], eye, t_ps, ALU.subtract).then_inc(tu_ready, 1)
                        else:
                            dve.wait_ge(lev_y, l * 2 * (LEVELS - 1) + 2 * (lev - 1) + g + 1)
                            dve.wait_ge(tu_ready, l * 2 * LEVELS + 2 * (lev - 1) + g + 1)
                            if lev < LEVELS - 1:
                                v.tensor_tensor(tinv[:, us, :], tinv[:, us, :], t_ps, ALU.subtract)
                            v.tensor_tensor(uinv[:, us, :], uinv[:, us, :], u_ps, ALU.subtract).then_inc(tu_ready, 1)
                for i in range(LEVELS - 1, SWAH + 1):
                    attend(i)

                dve.wait_ge(rec_pe, l * 6 + 4)
                v.tensor_tensor(resid[:], vb[:].rearrange("p (i c) k -> p i c k", c=NT)[:, :, 1, :],
                                bank[6][:, :].rearrange("p (i k) -> p i k", i=DNH), ALU.subtract).then_inc(rec_dve, 1)
                for p in range(SWAH // 2):
                    part_lo(4 + p, mix, att_o, l * 8 + 2 * p + 2, mix_lo)

                def out_norm(g):
                    dve.wait_ge(on_std, l * 2 + g + 1)
                    hs = slice(2 * g, 2 * g + 2)
                    ch.mark(v.reciprocal(rin[:, hs, :], rin[:, hs, :]))
                    ch.dep()
                    ch.mark(v.scalar_tensor_tensor(ot[:, hs, :], ot[:, hs, :], pa_("onorm"), rin[:, hs, :],
                                                   ALU.mult, ALU.mult))
                    ch.dep()
                    for k in range(2 * g, 2 * g + 2):
                        v.tensor_tensor(mix[:, k, :], ot[:, k, :], zs[:, k, :], ALU.mult).then_inc(mix_ready, 1)

                out_norm(0)
                out_norm(1)
                for k in range(DNH):
                    part_lo(k, mix, mix_hi, l * 4 + k + 1, mix_lo)

                for m in range(KD):
                    dve.wait_ge(tile_done, l * LAYER_TILES + T_WOUT + m + 1)
                    v.tensor_copy(y[:, m, :], bank[4 + m % 4][:, 0:S]).then_inc(y_done, 1)
                    refill(T_WOUT + m)
                dve.wait_ge(y_done, l * 16 + 8)
                norm_add(ch, l * 4 + 1, lambda k: pa_("post", k))
                dve.wait_ge(packf_in, l * 16 + 16)
                norm_apply(ch, l * 4 + 2, lambda k: pf_("pre", k), l * 16 + 8)

                def step(r, k, p, q, up=True, down=True):
                    if up:
                        for w, (dst, done) in enumerate(((glu_g, glu_ready), (glu_v, ffn_free))):
                            src = bank[2 * q + w]
                            dve.wait_ge(glu_first, (l * NP_FF + p) * 2 + w + 1)
                            for j in range(1, FCONV):
                                if j > 1:
                                    dve.wait_ge(ffn_chain, (l * NP_FF + p) * FFN_LINKS + w + 1)
                                ins = v.scalar_tensor_tensor(dst[:, q, j:], src[:, 0:S - j], pf_("conv", p * 6 + w * 3 + 2 - j),
                                                             dst[:, q, j:], ALU.mult, ALU.add)
                                ins.then_inc(ffn_chain if j < FCONV - 1 else done, 1)
                            refill_lo(r, k + w)
                        k = k + 2
                    if down:
                        refill_lo(r, k)
                    if up:
                        dve.wait_ge(gelu_done, l * NP_FF + p + 1 + CREDITS)
                        dve.wait_ge(ffn_free, l * NP_FF + p + 1 + CREDITS)
                        v.tensor_tensor(hid_hi[:, q, :], glu_a[:, q, :], glu_v[:, q, :], ALU.mult).then_inc(hi_done, 1)

                r0 = l * (LAYER_TILES // SLOTS) + T_UP // SLOTS
                for p in range(DOWN_LAG):
                    step(r0, 2 * p, p, p % PAIRS, down=False)
                for p in range(DOWN_LAG, PEEL):
                    step(r0 + (p - 1), 1, p, p % PAIRS)
                with dve.Fori(0, GLU_LOOPS) as i:
                    for q in range(PAIRS):
                        step(r0 + i * PAIRS + (q + PEEL - 1), 1, i * PAIRS + (q + PEEL), q)
                for p in range(NP_FF, NP_FF + DOWN_LAG):
                    step(r0 + (NP_FF - 1), 1 + p - NP_FF, p, p % PAIRS, up=False)
                dve.wait_ge(tile_done, (l + 1) * LAYER_TILES)
                for m in range(KD):
                    v.tensor_copy(y[:, m, :], bank[4 + m // 2][:, m % 2 * S:m % 2 * S + S]).then_inc(y_done, 1)
                dve.wait_ge(y_done, l * 16 + 16)
                norm_add(ch, l * 4 + 3, lambda k: pf_("post", k))
                assert ch.n == DVE_LINKS, ("DVE_LINKS", ch.n)

            with dve.Fori(0, DEPTH) as l:
                layer(l)
            second_vector(dve, norm_apply, softplus, refill_lo, part_lo)

        @block.gpsimd
        def _(pool):
            pool.dma_start(pa[:], packa[0]).then_inc(packa_in, 16)
            pool.dma_start(pf[:], packf[0]).then_inc(packf_in, 16)
            pl.memset(rows[:], 0.0).then_inc(rows_zero, 1)
            pool.wait_ge(rows_zero, 1)
            for q in range(PAIRS):
                pl.memset(credit[:, 3 * q:3 * q + 1], 0.0).then_inc(hid_done, 1)
                pl.memset(credit[:, 3 * q + 1:3 * q + 2], 0.0).then_inc(ffn_free, 1)
                pl.memset(credit[:, 3 * q + 2:3 * q + 3], 0.0).then_inc(gelu_done, 1)

            def layer(l):
                ch = Chain(pool, pool_chain, l * POOL_LINKS)
                for i in range(DNH):
                    pool.wait_ge(bc_act, l * 4 + i + 1)
                    pool.wait_ge(qk_ready, l * 8 + 8)
                    pl.tensor_tensor(qg[:, i, :], qkn[:, i, P:S], eg1[:, i, :], ALU.mult)
                    ch.mark(pl.tensor_tensor(kbg[:, i, :], qkn[:, 4 + i, P:S], eg1[:, i, :], ALU.mult))
                    ch.dep()
                    pl.tensor_tensor(kbg[:, i, :], kbg[:, i, :], bbc[:, i, P:S], ALU.mult).then_inc(kbg_ready, 1)
                    pool.wait_ge(gam_ready, l * 4 + i + 1)
                    pool.wait_ge(kbg_ready, l * 4 + i + 1)
                    pl.tensor_tensor(bbc[:, i, :], bbc[:, i, :], gam[:, i, :], ALU.mult).then_inc(gb_ready, 1)
                pool.wait_ge(gram_used, l * 4 + 4)
                for lev in range(LEVELS):
                    if lev >= 2:
                        pool.wait_ge(lev_x, l * 2 * LEVELS + 2 * (lev - 1))
                        pool.wait_ge(tu_ready, l * 2 * LEVELS + 2 * (lev - 1))
                    pl.tensor_tensor(bl[:, lev % 2], bp[:], cc("level", lev, P).unsqueeze(1).to_broadcast([P, 8, P]),
                                     ALU.mult).then_inc(bl_ready, 1)

                def product(p, q):
                    pool.wait_ge(gelu_done, l * NP_FF + p + 1 + CREDITS)
                    pool.wait_ge(ffn_free, l * NP_FF + p + 1 + CREDITS)
                    pool.wait_ge(hid_done, l * NP_FF + p + 1)
                    pl.tensor_tensor(glu_p[:, q, :], glu_a[:, q, :], glu_v[:, q, :], ALU.mult).then_inc(prod_done, 1)
                    pool.wait_ge(prod_done, l * NP_FF + p + 1)
                    pool.wait_ge(hi_done, l * NP_FF + p + 1)
                    pl.tensor_tensor(hid_lo[:, q, :], glu_p[:, q, :], hid_hi[:, q, :].bitcast(F32),
                                     ALU.subtract).then_inc(hid_done, 1)

                pool.wait_ge(x_ready, l * 16 + 16)
                pool.dma_start(pa[:], packa[bass.ds(l + 1, 1)].rearrange("o p n -> (o p) n")).then_inc(packa_in, 16)
                with pool.Fori(0, NP_FF // PAIRS) as i:
                    for q in range(PAIRS):
                        product(i * PAIRS + q, q)
                pool.wait_ge(x_ready, l * 16 + 24)
                pool.dma_start(pf[:], packf[bass.ds(l + 1, 1)].rearrange("o p n -> (o p) n")).then_inc(packf_in, 16)
                assert ch.n == POOL_LINKS, ("POOL_LINKS", ch.n)

            with pool.Fori(0, DEPTH) as l:
                layer(l)
            second_pool(pool)


def shape_constants():
    c = np.zeros((P, C_W), np.float32)

    def put(name, value):
        lo, hi = C_COLS[name]
        value = np.asarray(value, np.float32)
        c[:value.shape[0], lo:hi] = value

    i = np.arange(P)
    put("ident", np.eye(P))
    put("ones", np.ones((P, P)))
    put("ones256", np.ones((P, S)))
    put("bd64", i[:, None] // 64 == i[None, :] // 64)
    half, d = ROPE_DIM // 2, i % SWAD
    rot = np.zeros((P, P))
    for o in range(P):
        if d[o] < half:
            rot[o + half, o] = -1.0
        elif d[o] < ROPE_DIM:
            rot[o - half, o] = 1.0
    put("rot", rot)
    freq = np.float32(ROPE_THETA) ** (-np.arange(0, ROPE_DIM, 2, dtype=np.float32) / np.float32(ROPE_DIM))
    angle = np.arange(S, dtype=np.float32)[None, :] * freq[:, None]
    cos, sin = np.ones((P, S), np.float32), np.zeros((P, S), np.float32)
    for o in range(P):
        if d[o] < ROPE_DIM:
            cos[o], sin[o] = np.cos(angle[d[o] % half]), np.sin(angle[d[o] % half])
    put("cos", cos)
    put("sin", sin)
    put("decmask", np.where(i[None, :] >= i[:, None], 0.0, NEG))
    levels = []
    for lev in range(LEVELS):
        b = 2 ** lev
        same = i[:, None] // (2 * b) == i[None, :] // (2 * b)
        levels.append(same & (i[:, None] % (2 * b) < b) & (i[None, :] % (2 * b) >= b))
    put("level", np.concatenate(levels, axis=1))
    times = np.zeros((S, S))
    dist = np.arange(S)[:, None] - np.arange(S)[None, :]
    for window, dil in DIL:
        times += (dist >= 0) & (dist <= window) & (dist % dil == 0)
    logs = np.where(times > 0, np.log(np.maximum(times, 1)), NEG)
    put("dilmask", np.concatenate([logs[0:P, 0:P], logs[P:S, :]], axis=1))
    causal = np.where(dist >= 0, 0.0, NEG)
    put("causal", np.concatenate([causal[0:P, 0:P], causal[P:S, :]], axis=1))
    put("eps", np.full((P, 1), EPS))
    put("gmask", np.arange(GB)[None, :] >= i[:, None] % GB)
    put("selhead", i[:, None] // GDK == np.arange(GH)[None, :])
    put("first4", np.tile([4.0, 3.0, 2.0, 1.0], (P, 1)))
    return c


def kernel(**inputs):
    import concourse.bacc as bacc
    from concourse.bass_utils import run_bass_kernel_spmd

    w = {k: np.asarray(a) for k, a in inputs.items()}

    def tiles(m):
        k, n = m.shape
        return m.reshape(k // P, P, n // P, P).transpose(2, 1, 0, 3).reshape(n // P, P, k)

    def blocks(m, order):
        b = np.stack([m[r * P:(r + 1) * P, c * P:(c + 1) * P] for r, c in order])
        return b.reshape(-1, 8, P, P).transpose(0, 2, 1, 3).reshape(-1, P, 8 * P)

    def cols(v):
        return v.reshape(-1, P).T

    parts = []
    packa = np.zeros((DEPTH + 1, P, A_W), np.float32)
    packf = np.zeros((DEPTH + 1, P, F_W), np.float32)
    packb = np.zeros((P, B_W), np.float32)

    def put(pack, table, name, value):
        lo, hi = table[name]
        value = value.reshape(value.shape[0], -1)
        assert value.shape[1] == hi - lo, name
        pack[:value.shape[0], lo:hi] = value

    for l in range(DEPTH):
        wi = w["w_in"][l]
        small = 4 * DNH * P
        parts.append(tiles(wi[:, :small]))
        parts.append(tiles(wi[:, small + 2 * DNH:]))
        parts.append(tiles(w["w_out"][l]))
        up = tiles(w["ffn_up"][l])
        down = blocks(w["ffn_down"][l], [(k, m) for k in range(NP_FF) for m in range(KD)])
        for p in range(NP_FF + DOWN_LAG):
            if p < NP_FF:
                parts.append(up[[p, NP_FF + p]])
            if p >= DOWN_LAG:
                parts.append(down[p - DOWN_LAG:p - DOWN_LAG + 1])
        put(packa[l], A_COLS, "pre", cols(w["pre_mix_norm"][l]))
        put(packa[l], A_COLS, "post", cols(w["post_mix_norm"][l]))
        put(packa[l], A_COLS, "conv", w["dn_conv"][l].reshape(CONV, 12, P).transpose(2, 1, 0))
        put(packa[l], A_COLS, "onorm", w["dn_out_norm"][l].reshape(P, 1))
        lo = A_COLS["alog"][0]
        packa[l, 32:32 + DNH, lo] = w["dn_a_log"][l]
        lo = A_COLS["dt"][0]
        packa[l, 32:32 + DNH, lo] = w["dn_dt_bias"][l]
        ba = np.zeros((P, KD, 64), np.float32)
        ba[:, :, 0:DNH] = wi[:, small:small + DNH].reshape(KD, P, DNH).transpose(1, 0, 2)
        ba[:, :, 32:32 + DNH] = wi[:, small + DNH:small + 2 * DNH].reshape(KD, P, DNH).transpose(1, 0, 2)
        put(packa[l], A_COLS, "wba", ba)
        put(packf[l], F_COLS, "pre", cols(w["pre_ffn_norm"][l]))
        put(packf[l], F_COLS, "post", cols(w["post_ffn_norm"][l]))
        put(packf[l], F_COLS, "conv", w["ffn_conv"][l].reshape(FCONV, 2, NP_FF, P).transpose(3, 2, 1, 0))
        put(packf[l], F_COLS, "bias", w["ffn_conv_bias"][l].reshape(2, NP_FF, P).transpose(2, 1, 0))

    w2 = w["w_in_2"][0]
    edges = np.cumsum([GH * GDK, GH * GDK, GH * GDV, GRANK, GH * GDV, 512, 512, 512, 512])
    gq, gk, gv, glr, gog, cu, dq, dk, dv = np.split(w2, edges[:-1], axis=1)
    ct = tiles(cu)
    parts += [tiles(gq), tiles(gk), ct[[0, 2, 1, 3]], tiles(gog), tiles(gv), tiles(dq), tiles(dk), tiles(dv),
              tiles(w["w_out_2"][0])]
    ups, downs = [], []
    for e in range(NE):
        ups.append(np.concatenate([tiles(w["expert_w_gate_2"][0, e]), tiles(w["expert_w_up_2"][0, e])]))
        downs.append(blocks(w["expert_w_down_2"][0, e], [(k, m) for m in range(KD) for k in range(2)]))
    parts.append(ups[0])
    for e in range(NE - 1):
        parts += [ups[e + 1], downs[e]]
    parts.append(downs[-1])
    wtiles = np.concatenate(parts)
    assert wtiles.shape == (ALL_TILES, P, KD * P)

    put(packb, B_COLS, "mix", cols(w["mix_norm_g_2"][0]))
    put(packb, B_COLS, "ffn", cols(w["ffn_norm_g_2"][0]))
    put(packb, B_COLS, "wglr", glr.reshape(KD, P, GRANK).transpose(1, 0, 2))
    router = np.concatenate([w["router_group_w_2"][0], w["router_expert_w_2"][0]], axis=1)
    put(packb, B_COLS, "wrt", router.reshape(KD, P, NR).transpose(1, 0, 2))
    put(packb, B_COLS, "rbias", np.concatenate([w["router_group_b_2"][0], w["router_expert_b_2"][0]]).reshape(1, NR))
    put(packb, B_COLS, "glab", w["gla_gate_b_2"][0].reshape(P, 1))
    put(packb, B_COLS, "gatew", w["gla_gate_w_2"][0])
    put(packb, B_COLS, "convw", w["conv_w_2"][0].reshape(CW, 2, P).transpose(2, 1, 0))
    for name, key in (("convb", "conv_b_2"), ("cng", "conv_norm_g_2"), ("cnb", "conv_norm_b_2")):
        put(packb, B_COLS, name, cols(w[key][0]))
    for name, key in (("glan", "gla_norm_g_2"), ("qn", "diff_qnorm_g_2"), ("kn", "diff_knorm_g_2")):
        put(packb, B_COLS, name, np.tile(w[key][0], 2).reshape(P, 1))
    put(packb, B_COLS, "subln", w["diff_subln_g_2"][0].reshape(P, 1))
    put(packb, B_COLS, "lam", np.stack([w[f"diff_{n}_2"][0] for n in ("lq1", "lk1", "lq2", "lk2")], axis=1))

    arrays = {
        "xt": np.ascontiguousarray(w["x"][0].T.reshape(KD, P, S).transpose(1, 0, 2)),
        "wtiles": wtiles, "consts": shape_constants(), "packa": packa, "packf": packf, "packb": packb,
    }
    nc = bacc.Bacc("TRN2", target_bir_lowering=False, num_devices=1)
    args = [nc.dram_tensor(name, arr.shape, F32, kind="ExternalInput").ap() for name, arr in arrays.items()]
    out = nc.dram_tensor("out", (P, KD, S), F32, kind="ExternalOutput").ap()
    block_program(nc, *args, out)
    got = run_bass_kernel_spmd(nc, [arrays], core_ids=[0]).results[0]["out"]
    return got.transpose(1, 0, 2).reshape(1, D, S).transpose(0, 2, 1)
```

```python
from contextlib import ExitStack

import concourse.bass as bass
import numpy as np
from concourse import mybir

ALU = mybir.AluOpType
ACT = mybir.ActivationFunctionType
AX_X = mybir.AxisListType.X
F32 = mybir.dt.float32
F32R = mybir.dt.float32r

P = 128
S = 256
NT = S // P
D = 1024
KD = D // P
DEPTH = 2
EPS = 1e-6
NEG = -1e30

DNH, CONV = 4, 4
FF = 2816
NP_FF = FF // P
FCONV = 3
SWAH, SWAD = 8, 64
DIL = ((128, 1), (512, 4), (2048, 16))
ROPE_THETA, ROPE_DIM = 500000.0, 16
LEVELS = 7

GH, GDK, GDV, GRANK, GTAU = 4, 32, 64, 16, 16.0
GB = 16
NGB = S // GB
CW = 31
DFH = 4
LAMBDA_INIT = 0.2
NG, NPG = 4, 4
NE = NG * NPG
NR = NG + NE

RING = 6
SLOTS = 3
T_Z, T_BQ, T_BV, T_WOUT, T_UP = 12, 16, 24, 28, 36
DOWN_LAG = 2
LAYER_TILES = T_UP + 3 * NP_FF
T2 = DEPTH * LAYER_TILES
U_CONV, U_GOG, U_GV, U_DQ, U_DV, U_WOUT, U_EXP = 2, 6, 8, 10, 18, 22, 30
ALL_TILES = T2 + U_EXP + NE * RING
assert RING % SLOTS == 0 and LAYER_TILES % RING == 0 and (T2 + U_EXP) % RING == 0 and T_UP % RING == 0
PAIRS = 2
PEEL = 2 * DOWN_LAG
GLU_LOOPS = (NP_FF - PEEL) // PAIRS
assert (NP_FF - PEEL) % PAIRS == 0 and SLOTS == 3
CREDITS = PAIRS
MIX_ORDER = (4, 5, 6, 7, 0, 1, 2, 3)
EX_CREDITS = 2
NORM2 = DEPTH * 4
U_PAIRS, U_BETWEEN, U_SCORES, U_WITHIN = 13, 12, 16, 20
POOL_TAPS = (4, 10, 24)
SPREAD_STEPS = (16, 17, 20)
L2_STEPS = (T_BQ + 4, T_BQ + 6)
CONV_VALUES = (U_CONV, U_CONV + 2)


def in_features(u):
    return u < U_GV or U_DQ <= u < U_DV


def evacuated(u):
    return sum(i not in CONV_VALUES for i in range(u + 1))


def columns(*widths):
    at, out = 0, {}
    for name, w in widths:
        out[name] = (at, at + w)
        at += w
    return out, at


C_COLS, C_W = columns(
    ("ident", P), ("ones256", S), ("eps", 1), ("bd64", P), ("rot", P), ("cos", S), ("sin", S), ("decmask", P),
    ("level", LEVELS * P), ("dilmask", 3 * P), ("causal", 3 * P), ("gmask", P),
    ("selhead", GH), ("first4", 4))
C_FIRST = C_COLS["eps"][1]
A_COLS, A_W = columns(
    ("pre", KD), ("conv", 12 * CONV), ("onorm", 1), ("alog", 1), ("dt", 1), ("post", KD), ("wba", KD * 64))
F_COLS, F_W = columns(("pre", KD), ("conv", NP_FF * 2 * FCONV), ("bias", NP_FF * 2), ("post", KD))
B_COLS, B_W = columns(
    ("mix", KD), ("ffn", KD), ("wglr", KD * GRANK), ("wrt", KD * NR), ("glab", 1), ("glan", 1),
    ("convw", 2 * CW), ("convb", 2), ("cng", 2), ("cnb", 2), ("qn", 1), ("kn", 1), ("lam", 4),
    ("subln", 1), ("gatew", P), ("rbias", NR))

DVE_LINKS, POOL_LINKS = 66, 4
FFN_LINKS = 2


class Chain:

    def __init__(self, engine, sem, start):
        self.engine, self.sem, self.start, self.n = engine, sem, start, 0

    def mark(self, ins):
        self.n += 1
        ins.then_inc(self.sem, 1)

    def dep(self):
        self.engine.wait_ge(self.sem, self.start + self.n)

    def dep_before(self, back):
        self.engine.wait_ge(self.sem, self.start + self.n - back)


class Arena:

    def __init__(self, region, width):
        self.region, self.width, self.at = region, width, 0

    def take(self, *shape):
        n = int(np.prod(shape))
        assert self.at + n <= self.width, (self.at, n, self.width)
        v = self.region[:, self.at:self.at + n]
        self.at += n
        names = " ".join("abcd"[:len(shape)])
        sizes = {k: s for k, s in zip("abcd", shape)}
        return v if len(shape) == 1 else v.rearrange(f"p ({names}) -> p {names}", **sizes)


def block_program(nc, xt, wtiles, consts, packa, packf, packb, out):
    v, a, pl, t = nc.vector, nc.scalar, nc.gpsimd, nc.tensor
    ctx = ExitStack()
    with ctx:
        def sb(name, *shape):
            return ctx.enter_context(nc.sbuf_tensor(name, [P, *shape], F32))

        def sem(name):
            return ctx.enter_context(nc.semaphore(name))

        x = sb("x", KD, S)
        h = sb("h", KD, S)
        sq = sb("sq", KD, S)
        y = sb("y", KD, S)
        ring = sb("ring", SLOTS, 1024)

        def split(name, *shape):
            return [ctx.enter_context(nc.sbuf_tensor(f"{name}_{part}", [P, *shape], F32R)) for part in ("hi", "lo")]

        w_hi, w_lo = split("w", SLOTS, 1024)
        act_hi, act_lo = split("act", KD, S)
        cst = sb("cst", C_W)
        pa = sb("pa", A_W)
        pf = sb("pf", F_W)
        pb = sb("pb", B_W)
        rms = sb("rms", NT)
        rrms = sb("rrms", NT)
        mix = sb("mix", KD, S)
        ARENA = 23060
        credit = sb("credit", 24)
        region = sb("region", ARENA)
        hid_hi, hid_lo = split("hid", 2, S)

        ar = Arena(region, ARENA)
        qkvc = ar.take(12, S)
        qkvs = ar.take(12, S)
        sqk, ropet, raw = sq, y, h
        zs = ar.take(DNH, S)
        vtok = ar.take(NT, 512)
        rows = ar.take(S)
        cols = ar.take(NT, 64)
        l2_rms, l2_rrms = ar.take(2 * DNH * NT), ar.take(2 * DNH * NT)
        on_rms, on_rrms = ar.take(DNH * NT), ar.take(DNH * NT)
        gam = ar.take(DNH, S)
        bbc = ar.take(DNH, S)
        spt = region[:, ar.at - 8 * S:ar.at - 2 * S].rearrange("p (j s) -> p j s", j=6)
        eg1 = ar.take(DNH, P)
        kbg = ar.take(DNH, P)
        qg = ar.take(DNH, P)
        bp = ar.take(DNH * NT, P)
        qkt = ar.take(DNH * NT, P)
        vb = ar.take(DNH * NT, P)
        kd = ar.take(DNH, P)
        uinv = ar.take(DNH * NT, P)
        vnew = ar.take(2, DNH, P)
        st1 = ar.take(DNH, P)
        resid = ar.take(DNH, P)
        ot = ar.take(DNH, S)
        att_max = ar.take(16)
        att_z = ar.take(16)
        att_rz = ar.take(16)
        pt = ar.take(2, 3 * P)
        prob = qkvs[:].rearrange("p n s -> p (n s)").rearrange("p (i k) -> p i k", i=SWAH)
        qkn = qkvc[:, 0:8, :]
        tinv, xs = (sq[:, 4 * i:4 * i + 4, :].rearrange("p a (u k) -> p (a u) k", k=P) for i in range(2))
        bl = y[:].rearrange("p (w a) (u k) -> p w (a u) k", w=2, k=P)

        ar = Arena(region, ARENA)
        glu_g = ar.take(PAIRS, S)
        glu_v = ar.take(PAIRS, S)
        glu_a = ar.take(PAIRS, S)
        glu_p = ar.take(PAIRS, S)

        ar = Arena(region, ARENA)
        g_q = ar.take(S)
        g_k = ar.take(S)
        g_og = ar.take(2, S)
        g_v = ar.take(NT, S)
        g_lr = ar.take(S)
        g_c = ar.take(S)
        g_b = ar.take(S)
        g_ki = ar.take(NGB - 1, S)
        g_qe = ar.take(S)
        g_qb = ar.take(GH, S)
        g_pr = ar.take(GB, S)
        g_st = ar.take(GH, NT, S)
        g_in = ar.take(NT, GH, P)
        g_o = ar.take(2, S)
        g_sq = ar.take(2, S)
        c_sg = ar.take(2, S)
        c_z = ar.take(2, S + CW - 1)
        c_y = ar.take(2, S)
        c_sq = ar.take(2, S)
        c_tap = ar.take(S)
        d_raw, d_sq = h, sq
        d_rms, d_inv = ar.take(8 * 2 * NT), ar.take(8 * 2 * NT)
        g_rms, g_inv = ar.take(2 * 2 * NT), ar.take(2 * 2 * NT)
        c_rms, c_inv = ar.take(2 * 2 * NT), ar.take(2 * 2 * NT)
        o_rms, o_inv = ar.take(DFH * NT), ar.take(DFH * NT)
        d_v = ar.take(NT, 512)
        d_prob = ar.take(8, 3 * P)
        g_sp = region[:, ar.at - 24 * P:ar.at - 12 * P].rearrange("p (j s) -> p j s", j=6)
        d_max = ar.take(16)
        d_z = ar.take(16)
        d_rz = ar.take(16)
        d_pt = ar.take(2, 3 * P)
        d_o, d_osq = y[:, 0:4, :], sq[:, 0:4, :]
        lam_p = ar.take(2)
        lam_e = ar.take(2)
        nlam = ar.take(1)
        ngb = ar.take(1)
        ar = Arena(region, ARENA)
        r_log = ar.take(NT, NR)
        r_max = ar.take(NT)
        r_eq = ar.take(NT, 4)
        r_w = ar.take(NT, 4)
        r_m2 = ar.take(NT)
        r_oh = ar.take(NT, 4)
        r_e = ar.take(NT, 4)
        r_sum = ar.take(NT)
        r_pg = ar.take(NT)
        r_pro = ar.take(NT, 16)
        r_sel = ar.take(NT, 4)
        r_l1 = ar.take(NT)
        r_o1 = ar.take(NT, 4)
        r_s2 = ar.take(NT, 4)
        r_l2 = ar.take(NT)
        r_o2 = ar.take(NT, 4)
        r_d = ar.take(NT)
        r_e2 = ar.take(NT)
        r_u = ar.take(NT)
        r_w1 = ar.take(NT)
        r_w2 = ar.take(NT)
        r_t1 = ar.take(NT, 4)
        r_t2 = ar.take(NT, 4)
        r_gate = ar.take(NT, NE)
        gate_t = ar.take(S)
        gate_bc = ar.take(NE * S)
        e_act = ar.take(2, S)
        e_up = ar.take(2, S)
        e_prod = ar.take(2, S)

        bank = [ctx.enter_context(nc.psum_tensor(f"bank{i}", [P, 512], F32)) for i in range(8)]

        def cc(name, i=0, w=None, rows_=slice(0, P)):
            first, end = C_COLS[name]
            w = end - first if w is None else w
            return cst[rows_, first + i * w:first + (i + 1) * w]

        def pa_(name, i=0, w=1, rows_=slice(0, P)):
            return pa[rows_, A_COLS[name][0] + i:A_COLS[name][0] + i + w]

        def pf_(name, i=0):
            return pf[:, bass.ds(F_COLS[name][0] + i, 1)]

        def pb_(name, i=0, w=1, rows_=slice(0, P)):
            return pb[rows_, B_COLS[name][0] + i:B_COLS[name][0] + i + w]

        ident, ones, bd64, eps = cc("ident"), cc("ones256")[:, 0:P], cc("bd64"), cc("eps")

        x_in, consts_in, masks_in, packb_in = sem("x_in"), sem("consts_in"), sem("masks_in"), sem("packb_in")
        packa_in, packf_in = sem("packa_in"), sem("packf_in")
        w_in = [sem(f"w_in{i}") for i in range(SLOTS)]
        hi_ready, lo_ready = sem("hi_ready"), sem("lo_ready")
        tile_done = sem("tile_done")
        dve_chain, pool_chain = sem("dve_chain"), sem("pool_chain")
        norm_sq, norm_sum, norm_std, norm_inv, norm_row = (
            sem(f"norm_{n}") for n in ("sq", "sum", "std", "inv", "row"))
        norm_pair = sem("norm_pair")
        h_ready, h_hi, h_lo = (sem(f"h_{n}") for n in ("ready", "hi", "lo"))
        x_ready = sem("x_ready")
        mix_ready, mix_hi, mix_lo = (sem(f"mix_{n}") for n in ("ready", "hi", "lo"))
        conv_ready = sem("conv_ready")
        silu_ready = sem("silu_ready")
        sqk_ready = sem("sqk_ready")
        proj_evac = sem("proj_evac")
        ba_done = sem("ba_done")
        sp_act, sp_dve = sem("sp_act"), sem("sp_dve")
        beta_ready = sem("beta_ready")
        decay_ready = sem("decay_ready")
        rows_ready = sem("rows_ready")
        l2_sum, l2_std, l2_inv, l2_row, qk_ready = (sem(n) for n in ("l2_sum", "l2_std", "l2_inv", "l2_row", "qk_ready"))
        rope_rot, rope_used, rope_cos, rope_done = (
            sem(f"rope_{n}") for n in ("rot", "used", "cos", "done"))
        cols_done, cols_ready = sem("cols_done"), sem("cols_ready")
        bc_done, bc_act, bc_dve = sem("bc_done"), sem("bc_act"), sem("bc_dve")
        gam_ready, gb_ready, kbg_ready = sem("gam_ready"), sem("gb_ready"), sem("kbg_ready")
        gram_done, gram_used = sem("gram_done"), sem("gram_used")
        tr_done, tr_dve, tr_act = sem("tr_done"), sem("tr_dve"), sem("tr_act")
        bl_ready = sem("bl_ready")
        lev_x, lev_xs, lev_y, tu_ready = sem("lev_x"), sem("lev_xs"), sem("lev_y"), sem("tu_ready")
        rec_pe, rec_act, rec_dve = sem("rec_pe"), sem("rec_act"), sem("rec_dve")
        on_sum, on_std, on_inv, on_row = (sem(f"on_{n}") for n in ("sum", "std", "inv", "row"))
        att_s, att_sm, att_p, att_pn = (sem(f"att_{n}") for n in ("s", "sm", "p", "pn"))
        att_t, att_pt, att_pv, att_o = (sem(f"att_{n}") for n in ("t", "pt", "pv", "o"))
        ffn_free = sem("ffn_free")
        ffn_chain = sem("ffn_chain")
        glu_first = sem("glu_first")
        glu_ready, gelu_done, hid_done = sem("glu_ready"), sem("gelu_done"), sem("hid_done")
        down_done = sem("down_done")
        prod_done, hi_done = sem("prod_done"), sem("hi_done")
        conv_first = sem("conv_first")
        zeroed = sem("zeroed")
        lr_done, lr_ready, ngb_ready, gc_ready = (sem(f"gla_{n}") for n in ("lr_done", "lr_ready", "nb", "c"))
        u_evac, cz_ready, cy_ready = sem("u_evac"), sem("cz_ready"), sem("cy_ready")
        dsq_ready, dn_sum, dn_std, dn_inv, dn_row, dn_ready = (sem(f"dn_{n}") for n in ("sq", "sum", "std", "inv", "row", "ready"))
        lam_ready, lam_sum, lam_exp = sem("lam_ready"), sem("lam_sum"), sem("lam_exp")
        ge_ready, ki_ready, qe_ready, taps_done = (sem(n) for n in ("ge_ready", "ki_ready", "qe_ready", "taps_done"))
        st_done, st_copied = sem("st_done"), sem("st_copied")
        pr_sub, pr_exp, pr_q, pr_ready = (sem(f"pr_{n}") for n in ("sub", "exp", "q", "ready"))
        dg_ready = sem("dg_ready")
        go_sq, gla_mix = sem("go_sq"), sem("gla_mix")
        hn_sum, hn_std, hn_inv, hn_row = (sem(f"hn_{n}") for n in ("sum", "std", "inv", "row"))
        df_s, df_sm, df_p, df_pn, df_t, df_pt, df_pv, df_o = (
            sem(f"df_{n}") for n in ("s", "sm", "p", "pn", "t", "pt", "pv", "o"))
        diff_mix = sem("diff_mix")
        cm_done, cc_ready, csq_ready, cn_ready, conv_mix = (
            sem(f"conv_{n}") for n in ("mean", "centred", "sq", "norm", "mix"))
        x_added, rt_done, r_sub, r_exp, gates_ready = (sem(f"route_{n}") for n in ("x", "logits", "sub", "exp", "gates"))
        gt_done, gt_ready, gbc_done, gbc_ready = sem("gt_done"), sem("gt_ready"), sem("gbc_done"), sem("gbc_ready")
        ex_act, ex_up, ex_prod, ex_hi, ex_hid, ex_add = (sem(f"ex_{n}") for n in ("act", "up", "prod", "hi", "hid", "add"))
        out_done = sem("out_done")

        def second_tensor(pe, tile_in, product, wblock, project, project_two, project_tokens, lengths, spread, norm_sums, norm_rows, row_norm, transpose, scores):
            halves = bd64.rearrange("p (a b) -> p a b", b=64)[:, :, 0]
            def unit_rows(g):
                pe.wait_ge(dn_inv, g // 2 + 1)
                if g % 2:
                    pe.wait_ge(dn_ready, 2 * g)
                for i in range(2 * g, 2 * g + 2):
                    spread(bank[6 + g // 2][:, i % 2 * S:i % 2 * S + S], d_inv[:, 4 * i:4 * i + 4], 2).then_inc(dn_row, 1)

            row_norm(NORM2, 2 * DEPTH)
            pe.wait_ge(packb_in, 16)
            for k in range(KD):
                pe.wait_ge(h_ready, DEPTH * 16 + k + 1)
                mm = t.matmul(bank[5][0:GRANK, 0:S], pb_("wglr", k * GRANK, GRANK), h[:, k, :],
                              start=k == 0, stop=k == KD - 1)
            mm.then_inc(lr_done, 1)
            for u in range(U_WOUT):
                n = T2 + u
                if u >= 4:
                    if u - 4 in CONV_VALUES:
                        pe.wait_ge(cz_ready, CONV_VALUES.index(u - 4) + 1)
                    else:
                        pe.wait_ge(u_evac, evacuated((u if in_features(u) and in_features(u - 4) else u | 1) - 4))
                if not in_features(u):
                    project_tokens(n, n % SLOTS, u % 2, [bank[u // 2 * 2 % 4 + c] for c in range(NT)])
                elif u == 0:
                    project_two(n, 0, (h_lo, DEPTH * 16))
                elif u > 1:
                    project(n, n % SLOTS, bank[u % 4][:, 0:S])
                if u == 2:
                    pe.wait_ge(lr_ready, 1)
                    t.matmul(bank[5][:, S:2 * S], pb_("gatew", 0, P, slice(0, GRANK)), g_lr[0:GRANK, :],
                             start=True, stop=True).then_inc(lr_done, 1)
                if u == U_SCORES:
                    pe.wait_ge(ki_ready, 1)
                    for b in range(1, NGB):
                        at = (b - 1) % 8 * GH * GB
                        mm = t.matmul(bank[4 + (b - 1) // 8][:, at:at + GH * GB], g_ki[:, b - 1, 0:P],
                                      g_qb[:, :, b * GB:(b + 1) * GB], start=True, stop=True)
                        if b in (8, NGB - 1):
                            mm.then_inc(st_done, 1)
                if u == U_SCORES + 2:
                    pe.wait_ge(st_copied, 1)
                    for b in range(P // GB + 1, NGB):
                        at = (b - P // GB - 1) * GH * GB
                        mm = t.matmul(bank[4][:, at:at + GH * GB], g_ki[:, b - 1, P:S],
                                      g_qb[:, :, b * GB:(b + 1) * GB], start=True, stop=True)
                    mm.then_inc(st_done, 1)
                if U_WITHIN <= u < U_WITHIN + NT:
                    jt = u - U_WITHIN
                    pe.wait_ge(pr_ready, 1)
                    pe.wait_ge(st_copied, 3)
                    for r in range(GB):
                        at = (jt * GB + r) * GH
                        mm = t.matmul(bank[4][:, at:at + GH], g_pr[:, r, jt * P:(jt + 1) * P], cc("selhead"),
                                      start=True, stop=True)
                    if jt == NT - 1:
                        mm.then_inc(st_done, 1)
                i = u - U_DQ - 1
                if 0 <= i < 8:
                    pe.wait_ge(dsq_ready, i + 1)
                    mm = lengths(bank[6 + i // 4][:, i % 4 * 4:i % 4 * 4 + 4], d_sq[:, i, :], halves)
                    if i % 4 == 3:
                        mm.then_inc(dn_sum, 1)
                if u in SPREAD_STEPS:
                    unit_rows(SPREAD_STEPS.index(u))
            unit_rows(3)
            pe.wait_ge(dg_ready, 1)
            for i in range(GH):
                o_ = bank[5][64 * (i % 2):64 * (i % 2) + 64, i // 2 * S:i // 2 * S + S]
                vals = g_v[:, :, i * GDV:(i + 1) * GDV]
                t.matmul(o_[:, 0:P], vals[:, 0, :], g_st[:, i, 0, 0:P], start=True, stop=True)
                t.matmul(o_[:, P:S], vals[:, 0, :], g_st[:, i, 0, P:S], start=True, stop=False)
                mm = t.matmul(o_[:, P:S], vals[:, 1, :], g_st[:, i, 1, P:S], start=False, stop=True)
            mm.then_inc(st_done, 1)
            pe.wait_ge(go_sq, 2)
            for j in range(2):
                mm = lengths(bank[4][:, 4 * j:4 * j + 4], g_sq[:, j, :], halves)
            mm.then_inc(hn_sum, 1)
            pe.wait_ge(lam_ready, 1)
            pe.wait_ge(dn_ready, 4)
            t.matmul(bank[6][:, 0:2], ones[0:64, :], lam_p[0:64, :], start=True, stop=True).then_inc(lam_sum, 1)

            pe.wait_ge(u_evac, evacuated(U_WOUT - 1))
            pe.wait_ge(dn_ready, 8)
            for i in range(8 + 5):
                if i < 8:
                    if i >= 2:
                        pe.wait_ge(df_sm, i - 1)
                    scores(i, d_raw[:, 0:4, :], d_raw[:, 4:8, :], bank[2 + i % 2]).then_inc(df_s, 1)
                if i == 1:
                    pe.wait_ge(hn_inv, 1)
                    for j in range(2):
                        mm = spread(bank[4][:, j * S:(j + 1) * S], g_inv[:, 4 * j:4 * j + 4], 2)
                    mm.then_inc(hn_row, 1)
                if i == 3:
                    pe.wait_ge(cy_ready, 1)
                    for j in range(2):
                        mm = t.matmul(bank[5][:, j * S:(j + 1) * S], bd64, c_y[:, j, :], start=True, stop=True)
                    mm.then_inc(cm_done, 1)
                if i == 6:
                    pe.wait_ge(csq_ready, 2)
                    for j in range(2):
                        mm = lengths(bank[5][:, 4 * j:4 * j + 4], c_sq[:, j, :], halves)
                    mm.then_inc(hn_sum, 1)
                j, odd = divmod(i - 3, 2)
                if 0 <= j < DFH and odd == 0:
                    pe.wait_ge(df_pn, j + 1)
                    if j >= 2:
                        pe.wait_ge(df_pt, j - 1)
                    if j == 0:
                        pe.wait_ge(lam_exp, 1)
                    b = bank[6 + j % 2]
                    transpose(b[:, 0:P], d_prob[:, 2 * j, 0:P])
                    transpose(b[:, P:2 * P], d_prob[:, 2 * j, P:2 * P])
                    transpose(b[:, 2 * P:3 * P], d_prob[:, 2 * j, 2 * P:3 * P]).then_inc(df_t, 1)
                j, odd = divmod(i - 4, 2)
                if 0 <= j < DFH and odd == 0:
                    pe.wait_ge(df_pt, j + 1)
                    if j >= 2:
                        pe.wait_ge(df_o, 2 * j - 2)
                    o_ = bank[j % 2]
                    vals = d_v[:, :, j * P:(j + 1) * P]
                    t.matmul(o_[:, 0:P], vals[:, 0, :], d_pt[:, j % 2, 0:P], start=True, stop=True)
                    t.matmul(o_[:, P:S], vals[:, 0, :], d_pt[:, j % 2, P:2 * P], start=True, stop=False)
                    t.matmul(o_[:, P:S], vals[:, 1, :], d_pt[:, j % 2, 2 * P:3 * P], start=False,
                             stop=True).then_inc(df_pv, 1)
                j, odd = divmod(i - 5, 2)
                if 0 <= j < DFH and odd == 0:
                    if j == 0:
                        pe.wait_ge(gla_mix, 1)
                    pe.wait_ge(df_o, 2 * j + 2)
                    mm = lengths(bank[4][:, 2 * j:2 * j + 2], d_osq[:, j, :], ones[:, 0:1])
            mm.then_inc(hn_sum, 1)
            pe.wait_ge(hn_inv, 2)
            for j in range(2):
                mm = spread(bank[5][:, j * S:(j + 1) * S], c_inv[:, 4 * j:4 * j + 4], 2)
            mm.then_inc(hn_row, 1)
            pe.wait_ge(hn_inv, 3)
            for j in range(DFH):
                spread(bank[j // 2][:, j % 2 * S:j % 2 * S + S], o_inv[:, 2 * j:2 * j + 2]).then_inc(hn_row, 1)

            for m in range(KD):
                n = T2 + U_WOUT + m
                tile_in(n)
                if m >= 4:
                    pe.wait_ge(x_added, m - 3)
                for k in range(KD):
                    if m == 0:
                        pe.wait_ge(mix_lo, DEPTH * KD + k + 1)
                    mm = product(bank[4 + m % 4][:, 0:S], wblock(n % SLOTS, k), (act_hi[:, k, :], act_lo[:, k, :]),
                                 k == 0, k == KD - 1)
                mm.then_inc(tile_done, 1)
                if m % 2 and m >= 3:
                    norm_sums(NORM2 + 1, m // 2 - 1)
            norm_sums(NORM2 + 1, KD // 2 - 1)
            norm_rows(NORM2 + 1, 4)
            first = T2 + U_EXP
            project_two(first, 0, (h_lo, DEPTH * 16 + 8))

            pe.wait_ge(h_ready, DEPTH * 16 + 16)
            for c in range(NT):
                for k in range(KD):
                    t.matmul(bank[5][:, c * NR:(c + 1) * NR], h[:, k, c * P:(c + 1) * P], pb_("wrt", k * NR, NR),
                             start=k == 0, stop=False)
                mm = t.matmul(bank[5][:, c * NR:(c + 1) * NR], ones[0:1, :], pb_("rbias", 0, NR, slice(0, 1)),
                              start=False, stop=True)
            mm.then_inc(rt_done, 1)

            def expert_up(n, e, slots, between=None):
                for j, s in enumerate(slots):
                    if j == 2 and between:
                        between()
                    if j < 2:
                        pe.wait_ge(ex_act, 2 * e + j - 1)
                    else:
                        pe.wait_ge(ex_up, 2 * e + j - 3)
                    project(n + j, s, bank[j][:, 0:S])

            def expert_down(n, e, slots):
                pe.wait_ge(ex_hid, 2 * e + 2 + EX_CREDITS)
                for j, s in enumerate(slots):
                    tile_in(n + j)
                    for m in range(4 * j, 4 * j + 4):
                        if m % 2 == 0:
                            pe.wait_ge(ex_add, 4 * e + m // 2 + 1)
                        for k in range(2):
                            mm = product(bank[4 + m // 2][:, m % 2 * S:m % 2 * S + S], wblock(s, (m % 4) * 2 + k),
                                         (hid_hi[:, k, :], hid_lo[:, k, :]), k == 0, k == 1)
                    mm.then_inc(tile_done, 1)

            for j in range(2, 4):
                project(first + j, j % SLOTS, bank[j][:, 0:S])
            def gates_out():
                pe.wait_ge(gates_ready, 1)
                for c in range(NT):
                    mm = transpose(bank[4][0:NE, c * P:(c + 1) * P], r_gate[:, c, :])
                mm.then_inc(gt_done, 1)
                pe.wait_ge(gt_ready, 1)
                for i in range(NE // 2):
                    if i >= 2:
                        pe.wait_ge(gbc_ready, i - 1)
                    for j in range(2):
                        mm = t.matmul(bank[6 + i % 2][:, j * S:(j + 1) * S],
                                      ident[0:NE, 2 * i + j:2 * i + j + 1].to_broadcast([NE, P]), gate_t[0:NE, :],
                                      start=True, stop=True)
                    mm.then_inc(gbc_done, 1)

            expert_up(first + 4, 1, (1, 2, 0, 1), gates_out)
            expert_down(first + 8, 0, (2, 0))
            with pe.Fori(1, NE - 1) as e:
                expert_up(e * RING + (first + 4), e + 1, (1, 2, 0, 1))
                expert_down(e * RING + (first + 8), e, (2, 0))
            expert_down(first + NE * RING - 2, NE - 1, (1, 2))

        def second_scalar(act, pre_norm, pre_square, norm_root, pre_hi, softplus, refill_hi):
            def refill(u):
                refill_hi(T2 // SLOTS, u)

            def mix_part(k):
                a.activation(act_hi[:, k, :], mix[:, k, :], ACT.Copy).then_inc(mix_hi, 1)

            pre_norm(NORM2, x_ready, DEPTH * 16, DEPTH * 16)
            act.wait_ge(lr_done, 1)
            a.activation(g_lr[0:GRANK, :], bank[5][0:GRANK, 0:S], ACT.Copy).then_inc(lr_ready, 1)
            act.wait_ge(packb_in, 16)
            def gate(j):
                a.activation(c_sg[:, j, :], bank[(CONV_VALUES[j] + 1) % 4][:, 0:S], ACT.Sigmoid).then_inc(u_evac, 1)

            for u in range(U_WOUT):
                src = bank[u % 4]
                act.wait_ge(tile_done, T2 + u + 1)
                if u < 2:
                    a.activation((g_q, g_k)[u], src[:, 0:S], ACT.Copy, scale=(GDK ** -0.5, 1.0)[u]).then_inc(u_evac, 1)
                elif u in CONV_VALUES:
                    pass
                elif u < U_GOG:
                    if u == U_GOG - 1:
                        gate(1)
                elif u < U_GV:
                    a.activation(g_og[:, u - U_GOG, :], src[:, 0:S], ACT.Silu).then_inc(u_evac, 1)
                elif u < U_DQ:
                    if u % 2:
                        for c in range(NT):
                            a.activation(g_v[:, c, :], bank[(u - 1 + c) % 4][:, 0:S], ACT.Copy).then_inc(u_evac, 1)
                elif u < U_DV:
                    i = u - U_DQ
                    a.activation(d_sq[:, i, :], src[:, 0:S], ACT.Square).then_inc(dsq_ready, 1)
                    a.activation(d_raw[:, i, :], src[:, 0:S], ACT.Copy).then_inc(u_evac, 1)
                elif u % 2:
                    j = (u - U_DV) // 2
                    for c in range(NT):
                        a.activation(d_v[:, c, j * S:(j + 1) * S], bank[(u - 1 + c) % 4][:, 0:S], ACT.Copy).then_inc(u_evac, 1)
                refill(u)
                if U_CONV <= u < U_CONV + 3:
                    if u == U_CONV:
                        act.wait_ge(lr_done, 2)
                        act.wait_ge(ngb_ready, 1)
                    softplus(u - U_CONV, DEPTH, bank[5][:, S:2 * S], ngb, -1.0, g_sp, 0, P)
                if u == U_CONV + 2:
                    gate(0)
                if U_GV <= u < U_GV + 5:
                    if u == U_GV:
                        act.wait_ge(gc_ready, 1)
                        act.wait_ge(zeroed, 3)
                    for b in range(1 + 3 * (u - U_GV), 4 + 3 * (u - U_GV)):
                        ins = a.activation(g_ki[:, b - 1, 0:b * GB], g_c[:, 0:b * GB], ACT.Exp,
                                           bias=g_b[:, b * GB - 1:b * GB])
                    if b == NGB - 1:
                        ins.then_inc(ge_ready, 1)
                if u == U_GV + 1:
                    act.wait_ge(qe_ready, 1)
                    a.activation(g_qe[:, GB:], g_qe[:, GB:], ACT.Exp).then_inc(qe_ready, 1)
                if u == U_PAIRS - 1:
                    act.wait_ge(pr_sub, 1)
                    a.activation(g_pr[:], g_pr[:], ACT.Exp).then_inc(pr_exp, 1)
                if u in (U_SCORES + 1, U_SCORES + 3):
                    for jt, lo, hi in ((0, 1, 9), (0, 9, NGB)) if u == U_SCORES + 1 else ((1, P // GB + 1, NGB),):
                        if u == U_SCORES + 1:
                            src = bank[4 + lo // 9]
                            act.wait_ge(zeroed, 4)
                            act.wait_ge(st_done, 1 + lo // 9)
                        else:
                            src = bank[4]
                            act.wait_ge(st_done, 3)
                        a.activation(g_st[:, :, jt, lo * GB:hi * GB].rearrange("p h (b i) -> p h b i", i=GB),
                                     src[:, 0:(hi - lo) * GH * GB].rearrange("p (b h i) -> p h b i", h=GH, i=GB),
                                     ACT.Copy).then_inc(st_copied, 1)
                if u in (U_DQ + 4, U_DQ + 8):
                    b = (u - U_DQ - 4) // 4
                    act.wait_ge(dn_sum, b + 1)
                    a.activation(d_rms[:, 16 * b:16 * b + 16], bank[6 + b][:, 0:16], ACT.Sqrt, bias=eps,
                                 scale=1.0 / 64).then_inc(dn_std, 1)
            act.wait_ge(st_done, 5)
            outs = bank[5][:, :].rearrange("p (j s) -> p j s", j=2)
            a.activation(g_sq[:], outs, ACT.Square).then_inc(go_sq, 1)
            a.activation(g_o[:], outs, ACT.Copy).then_inc(go_sq, 1)
            act.wait_ge(hn_sum, 1)
            a.activation(g_rms[:], bank[4][:, 0:8], ACT.Sqrt, bias=eps, scale=1.0 / GDV).then_inc(hn_std, 1)
            act.wait_ge(lam_sum, 1)
            a.activation(lam_e[:], bank[6][:, 0:2], ACT.Exp).then_inc(lam_exp, 1)
            for i in range(8 + 5):
                if i < 8:
                    act.wait_ge(df_sm, i + 1)
                    a.activation(d_prob[:, i, 0:P], d_prob[:, i, 0:P], ACT.Exp, bias=d_max[:, 2 * i:2 * i + 1],
                                 accum_out=d_z[:, 2 * i:2 * i + 1])
                    a.activation(d_prob[:, i, P:3 * P], d_prob[:, i, P:3 * P], ACT.Exp,
                                 bias=d_max[:, 2 * i + 1:2 * i + 2],
                                 accum_out=d_z[:, 2 * i + 1:2 * i + 2]).then_inc(df_p, 1)
                if i == 3:
                    act.wait_ge(gla_mix, 1)
                    for k in range(2):
                        mix_part(k)
                j, odd = divmod(i - 3, 2)
                if 0 <= j < DFH and odd == 0:
                    act.wait_ge(df_t, j + 1)
                    if j >= 2:
                        act.wait_ge(df_pv, j - 1)
                    a.activation(d_pt[:, j % 2, :], bank[6 + j % 2][:, 0:3 * P], ACT.Copy).then_inc(df_pt, 1)
                j, odd = divmod(i - 4, 2)
                if 0 <= j < DFH and odd == 0:
                    act.wait_ge(df_pv, j + 1)
                    a.activation(d_osq[:, j, :], bank[j % 2][:, 0:S], ACT.Square).then_inc(df_o, 1)
                    a.activation(d_o[:, j, :], bank[j % 2][:, 0:S], ACT.Copy).then_inc(df_o, 1)
                if i == 5:
                    for j in range(2):
                        act.wait_ge(cc_ready, j + 1)
                        a.activation(c_sq[:, j, :], c_y[:, j, :], ACT.Square).then_inc(csq_ready, 1)
                if i == 10:
                    act.wait_ge(hn_sum, 2)
                    a.activation(c_rms[:], bank[5][:, 0:8], ACT.Sqrt, bias=eps, scale=1.0 / 64).then_inc(hn_std, 1)
            act.wait_ge(hn_sum, 3)
            a.activation(o_rms[:], bank[4][:, 0:2 * DFH], ACT.Sqrt, bias=eps, scale=1.0 / P).then_inc(hn_std, 1)
            for j in range(2):
                act.wait_ge(cn_ready, j + 1)
                a.activation(mix[:, 2 + j, :], c_y[:, j, :], ACT.Silu, bias=pb_("cnb", j),
                             scale=pb_("cng", j)).then_inc(conv_mix, 1)
            for j in range(2):
                act.wait_ge(conv_mix, j + 1)
                mix_part(2 + j)
            for j in range(DFH):
                act.wait_ge(diff_mix, j + 1)
                mix_part(4 + j)
            for m in range(KD):
                if m < KD - 1:
                    refill(U_WOUT + m)
                if m % 2:
                    pre_square(m - 1, x_added, 0)
            norm_root(NORM2 + 1)
            refill(U_EXP - 1)
            pre_hi(DEPTH * 16 + 8)

            first = (T2 + U_EXP) // SLOTS

            def gate(r, at, e, j):
                act.wait_ge(tile_done, r * SLOTS + at + j + 1)
                act.wait_ge(ex_hid, 2 * e + j + 1)
                a.activation(e_act[:, j, :], bank[j][:, 0:S], ACT.Silu).then_inc(ex_act, 1)

            for j in range(2):
                gate(first, 0, 0, j)
                refill_hi(first, j)
            act.wait_ge(r_sub, 1)
            a.activation(r_e[:], r_e[:], ACT.Exp).then_inc(r_exp, 1)
            refill_hi(first, 2)
            act.wait_ge(r_sub, 2)
            a.activation(r_e2[:], r_d[:], ACT.Exp).then_inc(r_exp, 1)
            refill_hi(first, 3)
            act.wait_ge(gt_done, 1)
            a.activation(gate_t[0:NE, :], bank[4][0:NE, 0:S], ACT.Copy).then_inc(gt_ready, 1)
            for i in range(NE // 2):
                act.wait_ge(gbc_done, i + 1)
                a.activation(gate_bc[:, 2 * i * S:2 * (i + 1) * S], bank[6 + i % 2][:, :], ACT.Copy).then_inc(gbc_ready, 1)

            def expert(e, refills):
                r = e * (RING // SLOTS) + first
                for j in range(refills):
                    if j < 2:
                        gate(r, 4, e + 1, j)
                    refill_hi(r, 4 + j)

            with act.Fori(0, NE - 2) as e:
                expert(e, RING)
            expert(NE - 2, RING - 1)

        def second_vector(dve, norm_apply, softplus, refill_lo, part_lo):
            def refill(u):
                refill_lo(T2 // SLOTS, u)

            ch = Chain(dve, dve_chain, DEPTH * DVE_LINKS)
            dve.wait_ge(packb_in, 16)
            v.tensor_scalar(ngb, pb_("glab"), -1.0, None, ALU.mult).then_inc(ngb_ready, 1)
            lam = pb[0:64, B_COLS["lam"][0]:B_COLS["lam"][0] + 4].rearrange("p (a b) -> p a b", b=2)
            v.tensor_tensor(lam_p[0:64, :], lam[:, :, 0], lam[:, :, 1], ALU.mult).then_inc(lam_ready, 1)
            norm_apply(NORM2, lambda k: pb_("mix", k), DEPTH * 16)

            def conv_value(j):
                dve.wait_ge(zeroed, 2)
                dve.wait_ge(u_evac, evacuated(CONV_VALUES[j] + 1))
                dve.wait_ge(tile_done, T2 + CONV_VALUES[j] + 1)
                v.tensor_tensor(c_z[:, j, CW - 1:], bank[CONV_VALUES[j] % 4][:, 0:S], c_sg[:, j, :],
                                ALU.mult).then_inc(cz_ready, 1)

            def log_decays():
                r = softplus(2, ch, DEPTH, g_sp, 0, P)
                ch.mark(v.tensor_tensor_scan(r, cc("ones256"), r, 0.0, ALU.mult, ALU.add))
                ch.dep()
                ch.mark(v.tensor_scalar(g_b, r, -1.0 / GTAU, None, ALU.mult))
                v.tensor_scalar(g_c, r, 1.0 / GTAU, None, ALU.mult).then_inc(gc_ready, 1)

            def taps(j, first, end):
                if first == 0:
                    dve.wait_ge(cz_ready, 2)
                if j == 1 and first == POOL_TAPS[-1]:
                    dve.wait_ge(taps_done, 1)
                for w in range(first, end):
                    src = c_z[:, j, w:w + S]
                    if w:
                        ch.dep()
                        ins = v.scalar_tensor_tensor(c_y[:, j, :], src, pb_("convw", j * CW + w), c_y[:, j, :],
                                                     ALU.mult, ALU.add)
                    else:
                        ins = v.tensor_scalar(c_y[:, j, :], src, pb_("convw", j * CW), pb_("convb", j), ALU.mult, ALU.add)
                    ch.mark(ins)

            def query_decays():
                by_block = g_c[:].rearrange("p (b r) -> p b r", r=GB)
                dve.wait_ge(gc_ready, 1)
                v.tensor_tensor(g_qe[:, GB:].rearrange("p (b r) -> p b r", r=GB),
                                by_block[:, 0:NGB - 1, GB - 1].unsqueeze(2).to_broadcast([P, NGB - 1, GB]),
                                by_block[:, 1:NGB, :], ALU.subtract).then_inc(qe_ready, 1)

            def between_blocks():
                dve.wait_ge(ge_ready, 1)
                for b in range(1, NGB):
                    v.tensor_tensor(g_ki[:, b - 1, 0:b * GB], g_ki[:, b - 1, 0:b * GB], g_k[:, 0:b * GB], ALU.mult)
                dve.wait_ge(qe_ready, 2)
                ch.mark(v.tensor_tensor(g_qe[:, GB:], g_qe[:, GB:], g_q[:, GB:], ALU.mult))
                ch.dep()
                v.tensor_tensor(g_qb[:, :, GB:], g_qe[:, GB:].unsqueeze(1).to_broadcast([P, GH, S - GB]),
                                cc("selhead").unsqueeze(2).to_broadcast([P, GH, S - GB]), ALU.mult).then_inc(ki_ready, 1)

            def pairs_q():
                dve.wait_ge(pr_exp, 1)
                for r in range(GB):
                    pr = g_pr[:, r, :].rearrange("p (b j) -> p b j", j=GB)[:, :, 0:r + 1]
                    q_i = g_q[:].rearrange("p (b r) -> p b r", r=GB)[:, :, r].unsqueeze(2).to_broadcast([P, NGB, r + 1])
                    ins = v.tensor_tensor(pr, pr, q_i, ALU.mult)
                ins.then_inc(pr_q, 1)

            def within_blocks():
                dve.wait_ge(st_done, 4)
                dve.wait_ge(st_copied, 3)
                nb = P // GB
                for jt in range(NT):
                    src = bank[4][:, jt * GB * GH:(jt + 1) * GB * GH].rearrange("p (r h) -> p h r", h=GH)
                    ch.mark(v.tensor_tensor(g_in[:, jt].rearrange("p h (b r) -> p h b r", r=GB),
                                            src.unsqueeze(2).to_broadcast([P, GH, nb, GB]),
                                            cc("gmask").rearrange("p (b r) -> p b r", r=GB).unsqueeze(1).to_broadcast([P, GH, nb, GB]),
                                            ALU.mult))
                for jt in range(NT):
                    ch.dep_before(NT - 1 - jt)
                    here = g_st[:, :, jt, jt * P:(jt + 1) * P]
                    ins = v.tensor_tensor(here, here, g_in[:, jt], ALU.add)
                ins.then_inc(dg_ready, 1)

            def unit_inverse(b):
                dve.wait_ge(dn_std, b + 1)
                v.reciprocal(d_inv[:, 16 * b:16 * b + 16], d_rms[:, 16 * b:16 * b + 16]).then_inc(dn_inv, 1)

            def unit(i):
                dve.wait_ge(dn_row, i // 2 * 2 + 2)
                dve.wait_ge(u_evac, evacuated(U_DQ + i))
                v.scalar_tensor_tensor(d_raw[:, i, :], d_raw[:, i, :], pb_("qn" if i < 4 else "kn"),
                                       bank[6 + i // 4][:, i % 2 * S:i % 2 * S + S], ALU.mult, ALU.mult).then_inc(dn_ready, 1)

            tap = [0, POOL_TAPS[-1]]

            def some_taps(n0, n1):
                for j, n in enumerate((n0, n1)):
                    n = min(n, CW - tap[j])
                    if n > 0:
                        taps(j, tap[j], tap[j] + n)
                        tap[j] += n

            for u in range(U_WOUT):
                if u in (U_GOG - 1, U_GOG):
                    conv_value(u - U_GOG + 1)
                if U_CONV + 1 <= u < U_CONV + 3:
                    softplus(u - U_CONV - 1, ch, DEPTH, g_sp, 0, P)
                if u == U_CONV + 3:
                    log_decays()
                if u == U_GOG:
                    query_decays()
                if u == U_PAIRS:
                    pairs_q()
                if u == U_BETWEEN:
                    between_blocks()
                if u in (U_DQ + 5, U_DQ + 9):
                    unit_inverse((u - U_DQ - 5) // 4)
                if u - 1 in SPREAD_STEPS:
                    g = SPREAD_STEPS.index(u - 1)
                    unit(2 * g)
                    unit(2 * g + 1)
                refill(u)
                if u == U_WITHIN + 1:
                    within_blocks()
                if U_GOG <= u:
                    some_taps(2, 1 if u >= U_SCORES + 2 else 0)
            unit(6)
            unit(7)
            dve.wait_ge(lam_exp, 1)
            ch.mark(v.scalar_tensor_tensor(nlam, lam_e[:, 1:2], -LAMBDA_INIT, lam_e[:, 0:1], ALU.add, ALU.subtract))
            dve.wait_ge(hn_std, 1)
            v.reciprocal(g_inv, g_rms).then_inc(hn_inv, 1)

            def masked(i):
                dve.wait_ge(df_s, i + 1)
                ch.mark(v.scalar_tensor_tensor(d_prob[:, i, :], bank[2 + i % 2][:, 0:3 * P], 64 ** -0.5,
                                               cc("causal"), ALU.mult, ALU.add))
                ch.dep()
                ch.mark(v.tensor_reduce(d_max[:, 2 * i:2 * i + 1], d_prob[:, i, 0:P], AX_X, ALU.max, negate=True))
                v.tensor_reduce(d_max[:, 2 * i + 1:2 * i + 2], d_prob[:, i, P:3 * P], AX_X, ALU.max,
                                negate=True).then_inc(df_sm, 1)

            def difference(j):
                dve.wait_ge(df_p, 2 * j + 2)
                ch.mark(v.reciprocal(d_rz[:, 4 * j:4 * j + 4], d_z[:, 4 * j:4 * j + 4]))
                ch.dep()
                ch.mark(v.tensor_scalar(d_rz[:, 4 * j + 2:4 * j + 4], d_rz[:, 4 * j + 2:4 * j + 4], nlam, None, ALU.mult))
                parts = (slice(0, P), slice(P, 3 * P))
                for c, part in enumerate(parts):
                    ch.mark(v.tensor_scalar(d_prob[:, 2 * j, part], d_prob[:, 2 * j, part],
                                            d_rz[:, 4 * j + c:4 * j + c + 1], None, ALU.mult))
                ch.dep()
                for c, part in enumerate(parts):
                    ins = v.scalar_tensor_tensor(d_prob[:, 2 * j, part], d_prob[:, 2 * j + 1, part],
                                                 d_rz[:, 4 * j + 2 + c:4 * j + 3 + c], d_prob[:, 2 * j, part],
                                                 ALU.mult, ALU.add)
                ins.then_inc(df_pn, 1)

            for i in range(8 + 2):
                if i < 8:
                    masked(i)
                if i == 2:
                    dve.wait_ge(hn_row, 1)
                    ch.mark(v.scalar_tensor_tensor(g_o[:], g_o[:], pb_("glan"), bank[4][:, :].rearrange("p (j s) -> p j s", j=2),
                                                   ALU.mult, ALU.mult))
                    ch.dep()
                    v.tensor_tensor(mix[:, 0:2, :], g_o[:], g_og[:], ALU.mult).then_inc(gla_mix, 1)
                if i == 4:
                    for k in range(2):
                        part_lo(k, mix, mix_hi, DEPTH * 4 + k + 1, mix_lo)
                    dve.wait_ge(cm_done, 1)
                    for j in range(2):
                        v.scalar_tensor_tensor(c_y[:, j, :], bank[5][:, j * S:(j + 1) * S], -1.0 / 64, c_y[:, j, :],
                                               ALU.mult, ALU.add).then_inc(cc_ready, 1)
                j, odd = divmod(i - 2, 2)
                if 0 <= j < DFH and odd == 0:
                    difference(j)
                if i < 2:
                    some_taps(CW, CW) if i else some_taps(3, 4)
                    if i == 1:
                        ch.dep()
                        v.memset(credit[:, 17:18], 0.0).then_inc(cy_ready, 1)
            dve.wait_ge(hn_std, 2)
            v.reciprocal(c_inv, c_rms).then_inc(hn_inv, 1)
            dve.wait_ge(hn_std, 3)
            ch.mark(v.reciprocal(o_inv, o_rms))
            ch.dep()
            v.tensor_scalar(o_inv, o_inv, 1.0 - LAMBDA_INIT, None, ALU.mult).then_inc(hn_inv, 1)
            dve.wait_ge(hn_row, 2)
            for j in range(2):
                v.tensor_tensor(c_y[:, j, :], c_y[:, j, :], bank[5][:, j * S:(j + 1) * S], ALU.mult).then_inc(cn_ready, 1)
            for j in range(DFH):
                dve.wait_ge(hn_row, 2 + j // 2 * 2 + 2)
                v.scalar_tensor_tensor(mix[:, 4 + j, :], d_o[:, j, :], pb_("subln"), bank[j // 2][:, j % 2 * S:j % 2 * S + S],
                                       ALU.mult, ALU.mult).then_inc(diff_mix, 1)
            for k in range(2, KD):
                part_lo(k, mix, mix_hi, DEPTH * 4 + k + 1, mix_lo)
            for m in range(KD):
                dve.wait_ge(tile_done, T2 + U_WOUT + m + 1)
                v.tensor_tensor(x[:, m, :], x[:, m, :], bank[4 + m % 4][:, 0:S], ALU.add).then_inc(x_added, 1)
                if m < KD - 1:
                    refill(U_WOUT + m)
            dve.wait_ge(x_added, KD)
            norm_apply(NORM2 + 1, lambda k: pb_("ffn", k), DEPTH * 16 + 8)
            refill(U_EXP - 1)

            def b4(col, n=4):
                return col.unsqueeze(2).to_broadcast([P, NT, n])

            order = cc("first4").unsqueeze(1).to_broadcast([P, NT, 4])

            def first_max(vals, best, onehot):
                ch.mark(v.tensor_reduce(best, vals, AX_X, ALU.max))
                ch.dep()
                ch.mark(v.tensor_tensor(r_eq[:], vals, b4(best), ALU.is_equal))
                ch.dep()
                ch.mark(v.tensor_tensor(r_w[:], r_eq[:], order, ALU.mult))
                ch.dep()
                ch.mark(v.tensor_reduce(r_m2[:], r_w[:], AX_X, ALU.max))
                ch.dep()
                ch.mark(v.tensor_tensor(onehot, r_w[:], b4(r_m2), ALU.is_equal))
                ch.dep()

            first = (T2 + U_EXP) // SLOTS
            for j in range(2):
                refill_lo(first, j)
            dve.wait_ge(rt_done, 1)
            ch.mark(v.tensor_copy(r_log[:], bank[5][:, 0:NT * NR].rearrange("p (c n) -> p c n", c=NT)))
            ch.dep()
            first_max(r_log[:, :, 0:NG], r_max, r_oh[:])
            v.tensor_tensor(r_e[:], r_log[:, :, 0:NG], b4(r_max), ALU.subtract).then_inc(r_sub, 1)
            by_group = r_log[:, :, NG:NR].rearrange("p c (g e) -> p c g e", g=NG)
            pro = r_pro[:].rearrange("p c (g e) -> p c g e", g=NG)
            for c in range(NT):
                ch.mark(v.tensor_tensor(pro[:, c], by_group[:, c], r_oh[:, c, :].unsqueeze(2).to_broadcast([P, NG, 4]), ALU.mult))
            ch.dep()
            ch.mark(v.tensor_reduce(r_sel[:], r_pro[:].rearrange("p c (g e) -> p c e g", g=NG), AX_X, ALU.add))
            ch.dep()
            first_max(r_sel[:], r_l1, r_o1[:])
            ch.mark(v.scalar_tensor_tensor(r_s2[:], r_o1[:], NEG, r_sel[:], ALU.mult, ALU.add))
            ch.dep()
            first_max(r_s2[:], r_l2, r_o2[:])
            v.tensor_tensor(r_d, r_l2, r_l1, ALU.subtract).then_inc(r_sub, 1)
            refill_lo(first, 2)
            dve.wait_ge(r_exp, 1)
            ch.mark(v.tensor_reduce(r_sum, r_e[:], AX_X, ALU.add))
            ch.dep()
            ch.mark(v.reciprocal(r_pg, r_sum))
            dve.wait_ge(r_exp, 2)
            ch.mark(v.tensor_scalar(r_u, r_e2, 1.0, None, ALU.add))
            ch.dep()
            ch.mark(v.reciprocal(r_w1, r_u))
            ch.dep()
            ch.mark(v.tensor_tensor(r_w1, r_w1, r_pg, ALU.mult))
            ch.dep()
            ch.mark(v.tensor_tensor(r_w2, r_w1, r_e2, ALU.mult))
            ch.dep()
            ch.mark(v.tensor_tensor(r_t1[:], r_o1[:], b4(r_w1), ALU.mult))
            ch.mark(v.tensor_tensor(r_t2[:], r_o2[:], b4(r_w2), ALU.mult))
            ch.dep()
            ch.mark(v.tensor_tensor(r_t1[:], r_t1[:], r_t2[:], ALU.add))
            ch.dep()
            gates = r_gate[:].rearrange("p c (g e) -> p c g e", g=NG)
            for c in range(NT):
                ins = v.tensor_tensor(gates[:, c], r_oh[:, c, :].unsqueeze(2).to_broadcast([P, NG, 4]),
                                      r_t1[:, c, :].unsqueeze(1).to_broadcast([P, NG, 4]), ALU.mult)
            ins.then_inc(gates_ready, 1)
            refill_lo(first, 3)
            dve.wait_ge(gbc_ready, NE // 2)

            def expert_gate(r, at, e, j):
                dve.wait_ge(tile_done, r * SLOTS + at + 2 + j + 1)
                dve.wait_ge(ex_hid, 2 * e + j + 1)
                v.tensor_tensor(e_up[:, j, :], bank[2 + j][:, 0:S], gate_bc[:, bass.ds(e * S, S)],
                                ALU.mult).then_inc(ex_up, 1)

            def expert_hi(e):
                for j in range(2):
                    dve.wait_ge(ex_act, 2 * e + j + 1)
                    dve.wait_ge(ex_up, 2 * e + j + 1)
                    v.tensor_tensor(hid_hi[:, j, :], e_act[:, j, :], e_up[:, j, :], ALU.mult).then_inc(ex_hi, 1)

            def expert_add(r, at, j):
                dve.wait_ge(tile_done, r * SLOTS + at + j + 1)
                for b in range(2 * j, 2 * j + 2):
                    v.tensor_tensor(x[:, 2 * b:2 * b + 2, :], x[:, 2 * b:2 * b + 2, :],
                                    bank[4 + b][:, :].rearrange("p (j s) -> p j s", j=2), ALU.add).then_inc(ex_add, 1)

            def expert(e, refills):
                r = e * (RING // SLOTS) + first
                for j in range(RING):
                    if 2 <= j < 4:
                        expert_gate(r, 4, e + 1, j - 2)
                    if j == RING - 1:
                        dve.wait_ge(tile_done, r * SLOTS + 4 + RING)
                        expert_hi(e + 1)
                    if j >= 4:
                        expert_add(r, 8, j - 4)
                    if j < refills:
                        refill_lo(r, 4 + j)

            for j in range(2):
                expert_gate(first, 0, 0, j)
            expert_hi(0)
            with dve.Fori(0, NE - 2) as e:
                expert(e, RING)
            expert(NE - 2, RING - 1)
            for j in range(2):
                expert_add(first + (NE - 1) * (RING // SLOTS), 4, j)

        def second_pool(pool, pre_sums):
            pre_sums(NORM2)
            pool.wait_ge(x_ready, DEPTH * 16 + 8)
            ch = Chain(pool, pool_chain, DEPTH * POOL_LINKS)
            pl.memset(c_z[:, :, 0:CW - 1], 0.0).then_inc(zeroed, 1)
            pl.memset(g_ki[:], 0.0).then_inc(zeroed, 1)
            ch.mark(pl.memset(g_pr[:], 0.0))
            pl.memset(g_st[:], 0.0).then_inc(zeroed, 1)

            def taps(first, end):
                for w in range(first, end):
                    if w == 0:
                        pool.wait_ge(packb_in, 16)
                        pool.wait_ge(cz_ready, 2)
                    else:
                        ch.dep()
                    ch.mark(pl.tensor_tensor(c_tap, c_z[:, 1, w:w + S], pb_("convw", CW + w).to_broadcast([P, S]), ALU.mult))
                    ch.dep()
                    other = c_y[:, 1, :] if w else pb_("convb", 1).to_broadcast([P, S])
                    ins = pl.tensor_tensor(c_y[:, 1, :], c_tap, other, ALU.add)
                    if w == POOL_TAPS[-1] - 1:
                        ins.then_inc(taps_done, 1)
                    else:
                        ch.mark(ins)

            def pairs(other, op):
                for r in range(GB):
                    pr = g_pr[:, r, :].rearrange("p (b j) -> p b j", j=GB)[:, :, 0:r + 1]
                    ins = op(pr, r, other[:].rearrange("p (b j) -> p b j", j=GB)[:, :, 0:r + 1])
                return ins

            def decay(pr, r, b_j):
                b_i = g_b[:].rearrange("p (b r) -> p b r", r=GB)[:, :, r].unsqueeze(2).to_broadcast([P, NGB, r + 1])
                return pl.tensor_tensor(pr, b_i, b_j, ALU.subtract)

            taps(0, POOL_TAPS[0])
            pool.wait_ge(gc_ready, 1)
            pairs(g_b, decay).then_inc(pr_sub, 1)
            taps(POOL_TAPS[0], POOL_TAPS[1])
            pool.wait_ge(pr_q, 1)
            pairs(g_k, lambda pr, r, k_j: pl.tensor_tensor(pr, pr, k_j, ALU.mult)).then_inc(pr_ready, 1)
            taps(POOL_TAPS[1], POOL_TAPS[2])
            pool.wait_ge(x_added, KD)
            for j in range(EX_CREDITS):
                pl.memset(credit[:, j:j + 1], 0.0).then_inc(ex_hid, 1)
            for j in range(4):
                pl.memset(credit[:, 2 + j:3 + j], 0.0).then_inc(ex_add, 1)

            def expert(e):
                for j in range(2):
                    pool.wait_ge(ex_act, 2 * e + j + 1)
                    pool.wait_ge(ex_up, 2 * e + j + 1)
                    pool.wait_ge(ex_hid, 2 * e + j + 1)
                    pl.tensor_tensor(e_prod[:, j, :], e_act[:, j, :], e_up[:, j, :], ALU.mult).then_inc(ex_prod, 1)
                for j in range(2):
                    pool.wait_ge(ex_prod, 2 * e + j + 1)
                    pool.wait_ge(ex_hi, 2 * e + j + 1)
                    pl.tensor_tensor(hid_lo[:, j, :], e_prod[:, j, :], hid_hi[:, j, :].bitcast(F32),
                                     ALU.subtract).then_inc(ex_hid, 1)

            with pool.Fori(0, NE) as e:
                expert(e)

        block = ctx.enter_context(nc.Block())

        @block.sync
        def _(sp):
            sp.dma_start(cst[:, 0:C_FIRST], consts[:, 0:C_FIRST]).then_inc(consts_in, 16)
            for s in range(SLOTS):
                sp.dma_start(ring[:, s, :], wtiles[s]).then_inc(w_in[s], 16)
            sp.dma_start(x[:], xt).then_inc(x_in, 16)
            sp.dma_start(cst[:, C_FIRST:], consts[:, C_FIRST:]).then_inc(masks_in, 16)
            sp.dma_start(pb[:], packb).then_inc(packb_in, 16)
            for n in range(SLOTS, RING):
                sp.wait_ge(lo_ready, n - SLOTS + 1)
                sp.dma_start(ring[:, n % SLOTS, :], wtiles[n]).then_inc(w_in[n % SLOTS], 16)
            with sp.Fori(1, ALL_TILES // RING) as r:
                for s in range(RING):
                    sp.wait_ge(lo_ready, r * RING + s - SLOTS + 1)
                    sp.dma_start(ring[:, s % SLOTS, :], wtiles[bass.ds(r * RING + s, 1)].rearrange("o p n -> (o p) n")
                                 ).then_inc(w_in[s % SLOTS], 16)
            for j in range(2):
                half = slice(j * KD // 2, (j + 1) * KD // 2)
                sp.wait_ge(ex_add, 4 * NE + 2 * j + 2)
                sp.dma_start(out[:, half, :], x[:, half, :]).then_inc(out_done, 16)
            sp.wait_ge(out_done, 32)

        @block.tensor
        def _(pe):
            def tile_in(n):
                pe.wait_ge(lo_ready, n + 1)

            def product(out_, w_part, x_parts, first, last):
                (wh, wl), (xh, xl) = w_part, x_parts
                t.matmul(out_, wh, xh, start=first, stop=False)
                t.matmul(out_, wh, xl, start=False, stop=False)
                return t.matmul(out_, wl, xh, start=False, stop=last)

            def wblock(s, k):
                return w_hi[:, s, k * P:(k + 1) * P], w_lo[:, s, k * P:(k + 1) * P]

            def project(n, s, out_):
                tile_in(n)
                for k in range(KD):
                    mm = product(out_, wblock(s, k), (act_hi[:, k, :], act_lo[:, k, :]), k == 0, k == KD - 1)
                mm.then_inc(tile_done, 1)

            def project_two(n, s, ready):
                for j in range(2):
                    tile_in(n + j)
                for k in range(KD):
                    pe.wait_ge(ready[0], ready[1] + k + 1)
                    for j in range(2):
                        mm = product(bank[j][:, 0:S], wblock((s + j) % SLOTS, k), (act_hi[:, k, :], act_lo[:, k, :]),
                                     k == 0, k == KD - 1)
                        if k == KD - 1:
                            mm.then_inc(tile_done, 1)

            def project_tokens(n, s, half, banks):
                tile_in(n)
                for c in range(NT):
                    here = slice(c * P, (c + 1) * P)
                    for i in range(KD // 2):
                        k, both = half * (KD // 2) + i, slice(i * S, (i + 1) * S)
                        mm = product(banks[c][:, 0:S], (act_hi[:, k, here], act_lo[:, k, here]),
                                     (w_hi[:, s, both], w_lo[:, s, both]), k == 0, k == KD - 1)
                mm.then_inc(tile_done, 1)

            def lengths(out_, x_part, select, first=True, last=True):
                n = select.shape[1]
                for c in range(NT):
                    mm = t.matmul(out_[:, c * n:(c + 1) * n], x_part[:, c * P:(c + 1) * P], select,
                                  start=first and c == 0, stop=last and c == NT - 1)
                return mm

            def spread(out_, by_token, n=1):
                w = P // n
                for c in range(NT):
                    for i in range(n):
                        mm = t.matmul(out_[i * w:(i + 1) * w, c * P:(c + 1) * P],
                                      by_token[:, c * n + i:c * n + i + 1].to_broadcast([P, w]), ident, start=True, stop=True)
                return mm

            def keep_warm(n):
                for _ in range(n):
                    t.matmul(bank[3][:, 0:P], ident, ones, start=True, stop=True)

            def norm_sums(i, g):
                pe.wait_ge(norm_sq, i * (KD // 2) + g + 1)
                for k in range(2 * g, 2 * g + 2):
                    mm = lengths(bank[0], sq[:, k, :], ones[:, 0:1], k == 0, k == KD - 1)
                if g == KD // 2 - 1:
                    mm.then_inc(norm_sum, 1)

            def norm_rows(i, warm):
                pe.wait_ge(norm_inv, i + 1)
                spread(bank[7], rrms).then_inc(norm_row, 1)
                keep_warm(warm)

            def row_norm(i, pre):
                for g in range(KD // 2):
                    pe.wait_ge(norm_pair, pre * (KD // 2) + g + 1)
                    mm = lengths(bank[0], sq[:, 2 * g, :], ones[:, 0:1], g == 0, g == KD // 2 - 1)
                    if g < KD // 2 - 1:
                        keep_warm(2)
                mm.then_inc(norm_sum, 1)
                keep_warm(1)
                norm_rows(i, 4)

            def transpose(out_, in_):
                return t.transpose(out_, in_, ident)

            def scores(i, q, k, b):
                lo, j = 64 * (i % 2), i // 2
                t.matmul(b[:, 0:P], q[lo:lo + 64, j, 0:P], k[lo:lo + 64, j, 0:P], start=True, stop=True)
                return t.matmul(b[:, P:3 * P], q[lo:lo + 64, j, P:S], k[lo:lo + 64, j, :], start=True, stop=True)

            pe.wait_ge(consts_in, 16)
            keep_warm(36)

            def layer(l):
                row_norm(l * 4, 2 * l)
                pe.wait_ge(packa_in, l * 16 + 16)
                for n in range(T_WOUT):
                    if 4 <= n < T_Z + 4:
                        pe.wait_ge(conv_ready, l * 12 + n - 3)
                    elif n >= T_Z + 4:
                        pe.wait_ge(proj_evac, l * 16 + (n if n < T_BV else n | 1) - T_Z - 3)
                    if n == 0:
                        project_two(l * LAYER_TILES, 0, (h_lo, l * 16))
                    elif n == 1:
                        pass
                    elif n < T_BV:
                        project(l * LAYER_TILES + n, n % SLOTS, bank[n % 4][:, 0:S])
                    else:
                        project_tokens(l * LAYER_TILES + n, n % SLOTS, n % 2, [bank[n // 2 * 2 % 4 + c] for c in range(NT)])
                    if n == T_Z - 1:
                        for k in range(KD):
                            mm = t.matmul(bank[4][0:64, S:2 * S], pa_("wba", k * 64, 64), h[:, k, :],
                                          start=k == 0, stop=k == KD - 1)
                        mm.then_inc(ba_done, 1)
                    if T_Z <= n < T_BQ:
                        for i in range(2 * (n - T_Z), 2 * (n - T_Z) + 2):
                            pe.wait_ge(sqk_ready, l * 8 + i + 1)
                            mm = lengths(bank[6][:, 2 * i:2 * i + 2], sqk[:, i, :], ones[:, 0:1])
                        if n == T_BQ - 1:
                            mm.then_inc(l2_sum, 1)
                    if n in L2_STEPS:
                        pe.wait_ge(l2_inv, l + 1)
                        for g in range(2 * L2_STEPS.index(n), 2 * L2_STEPS.index(n) + 2):
                            if g >= 2:
                                pe.wait_ge(qk_ready, l * 4 + g - 1)
                            for i in range(2 * g, 2 * g + 2):
                                mm = spread(bank[6 + g % 2][:, i % 2 * S:i % 2 * S + S], l2_rrms[:, 2 * i:2 * i + 2])
                            mm.then_inc(l2_row, 1)
                    if n == T_BQ:
                        pe.wait_ge(masks_in, 16)
                    if T_BQ + 2 <= n < T_BQ + 10:
                        j = n - T_BQ - 2
                        pe.wait_ge(proj_evac, l * 16 + 4 + j + 1)
                        if j >= 2:
                            pe.wait_ge(rope_used, l * 8 + j - 1)
                        t.matmul(bank[4 + j % 2][:, 0:S], cc("rot"), raw[:, j, :],
                                 start=True, stop=True).then_inc(rope_rot, 1)

                pe.wait_ge(rows_ready, l + 1)
                pe.wait_ge(rope_used, l * 8 + 8)
                for c in range(NT):
                    mm = t.matmul(bank[4][:, S + 64 * c:S + 64 * c + 64], rows[0:64, c * P:(c + 1) * P],
                                  ident[0:64, 0:64], start=True, stop=True)
                mm.then_inc(cols_done, 1)
                pe.wait_ge(proj_evac, l * 16 + 16)
                pe.wait_ge(qk_ready, l * 4 + 4)
                for i in range(DNH):
                    if i >= 2:
                        pe.wait_ge(bc_act, l * 4 + i - 1)
                        pe.wait_ge(bc_dve, l * 4 + i - 1)
                    t.matmul(bank[i % 2][:, 0:S], ident[0:64, 32 + i:33 + i].to_broadcast([64, P]), rows[0:64, :],
                             start=True, stop=True)
                    t.matmul(bank[i % 2][:, S:2 * S], ident[0:64, i:i + 1].to_broadcast([64, P]), rows[0:64, :],
                             start=True, stop=True).then_inc(bc_done, 1)
                    if i >= 2:
                        pe.wait_ge(tr_dve, l * 4 + i - 1)
                        pe.wait_ge(tr_act, l * 4 + i - 1)
                    pe.wait_ge(silu_ready, l * 12 + 8 + i + 1)
                    transpose(bank[6 + i % 2][:, 0:P], qkvs[:, 8 + i, 0:P])
                    transpose(bank[6 + i % 2][:, P:2 * P], qkvs[:, 8 + i, P:S])
                    transpose(bank[6 + i % 2][:, 2 * P:3 * P], qkn[:, 4 + i, 0:P]).then_inc(tr_done, 1)
                    if i >= 2:
                        pe.wait_ge(gram_used, l * 4 + i - 1)
                    for c in range(NT):
                        keys = qkn[:, 4 + i, c * P:(c + 1) * P]
                        t.matmul(bank[2 + i % 2][:, c * S:c * S + P], keys, keys, start=True, stop=True)
                        mm = t.matmul(bank[2 + i % 2][:, c * S + P:c * S + 2 * P], keys, qkn[:, i, c * P:(c + 1) * P],
                                      start=True, stop=True)
                    mm.then_inc(gram_done, 1)

                def attend(i):
                    if i == 0:
                        pe.wait_ge(rope_done, l * 8 + 8)
                        pe.wait_ge(gram_used, l * 4 + 4)
                    if i < SWAH:
                        if i >= 2:
                            pe.wait_ge(att_sm, l * 8 + i - 1)
                        scores(i, raw[:, 0:4, :], raw[:, 4:8, :], bank[2 + i % 2]).then_inc(att_s, 1)
                    j = i - 2
                    if 0 <= j < SWAH:
                        pe.wait_ge(att_pn, l * 8 + j + 1)
                        if j >= 1:
                            pe.wait_ge(att_pt, l * 8 + j)
                        transpose(bank[4][:, 0:P], prob[:, j, 0:P])
                        transpose(bank[4][:, P:2 * P], prob[:, j, P:2 * P])
                        transpose(bank[4][:, 2 * P:3 * P], prob[:, j, 2 * P:3 * P]).then_inc(att_t, 1)
                    j = i - 3
                    if 0 <= j < SWAH:
                        pe.wait_ge(att_pt, l * 8 + j + 1)
                        if j >= 2 and j % 2 == 0:
                            pe.wait_ge(att_o, l * 8 + j)
                        o_ = bank[5][64 * (j % 2):64 * (j % 2) + 64, :]
                        vals = vtok[:, :, j * 64:(j + 1) * 64]
                        t.matmul(o_[:, 0:P], vals[:, 0, :], pt[:, j % 2, 0:P], start=True, stop=True)
                        t.matmul(o_[:, P:S], vals[:, 0, :], pt[:, j % 2, P:2 * P], start=True, stop=False)
                        t.matmul(o_[:, P:S], vals[:, 1, :], pt[:, j % 2, 2 * P:3 * P], start=False,
                                 stop=True).then_inc(att_pv, 1)

                pe.wait_ge(bc_act, l * 4 + 4)
                pe.wait_ge(bc_dve, l * 4 + 4)
                for g in range(2):
                    pe.wait_ge(bl_ready, l * (LEVELS + 1) + g + 1)
                    for u in range(4):
                        mm = t.matmul(bank[g][:, u * P:(u + 1) * P], bl[:, 0, 4 * g + u, :], ident, start=True, stop=True)
                    mm.then_inc(lev_x, 1)
                pe.wait_ge(tr_dve, l * 4 + 4)
                pe.wait_ge(tr_act, l * 4 + 4)
                for lev in range(1, LEVELS):
                    pe.wait_ge(bl_ready, l * (LEVELS + 1) + lev + 2)
                    for g in range(2):
                        pe.wait_ge(tu_ready, l * 2 * LEVELS + 2 * (lev - 1) + g + 1)
                        for u in range(4 * g, 4 * g + 4):
                            mm = t.matmul(bank[6 + g][:, u % 4 * P:u % 4 * P + P], bl[:, lev % 2, u, :], tinv[:, u, :],
                                          start=True, stop=True)
                        mm.then_inc(lev_x, 1)
                    attend(lev - 1)
                    for g in range(2):
                        pe.wait_ge(lev_xs, l * 2 * (LEVELS - 1) + 2 * (lev - 1) + g + 1)
                        for u in range(4 * g, 4 * g + 4):
                            if lev < LEVELS - 1:
                                t.matmul(bank[g][:, u % 4 * P:u % 4 * P + P], uinv[:, u, :], xs[:, u, :],
                                         start=True, stop=True)
                            mm = t.matmul(bank[6 + g][:, u % 4 * P:u % 4 * P + P], xs[:, u, :], uinv[:, u, :],
                                          start=True, stop=True)
                        mm.then_inc(lev_y, 1)

                attend(LEVELS - 1)
                pe.wait_ge(tu_ready, l * 2 * LEVELS + 2 * LEVELS)
                for i in range(DNH):
                    mm = t.matmul(bank[6][:, i * P:(i + 1) * P], uinv[:, 2 * i, :], vb[:, 2 * i, :], start=True, stop=True)
                mm.then_inc(rec_pe, 1)
                attend(LEVELS)
                pe.wait_ge(rec_act, l * 7 + 1)
                for i in range(DNH):
                    mm = t.matmul(bank[7][:, i * P:(i + 1) * P], kd[:, i, :], vnew[:, 0, i, :], start=True, stop=True)
                mm.then_inc(rec_pe, 1)
                for i in range(DNH):
                    mm = t.matmul(bank[0][:, i * P:(i + 1) * P], vnew[:, 0, i, :], qkt[:, 2 * i, :], start=True, stop=True)
                mm.then_inc(rec_pe, 1)
                attend(LEVELS + 1)
                pe.wait_ge(rec_act, l * 7 + 2)
                pe.wait_ge(kbg_ready, l * 4 + 4)
                for i in range(DNH):
                    mm = t.matmul(bank[6][:, i * P:(i + 1) * P], kbg[:, i, :], st1[:, i, :], start=True, stop=True)
                mm.then_inc(rec_pe, 1)
                attend(LEVELS + 2)
                pe.wait_ge(rec_dve, l + 1)
                for i in range(DNH):
                    mm = t.matmul(bank[7][:, i * P:(i + 1) * P], uinv[:, 2 * i + 1, :], resid[:, i, :], start=True, stop=True)
                mm.then_inc(rec_pe, 1)
                attend(LEVELS + 3)
                pe.wait_ge(rec_act, l * 7 + 5)
                for i in range(DNH):
                    t.matmul(bank[6][:, i * P:(i + 1) * P], st1[:, i, :], qg[:, i, :], start=True, stop=False)
                    mm = t.matmul(bank[6][:, i * P:(i + 1) * P], vnew[:, 1, i, :], qkt[:, 2 * i + 1, :],
                                  start=False, stop=True)
                mm.then_inc(rec_pe, 1)
                def head_lengths(c):
                    for i in range(DNH):
                        mm = t.matmul(bank[1][:, NT * i + c:NT * i + c + 1], sq[:, i, c * P:(c + 1) * P], ones[:, 0:1],
                                      start=True, stop=True)
                    return mm

                def out_part(m, part):
                    n = T_WOUT + m
                    if part == 0:
                        tile_in(l * LAYER_TILES + n)
                    for i in range(part * DNH, part * DNH + DNH):
                        k = MIX_ORDER[i]
                        if m == 0:
                            pe.wait_ge(mix_lo, l * KD + i + 1)
                        mm = product(bank[4 + m // 2][:, m % 2 * S:m % 2 * S + S], wblock(n % SLOTS, k),
                                     (act_hi[:, k, :], act_lo[:, k, :]), m % 2 == 0 and i == 0,
                                     m % 2 == 1 and i == KD - 1)
                    if part:
                        mm.then_inc(tile_done, 1)

                head_lengths(0)
                out_part(0, 0)
                pe.wait_ge(rec_act, l * 7 + 7)
                head_lengths(1).then_inc(on_sum, 1)
                out_part(1, 0)
                pe.wait_ge(on_inv, l + 1)
                for i in range(DNH):
                    spread(bank[i // 2][:, i % 2 * S:i % 2 * S + S], on_rrms[:, NT * i:NT * i + NT]).then_inc(on_row, 1)
                out_part(2, 0)
                for m in range(KD):
                    if m >= SLOTS:
                        out_part(m, 0)
                    out_part(m, 1)
                    if m % 2 and m >= 3:
                        norm_sums(l * 4 + 1, m // 2 - 1)
                norm_sums(l * 4 + 1, KD // 2 - 1)
                norm_rows(l * 4 + 1, 10)

                row_norm(l * 4 + 2, 2 * l + 1)

                def step(r, k, p, q, up=True, down=True, start=False, stop=False):
                    if up:
                        pe.wait_ge(ffn_free, l * NP_FF + p + 1)
                        for w in range(2):
                            project(r * SLOTS + (k + w), (k + w) % SLOTS, bank[2 * q + w][:, 0:S])
                        k = k + 2
                    if down:
                        tile_in(r * SLOTS + k)
                        pe.wait_ge(hid_done, l * NP_FF + p + 1)
                        for m in range(KD):
                            mm = product(bank[4 + m // 2][:, m % 2 * S:m % 2 * S + S], wblock(k % SLOTS, m),
                                         (hid_hi[:, q, :], hid_lo[:, q, :]), start and m % 2 == 0,
                                         stop and m % 2 == 1)
                            if stop and m % 2 == 1 and m < KD - 1:
                                mm.then_inc(down_done, 1)
                            if stop and m % 2 == 1 and m >= 5:
                                if m == KD - 1:
                                    mm.then_inc(tile_done, 1)
                                norm_sums(l * 4 + 3, m // 2 - 2)
                        if not stop:
                            mm.then_inc(tile_done, 1)

                r0 = l * (LAYER_TILES // SLOTS) + T_UP // SLOTS
                pe.wait_ge(ffn_free, l * NP_FF + 1)
                project_two(r0 * SLOTS, 0, (h_lo, l * 16 + 8))
                for p in range(1, DOWN_LAG):
                    step(r0, 2 * p, p, p % PAIRS, down=False)
                for p in range(DOWN_LAG, PEEL):
                    step(r0 + (p - 1), 1, p, p % PAIRS, start=p == DOWN_LAG)
                with pe.Fori(0, GLU_LOOPS) as i:
                    for q in range(PAIRS):
                        step(r0 + i * PAIRS + (q + PEEL - 1), 1, i * PAIRS + (q + PEEL), q)
                for p in range(NP_FF, NP_FF + DOWN_LAG):
                    step(r0 + (NP_FF - 1), 1 + p - NP_FF, p, p % PAIRS, up=False, stop=p == NP_FF + DOWN_LAG - 1)
                for g in range(KD // 2 - 2, KD // 2):
                    norm_sums(l * 4 + 3, g)
                norm_rows(l * 4 + 3, 10)

            with pe.Fori(0, DEPTH) as l:
                layer(l)
            second_tensor(pe, tile_in, product, wblock, project, project_two, project_tokens, lengths, spread, norm_sums, norm_rows, row_norm, transpose, scores)

        @block.scalar
        def _(act):
            def make_hi(n, s, loads):
                act.wait_ge(w_in[s], loads * 16)
                a.activation(w_hi[:, s, :], ring[:, s, :], ACT.Copy).then_inc(hi_ready, 1)

            def refill_hi(r, k):
                act.wait_ge(tile_done, r * SLOTS + k + 1)
                make_hi(r * SLOTS + k + SLOTS, k % SLOTS, r + (k // SLOTS + 2))

            def norm_root(i):
                act.wait_ge(norm_sum, i + 1)
                a.activation(rms[:], bank[0][:, 0:NT], ACT.Sqrt, bias=eps, scale=1.0 / D).then_inc(norm_std, 1)

            def pre_square(k, x_parts, first):
                act.wait_ge(x_parts, first + k + 2)
                a.activation(sq[:, k:k + 2, :], x[:, k:k + 2, :], ACT.Square).then_inc(norm_sq, 1)

            def pre_hi(at):
                for k in range(KD):
                    act.wait_ge(h_ready, at + k + 1)
                    a.activation(act_hi[:, k, :], h[:, k, :], ACT.Copy).then_inc(h_hi, 1)

            def pre_norm(i, x_parts, first, at):
                for k in range(0, KD, 2):
                    pre_square(k, x_parts, first)
                norm_root(i)
                pre_hi(at)

            def post_square(g):
                a.activation(sq[:, 2 * g:2 * g + 2, :], bank[4 + g][:, :].rearrange("p (k s) -> p k s", k=2),
                             ACT.Square).then_inc(norm_sq, 1)

            def softplus(step, l, src, bias, scale, sp, lo, hi):
                if step == 0:
                    a.activation(sp[lo:hi, 0, :], src, ACT.Identity, bias=bias, scale=scale).then_inc(sp_act, 1)
                elif step == 1:
                    act.wait_ge(sp_dve, l * 2 + 1)
                    a.activation(sp[lo:hi, 2, :], sp[lo:hi, 1, :], ACT.Exp, scale=-1.0).then_inc(sp_act, 1)
                else:
                    act.wait_ge(sp_dve, l * 2 + 2)
                    a.activation(sp[lo:hi, 4, :], sp[lo:hi, 3, :], ACT.Ln).then_inc(sp_act, 1)

            act.wait_ge(consts_in, 16)
            for n in range(SLOTS):
                make_hi(n, n, 1)

            def layer(l):
                def refill(n):
                    refill_hi(l * (LAYER_TILES // SLOTS), n)

                pre_norm(l * 4, x_ready, l * 16, l * 16)
                act.wait_ge(packa_in, l * 16 + 16)

                def silu(n):
                    act.wait_ge(conv_ready, l * 12 + n + 1)
                    a.activation(qkvs[:, n, :], qkvc[:, n, :], ACT.Silu).then_inc(silu_ready, 1)
                    if n < 8:
                        act.wait_ge(silu_ready, l * 12 + n + 1)
                        a.activation(sqk[:, n, :], qkvs[:, n, :], ACT.Square).then_inc(sqk_ready, 1)

                for n in range(T_Z):
                    act.wait_ge(tile_done, l * LAYER_TILES + n + 1)
                    a.activation(qkvc[:, n, :], bank[n % 4][:, 0:S], ACT.Copy,
                                 scale=pa_("conv", n * CONV + CONV - 1)).then_inc(conv_first, 1)
                    refill(n)
                    if n >= 1:
                        silu(n - 1)
                for n in range(T_Z, T_WOUT):
                    act.wait_ge(tile_done, l * LAYER_TILES + n + 1)
                    src = bank[n % 4]
                    if n < T_BQ:
                        for z in {T_Z: (0,), T_BQ - 1: (1, 2, 3)}.get(n, ()):
                            a.activation(zs[:, z, :], bank[(T_Z + z) % 4][:, 0:S], ACT.Silu).then_inc(proj_evac, 1)
                    elif n < T_BV:
                        a.activation(raw[:, n - T_BQ, :], src[:, 0:S], ACT.Copy).then_inc(proj_evac, 1)
                    elif n % 2:
                        j = (n - T_BV) // 2
                        for c in range(NT):
                            a.activation(vtok[:, c, j * S:(j + 1) * S], bank[(n - 1 + c) % 4][:, 0:S],
                                         ACT.Copy).then_inc(proj_evac, 1)
                    if n == T_Z:
                        silu(T_Z - 1)
                        act.wait_ge(ba_done, l + 1)
                        softplus(0, l, bank[4][32:36, S:2 * S], pa_("dt", rows_=slice(32, 36)), 1.0, spt, 32, 36)
                    refill(n)
                    if n == T_Z:
                        a.activation(cols[32:36, 1, 0:1], pa_("alog", rows_=slice(32, 36)), ACT.Exp).then_inc(decay_ready, 1)
                    if T_Z <= n < T_Z + 2:
                        softplus(n - T_Z + 1, l, None, None, None, spt, 32, 36)
                    if n == T_Z + 2:
                        act.wait_ge(zeroed, 1)
                        a.activation(rows[0:4, :], bank[4][0:4, S:2 * S], ACT.Sigmoid).then_inc(beta_ready, 1)
                    if n == T_BQ + 2:
                        act.wait_ge(l2_sum, l + 1)
                        a.activation(l2_rms[:], bank[6][:, 0:2 * DNH * NT], ACT.Sqrt, bias=eps).then_inc(l2_std, 1)

                for i in range(DNH + 1):
                    if i < DNH:
                        act.wait_ge(bc_done, l * 4 + i + 1)
                        a.activation(eg1[:, i, :], bank[i % 2][:, P:S], ACT.Exp)
                        a.activation(bbc[:, i, :], bank[i % 2][:, S:2 * S], ACT.Copy).then_inc(bc_act, 1)
                    i -= 1
                    if i < 0:
                        continue
                    act.wait_ge(bc_dve, l * 4 + i + 1)
                    a.activation(gam[:, i, :], gam[:, i, :], ACT.Exp).then_inc(gam_ready, 1)
                    act.wait_ge(tr_dve, l * 4 + i + 1)
                    act.wait_ge(gam_ready, l * 4 + i + 1)
                    a.activation(kd[:, i, :], bank[6 + i % 2][:, 2 * P:3 * P], ACT.Copy,
                                 scale=gam[:, i, P - 1:P]).then_inc(tr_act, 1)

                def attend(i):
                    if i < SWAH:
                        act.wait_ge(att_sm, l * 8 + i + 1)
                        a.activation(prob[:, i, 0:P], prob[:, i, 0:P], ACT.Exp, bias=att_max[:, 2 * i:2 * i + 1],
                                     accum_out=att_z[:, 2 * i:2 * i + 1])
                        a.activation(prob[:, i, P:3 * P], prob[:, i, P:3 * P], ACT.Exp,
                                     bias=att_max[:, 2 * i + 1:2 * i + 2],
                                     accum_out=att_z[:, 2 * i + 1:2 * i + 2]).then_inc(att_p, 1)
                    j = i - 2
                    if 0 <= j < SWAH:
                        act.wait_ge(att_t, l * 8 + j + 1)
                        if j >= 2:
                            act.wait_ge(att_pv, l * 8 + j - 1)
                        a.activation(pt[:, j % 2, :], bank[4][:, 0:3 * P], ACT.Copy).then_inc(att_pt, 1)
                    j = i - 3
                    if j % 2 == 1 and 0 <= j < SWAH:
                        act.wait_ge(att_pv, l * 8 + j + 1)
                        a.activation(mix[:, 4 + j // 2, :], bank[5][:, 0:S], ACT.Copy).then_inc(att_o, 1)
                        a.activation(act_hi[:, 4 + j // 2, :], bank[5][:, 0:S], ACT.Copy).then_inc(att_o, 1)

                for lev in range(1, LEVELS):
                    for g in range(2):
                        act.wait_ge(lev_x, l * 2 * LEVELS + 2 * lev + g + 1)
                        a.activation(xs[:, 4 * g:4 * g + 4, :], bank[6 + g][:, :].rearrange("p (u k) -> p u k", u=4),
                                     ACT.Copy).then_inc(lev_xs, 1)
                    attend(lev - 1)

                def heads(b):
                    return b[:, :].rearrange("p (i k) -> p i k", i=DNH)

                attend(LEVELS - 1)
                act.wait_ge(rec_pe, l * 6 + 1)
                a.activation(vnew[:, 0], heads(bank[6]), ACT.Copy).then_inc(rec_act, 1)
                attend(LEVELS)
                act.wait_ge(rec_pe, l * 6 + 2)
                a.activation(st1[:], heads(bank[7]), ACT.Copy).then_inc(rec_act, 1)
                act.wait_ge(rec_pe, l * 6 + 3)
                a.activation(ot[:, :, 0:P], heads(bank[0]), ACT.Copy).then_inc(rec_act, 1)
                a.activation(sq[:, 0:4, 0:P], heads(bank[0]), ACT.Square).then_inc(rec_act, 1)
                attend(LEVELS + 1)
                attend(LEVELS + 2)
                act.wait_ge(rec_pe, l * 6 + 5)
                a.activation(vnew[:, 1], heads(bank[7]), ACT.Copy).then_inc(rec_act, 1)
                attend(LEVELS + 3)
                act.wait_ge(rec_pe, l * 6 + 6)
                a.activation(ot[:, :, P:S], heads(bank[6]), ACT.Copy).then_inc(rec_act, 1)
                a.activation(sq[:, 0:4, P:S], heads(bank[6]), ACT.Square).then_inc(rec_act, 1)
                act.wait_ge(on_sum, l + 1)
                a.activation(on_rms[:], bank[1][:, 0:DNH * NT], ACT.Sqrt, bias=eps, scale=1.0 / P).then_inc(on_std, 1)
                for k in range(DNH):
                    act.wait_ge(mix_ready, l * 4 + k + 1)
                    a.activation(act_hi[:, k, :], mix[:, k, :], ACT.Copy).then_inc(mix_hi, 1)

                for m in range(KD):
                    if m < KD - 1:
                        refill(T_WOUT + m)
                    else:
                        act.wait_ge(tile_done, l * LAYER_TILES + T_UP)
                    if m % 2:
                        post_square(m // 2)
                norm_root(l * 4 + 1)
                refill(T_UP - 1)
                pre_norm(l * 4 + 2, x_ready, l * 16 + 8, l * 16 + 8)
                act.wait_ge(packf_in, l * 16 + 16)

                def step(r, k, p, q, up=True, down=True):
                    if up:
                        act.wait_ge(gelu_done, l * NP_FF + p + 1)
                        act.wait_ge(hid_done, l * NP_FF + p + 1)
                        for w, dst in enumerate((glu_g, glu_v)):
                            act.wait_ge(tile_done, r * SLOTS + (k + w + 1))
                            a.activation(dst[:, q, :], bank[2 * q + w][:, 0:S], ACT.Identity,
                                         scale=pf_("conv", p * 6 + w * 3 + 2), bias=pf_("bias", p * 2 + w)).then_inc(glu_first, 1)
                            refill_hi(r, k + w)
                        act.wait_ge(glu_ready, l * NP_FF + p + 1)
                        a.activation(glu_a[:, q, :], glu_g[:, q, :], ACT.Gelu_apprx_tanh).then_inc(gelu_done, 1)
                        k = k + 2
                    if down:
                        refill_hi(r, k)

                r0 = l * (LAYER_TILES // SLOTS) + T_UP // SLOTS
                for p in range(DOWN_LAG):
                    step(r0, 2 * p, p, p % PAIRS, down=False)
                for p in range(DOWN_LAG, PEEL):
                    step(r0 + (p - 1), 1, p, p % PAIRS)
                with act.Fori(0, GLU_LOOPS) as i:
                    for q in range(PAIRS):
                        step(r0 + i * PAIRS + (q + PEEL - 1), 1, i * PAIRS + (q + PEEL), q)
                for p in range(NP_FF, NP_FF + DOWN_LAG - 1):
                    step(r0 + (NP_FF - 1), 1 + p - NP_FF, p, p % PAIRS, up=False)
                for g in range(KD // 2):
                    if g < KD // 2 - 1:
                        act.wait_ge(down_done, l * (KD // 2 - 1) + g + 1)
                    else:
                        act.wait_ge(tile_done, (l + 1) * LAYER_TILES)
                    post_square(g)
                norm_root(l * 4 + 3)
                refill_hi(r0 + (NP_FF - 1), DOWN_LAG)

            with act.Fori(0, DEPTH) as l:
                layer(l)
            second_scalar(act, pre_norm, pre_square, norm_root, pre_hi, softplus, refill_hi)

        @block.vector
        def _(dve):
            def make_lo(n, s):
                dve.wait_ge(hi_ready, n + 1)
                v.tensor_tensor(w_lo[:, s, :], ring[:, s, :], w_hi[:, s, :].bitcast(F32), ALU.subtract).then_inc(lo_ready, 1)

            def refill_lo(r, k):
                make_lo(r * SLOTS + k + SLOTS, k % SLOTS)

            def part_lo(k, src, hi, made, done):
                dve.wait_ge(hi, made)
                v.tensor_tensor(act_lo[:, k, :], src[:, k, :], act_hi[:, k, :].bitcast(F32), ALU.subtract).then_inc(done, 1)

            def invert(i):
                dve.wait_ge(norm_std, i + 1)
                v.reciprocal(rrms[:], rms[:]).then_inc(norm_inv, 1)
                dve.wait_ge(norm_row, i + 1)

            def norm_apply(i, gain, at):
                invert(i)
                for k in range(KD + 2):
                    if k < KD:
                        v.scalar_tensor_tensor(h[:, k, :], x[:, k, :], gain(k), bank[7][:, 0:S], ALU.mult,
                                               ALU.mult).then_inc(h_ready, 1)
                    if k >= 2:
                        part_lo(k - 2, h, h_hi, at + k - 1, h_lo)

            def result_gain(i, g, gain):
                dve.wait_ge(norm_sq, i * (KD // 2) + g + 1)
                for k in range(2 * g, 2 * g + 2):
                    ins = v.tensor_scalar(y[:, k, :], bank[4 + g][:, k % 2 * S:k % 2 * S + S], gain(k), None, ALU.mult)
                return ins

            def norm_add(ch, i):
                invert(i)
                ch.dep()
                rows_ = bank[7][:, 0:S].unsqueeze(1).to_broadcast([P, 2, S])
                for g in range(KD // 2 + 1):
                    if g < KD // 2:
                        two = slice(2 * g, 2 * g + 2)
                        ch.mark(v.tensor_tensor(y[:, two, :], y[:, two, :], rows_, ALU.mult))
                    if g >= 1:
                        if g < KD // 2:
                            ch.dep_before(1)
                        else:
                            ch.dep()
                        two = slice(2 * g - 2, 2 * g)
                        v.tensor_tensor(x[:, two, :], x[:, two, :], y[:, two, :], ALU.add).then_inc(x_ready, 2)

            def softplus(step, ch, l, sp, lo, hi):
                z, ab, e, u, ln, r = (sp[lo:hi, j, :] for j in range(6))
                if step == 0:
                    dve.wait_ge(sp_act, l * 3 + 1)
                    v.scalar_tensor_tensor(ab, z, -1.0, z, ALU.mult, ALU.max).then_inc(sp_dve, 1)
                elif step == 1:
                    dve.wait_ge(sp_act, l * 3 + 2)
                    v.tensor_scalar(u, e, 1.0, None, ALU.add).then_inc(sp_dve, 1)
                else:
                    dve.wait_ge(sp_dve, l * 2 + 2)
                    ch.mark(v.scalar_tensor_tensor(ab, u, -1.0, e, ALU.add, ALU.subtract))
                    ch.mark(v.reciprocal(r, u))
                    ch.dep()
                    ch.mark(v.tensor_tensor(ab, ab, r, ALU.mult))
                    ch.dep()
                    dve.wait_ge(sp_act, l * 3 + 3)
                    ch.mark(v.scalar_tensor_tensor(r, z, 0.0, ln, ALU.max, ALU.add))
                    ch.dep()
                    ch.mark(v.tensor_tensor(r, r, ab, ALU.subtract))
                    ch.dep()
                return r

            dve.wait_ge(x_in, 16)
            dve.wait_ge(consts_in, 16)
            for k in range(KD):
                v.memset(credit[:, 9 + k:10 + k], 0.0).then_inc(x_ready, 1)
            for n in range(SLOTS):
                make_lo(n, n)

            def layer(l):
                ch = Chain(dve, dve_chain, l * DVE_LINKS)

                def refill(n):
                    refill_lo(l * (LAYER_TILES // SLOTS), n)

                dve.wait_ge(packa_in, l * 16 + 16)
                norm_apply(l * 4, lambda k: pa_("pre", k), l * 16)

                for n in range(T_Z):
                    src, dst = bank[n % 4], qkvc[:, n, :]
                    dve.wait_ge(conv_first, l * 12 + n + 1)
                    for j in range(1, CONV):
                        if j > 1:
                            ch.dep()
                        ins = v.scalar_tensor_tensor(dst[:, j:], src[:, 0:S - j], pa_("conv", n * CONV + CONV - 1 - j),
                                                     dst[:, j:], ALU.mult, ALU.add)
                        if j < CONV - 1:
                            ch.mark(ins)
                    ins.then_inc(conv_ready, 1)
                    refill(n)

                def decays():
                    r = softplus(2, ch, l, spt, 32, 36)
                    dve.wait_ge(decay_ready, l + 1)
                    ch.mark(v.tensor_scalar(r, r, cols[32:36, 1, 0:1], -1.0, ALU.mult, ALU.mult))
                    ch.dep()
                    dve.wait_ge(beta_ready, l + 1)
                    dve.wait_ge(zeroed, 1)
                    for c in range(NT):
                        ins = v.tensor_tensor_scan(rows[32:36, c * P:(c + 1) * P], ones[32:36, :],
                                                   r[:, c * P:(c + 1) * P], 0.0, ALU.mult, ALU.add)
                    ins.then_inc(rows_ready, 1)

                def rotary(j):
                    if 0 <= j < 8:
                        dve.wait_ge(rope_rot, l * 8 + j + 1)
                        v.tensor_tensor(ropet[:, j, :], bank[4 + j % 2][:, 0:S], cc("sin"),
                                        ALU.mult).then_inc(rope_used, 1)
                    if 1 <= j < 9:
                        dve.wait_ge(rope_used, l * 8 + j)
                        dve.wait_ge(rope_cos, l * 8 + j)
                        v.tensor_tensor(raw[:, j - 1, :], raw[:, j - 1, :], ropet[:, j - 1, :],
                                        ALU.add).then_inc(rope_done, 1)

                for n in range(T_Z, T_WOUT):
                    if n == T_Z:
                        softplus(0, ch, l, spt, 32, 36)
                    if n == T_Z + 1:
                        softplus(1, ch, l, spt, 32, 36)
                    if n == T_Z + 3:
                        decays()
                    if n == T_BQ + 3:
                        dve.wait_ge(l2_std, l + 1)
                        v.reciprocal(l2_rrms[:], l2_rms[:]).then_inc(l2_inv, 1)
                    if n - 1 in L2_STEPS:
                        for g in range(2 * L2_STEPS.index(n - 1), 2 * L2_STEPS.index(n - 1) + 2):
                            dve.wait_ge(l2_row, l * 4 + g + 1)
                            dve.wait_ge(silu_ready, l * 12 + 2 * g + 2)
                            v.scalar_tensor_tensor(qkn[:, 2 * g:2 * g + 2, :], qkvs[:, 2 * g:2 * g + 2, :],
                                                   float(P) ** -0.5 if g < 2 else 1.0,
                                                   bank[6 + g % 2][:, :].rearrange("p (i s) -> p i s", i=2),
                                                   ALU.mult, ALU.mult).then_inc(qk_ready, 1)
                    if n == T_BQ + 3:
                        dve.wait_ge(masks_in, 16)
                    rotary(n - T_BQ - 3)
                    refill(n)

                dve.wait_ge(cols_done, l + 1)
                v.tensor_copy(cols[:], bank[4][:, S:S + 128].rearrange("p (c k) -> p c k", c=NT)).then_inc(cols_ready, 1)
                dve.wait_ge(cols_ready, l + 1)
                for i in range(DNH + 1):
                    if i < DNH:
                        dve.wait_ge(bc_act, l * 4 + i + 1)
                        for c in range(NT):
                            ins = v.scalar_tensor_tensor(gam[:, i, c * P:(c + 1) * P], bank[i % 2][:, c * P:(c + 1) * P],
                                                         cols[:, c, 32 + i:33 + i], cc("decmask"), ALU.subtract, ALU.add)
                        ins.then_inc(bc_dve, 1)
                        dve.wait_ge(tr_done, l * 4 + i + 1)
                        for c in range(NT):
                            ins = v.tensor_scalar(vb[:, 2 * i + c, :], bank[6 + i % 2][:, c * P:(c + 1) * P],
                                                  cols[:, c, i:i + 1], None, ALU.mult)
                        ins.then_inc(tr_dve, 1)
                    i -= 1
                    if i < 0:
                        continue
                    dve.wait_ge(gram_done, l * 4 + i + 1)
                    dve.wait_ge(gam_ready, l * 4 + i + 1)
                    dve.wait_ge(gb_ready, l * 4 + i + 1)
                    pair = bank[2 + i % 2][:, :].rearrange("p (c w k) -> p c w k", c=NT, w=2)
                    v.tensor_tensor(qkt[:, 2 * i:2 * i + 2, :], pair[:, :, 1, :],
                                    gam[:, i, :].rearrange("p (c k) -> p c k", c=NT), ALU.mult)
                    v.tensor_tensor(bp[:, 2 * i:2 * i + 2, :], pair[:, :, 0, :],
                                    bp[:, 2 * i:2 * i + 2, :], ALU.mult).then_inc(gram_used, 1)

                def attend(i):
                    if i < SWAH:
                        dve.wait_ge(att_s, l * 8 + i + 1)
                        ch.mark(v.scalar_tensor_tensor(prob[:, i, :], bank[2 + i % 2][:, 0:3 * P], SWAD ** -0.5,
                                                       cc("dilmask"), ALU.mult, ALU.add))
                        ch.dep()
                        ch.mark(v.tensor_reduce(att_max[:, 2 * i:2 * i + 1], prob[:, i, 0:P], AX_X, ALU.max, negate=True))
                        v.tensor_reduce(att_max[:, 2 * i + 1:2 * i + 2], prob[:, i, P:3 * P], AX_X, ALU.max,
                                        negate=True).then_inc(att_sm, 1)
                    j = i - 1
                    if 0 <= j < SWAH:
                        dve.wait_ge(att_p, l * 8 + j + 1)
                        ch.mark(v.reciprocal(att_rz[:, 2 * j:2 * j + 2], att_z[:, 2 * j:2 * j + 2]))
                        ch.dep()
                        v.tensor_scalar(prob[:, j, 0:P], prob[:, j, 0:P], att_rz[:, 2 * j:2 * j + 1], None, ALU.mult)
                        v.tensor_scalar(prob[:, j, P:3 * P], prob[:, j, P:3 * P], att_rz[:, 2 * j + 1:2 * j + 2], None,
                                        ALU.mult).then_inc(att_pn, 1)

                for lev in range(LEVELS):
                    if lev >= 1:
                        attend(lev - 1)
                    for g in range(2):
                        us = slice(4 * g, 4 * g + 4)
                        t_ps = bank[g][:, :].rearrange("p (u k) -> p u k", u=4)
                        u_ps = bank[6 + g][:, :].rearrange("p (u k) -> p u k", u=4)
                        if lev == 0:
                            eye = ident.unsqueeze(1).to_broadcast([P, 4, P])
                            dve.wait_ge(bl_ready, l * (LEVELS + 1) + g + 1)
                            v.tensor_tensor(uinv[:, us, :], eye, bl[:, 0, us, :], ALU.subtract)
                            dve.wait_ge(lev_x, l * 2 * LEVELS + g + 1)
                            v.tensor_tensor(tinv[:, us, :], eye, t_ps, ALU.subtract).then_inc(tu_ready, 1)
                        else:
                            dve.wait_ge(lev_y, l * 2 * (LEVELS - 1) + 2 * (lev - 1) + g + 1)
                            dve.wait_ge(tu_ready, l * 2 * LEVELS + 2 * (lev - 1) + g + 1)
                            if lev < LEVELS - 1:
                                v.tensor_tensor(tinv[:, us, :], tinv[:, us, :], t_ps, ALU.subtract)
                            v.tensor_tensor(uinv[:, us, :], uinv[:, us, :], u_ps, ALU.subtract).then_inc(tu_ready, 1)
                for i in range(LEVELS - 1, SWAH + 1):
                    attend(i)

                dve.wait_ge(rec_pe, l * 6 + 4)
                v.tensor_tensor(resid[:], vb[:].rearrange("p (i c) k -> p i c k", c=NT)[:, :, 1, :],
                                bank[6][:, :].rearrange("p (i k) -> p i k", i=DNH), ALU.subtract).then_inc(rec_dve, 1)

                def gated(c):
                    half = ot[:, :, c * P:(c + 1) * P]
                    ch.mark(v.scalar_tensor_tensor(half, half, pa_("onorm"), zs[:, :, c * P:(c + 1) * P], ALU.mult, ALU.mult))

                dve.wait_ge(rec_act, l * 7 + 4)
                gated(0)
                for p in range(SWAH // 2):
                    part_lo(4 + p, mix, att_o, l * 8 + 2 * p + 2, mix_lo)
                dve.wait_ge(rec_act, l * 7 + 6)
                gated(1)
                dve.wait_ge(on_std, l + 1)
                v.reciprocal(on_rrms[:], on_rms[:]).then_inc(on_inv, 1)
                ch.dep()
                for k in range(DNH + 1):
                    if k < DNH:
                        dve.wait_ge(on_row, l * 4 + (k // 2 * 2 + 2))
                        v.tensor_tensor(mix[:, k, :], ot[:, k, :], bank[k // 2][:, k % 2 * S:k % 2 * S + S],
                                        ALU.mult).then_inc(mix_ready, 1)
                    if k >= 1:
                        part_lo(k - 1, mix, mix_hi, l * 4 + k, mix_lo)

                for m in range(KD):
                    if m < KD - 1:
                        refill(T_WOUT + m)
                    if m % 2:
                        ins = result_gain(l * 4 + 1, m // 2, lambda k: pa_("post", k))
                ch.mark(ins)
                norm_add(ch, l * 4 + 1)
                refill(T_UP - 1)
                dve.wait_ge(packf_in, l * 16 + 16)
                norm_apply(l * 4 + 2, lambda k: pf_("pre", k), l * 16 + 8)

                def step(r, k, p, q, up=True, down=True):
                    if up:
                        for w, (dst, done) in enumerate(((glu_g, glu_ready), (glu_v, ffn_free))):
                            src = bank[2 * q + w]
                            dve.wait_ge(glu_first, (l * NP_FF + p) * 2 + w + 1)
                            for j in range(1, FCONV):
                                if j > 1:
                                    dve.wait_ge(ffn_chain, (l * NP_FF + p) * FFN_LINKS + w + 1)
                                ins = v.scalar_tensor_tensor(dst[:, q, j:], src[:, 0:S - j], pf_("conv", p * 6 + w * 3 + 2 - j),
                                                             dst[:, q, j:], ALU.mult, ALU.add)
                                ins.then_inc(ffn_chain if j < FCONV - 1 else done, 1)
                            refill_lo(r, k + w)
                        k = k + 2
                    if down:
                        refill_lo(r, k)
                    if up:
                        dve.wait_ge(gelu_done, l * NP_FF + p + 1 + CREDITS)
                        dve.wait_ge(ffn_free, l * NP_FF + p + 1 + CREDITS)
                        v.tensor_tensor(hid_hi[:, q, :], glu_a[:, q, :], glu_v[:, q, :], ALU.mult).then_inc(hi_done, 1)

                r0 = l * (LAYER_TILES // SLOTS) + T_UP // SLOTS
                for p in range(DOWN_LAG):
                    step(r0, 2 * p, p, p % PAIRS, down=False)
                for p in range(DOWN_LAG, PEEL):
                    step(r0 + (p - 1), 1, p, p % PAIRS)
                with dve.Fori(0, GLU_LOOPS) as i:
                    for q in range(PAIRS):
                        step(r0 + i * PAIRS + (q + PEEL - 1), 1, i * PAIRS + (q + PEEL), q)
                for p in range(NP_FF, NP_FF + DOWN_LAG - 1):
                    step(r0 + (NP_FF - 1), 1 + p - NP_FF, p, p % PAIRS, up=False)
                for g in range(KD // 2):
                    ins = result_gain(l * 4 + 3, g, lambda k: pf_("post", k))
                ch.mark(ins)
                norm_add(ch, l * 4 + 3)
                refill_lo(r0 + (NP_FF - 1), DOWN_LAG)
                assert ch.n == DVE_LINKS, ("DVE_LINKS", ch.n)

            with dve.Fori(0, DEPTH) as l:
                layer(l)
            second_vector(dve, norm_apply, softplus, refill_lo, part_lo)

        @block.gpsimd
        def _(pool):
            pool.dma_start(pa[:], packa[0]).then_inc(packa_in, 16)
            pl.memset(rows[:], 0.0).then_inc(zeroed, 1)
            pool.wait_ge(zeroed, 1)
            for q in range(PAIRS):
                pl.memset(credit[:, 3 * q:3 * q + 1], 0.0).then_inc(hid_done, 1)
                pl.memset(credit[:, 3 * q + 1:3 * q + 2], 0.0).then_inc(ffn_free, 1)
                pl.memset(credit[:, 3 * q + 2:3 * q + 3], 0.0).then_inc(gelu_done, 1)

            def pre_sums(i):
                for g in range(KD // 2):
                    pool.wait_ge(norm_sq, i * (KD // 2) + g + 1)
                    pl.tensor_tensor(sq[:, 2 * g, :], sq[:, 2 * g, :], sq[:, 2 * g + 1, :], ALU.add).then_inc(norm_pair, 1)

            def layer(l):
                ch = Chain(pool, pool_chain, l * POOL_LINKS)
                pre_sums(l * 4)
                pool.wait_ge(x_ready, l * 16 + 8)
                pool.dma_start(pf[:], packf[bass.ds(l, 1)].rearrange("o p n -> (o p) n")).then_inc(packf_in, 16)
                pool.wait_ge(masks_in, 16)
                for j in range(8):
                    pool.wait_ge(proj_evac, l * 16 + 4 + j + 1)
                    pool.wait_ge(rope_rot, l * 8 + j + 1)
                    pl.tensor_tensor(raw[:, j, :], raw[:, j, :], cc("cos"), ALU.mult).then_inc(rope_cos, 1)
                for i in range(DNH):
                    pool.wait_ge(bc_act, l * 4 + i + 1)
                    pool.wait_ge(gam_ready, l * 4 + i + 1)
                    pl.tensor_tensor(bp[:, 2 * i:2 * i + 2, :].rearrange("p c k -> p (c k)"), bbc[:, i, :], gam[:, i, :],
                                     ALU.mult).then_inc(gb_ready, 1)
                for lev in range(LEVELS):
                    if lev >= 2:
                        pool.wait_ge(lev_x, l * 2 * LEVELS + 2 * (lev - 1))
                        pool.wait_ge(tu_ready, l * 2 * LEVELS + 2 * (lev - 1))
                    for us in (slice(0, DNH), slice(DNH, 2 * DNH)) if lev == 0 else (slice(0, 2 * DNH),):
                        pool.wait_ge(gram_used, l * 4 + us.stop // NT)
                        pl.tensor_tensor(bl[:, lev % 2, us], bp[:, us],
                                         cc("level", lev, P).unsqueeze(1).to_broadcast([P, us.stop - us.start, P]),
                                         ALU.mult).then_inc(bl_ready, 1)
                    for i in range(DNH) if lev == 1 else ():
                        pool.wait_ge(qk_ready, l * 4 + 4)
                        pl.tensor_tensor(qg[:, i, :], qkn[:, i, P:S], eg1[:, i, :], ALU.mult)
                        ch.mark(pl.tensor_tensor(kbg[:, i, :], qkn[:, 4 + i, P:S], eg1[:, i, :], ALU.mult))
                        ch.dep()
                        pl.tensor_tensor(kbg[:, i, :], kbg[:, i, :], bbc[:, i, P:S], ALU.mult).then_inc(kbg_ready, 1)

                def product(p, q):
                    pool.wait_ge(gelu_done, l * NP_FF + p + 1 + CREDITS)
                    pool.wait_ge(ffn_free, l * NP_FF + p + 1 + CREDITS)
                    pool.wait_ge(hid_done, l * NP_FF + p + 1)
                    pl.tensor_tensor(glu_p[:, q, :], glu_a[:, q, :], glu_v[:, q, :], ALU.mult).then_inc(prod_done, 1)
                    pool.wait_ge(prod_done, l * NP_FF + p + 1)
                    pool.wait_ge(hi_done, l * NP_FF + p + 1)
                    pl.tensor_tensor(hid_lo[:, q, :], glu_p[:, q, :], hid_hi[:, q, :].bitcast(F32),
                                     ALU.subtract).then_inc(hid_done, 1)

                pre_sums(l * 4 + 2)
                pool.wait_ge(x_ready, l * 16 + 16)
                pool.dma_start(pa[:], packa[bass.ds(l + 1, 1)].rearrange("o p n -> (o p) n")).then_inc(packa_in, 16)
                with pool.Fori(0, NP_FF // PAIRS) as i:
                    for q in range(PAIRS):
                        product(i * PAIRS + q, q)
                assert ch.n == POOL_LINKS, ("POOL_LINKS", ch.n)

            with pool.Fori(0, DEPTH) as l:
                layer(l)
            second_pool(pool, pre_sums)


def shape_constants():
    c = np.zeros((P, C_W), np.float32)

    def put(name, value):
        lo, hi = C_COLS[name]
        value = np.asarray(value, np.float32)
        c[:value.shape[0], lo:hi] = value

    i = np.arange(P)
    put("ident", np.eye(P))
    put("ones256", np.ones((P, S)))
    put("bd64", i[:, None] // 64 == i[None, :] // 64)
    half, d = ROPE_DIM // 2, i % SWAD
    rot = np.zeros((P, P))
    for o in range(P):
        if d[o] < half:
            rot[o + half, o] = -1.0
        elif d[o] < ROPE_DIM:
            rot[o - half, o] = 1.0
    put("rot", rot)
    freq = np.float32(ROPE_THETA) ** (-np.arange(0, ROPE_DIM, 2, dtype=np.float32) / np.float32(ROPE_DIM))
    angle = np.arange(S, dtype=np.float32)[None, :] * freq[:, None]
    cos, sin = np.ones((P, S), np.float32), np.zeros((P, S), np.float32)
    for o in range(P):
        if d[o] < ROPE_DIM:
            cos[o], sin[o] = np.cos(angle[d[o] % half]), np.sin(angle[d[o] % half])
    put("cos", cos)
    put("sin", sin)
    put("decmask", np.where(i[None, :] >= i[:, None], 0.0, NEG))
    levels = []
    for lev in range(LEVELS):
        b = 2 ** lev
        same = i[:, None] // (2 * b) == i[None, :] // (2 * b)
        levels.append(same & (i[:, None] % (2 * b) < b) & (i[None, :] % (2 * b) >= b))
    put("level", np.concatenate(levels, axis=1))
    times = np.zeros((S, S))
    dist = np.arange(S)[:, None] - np.arange(S)[None, :]
    for window, dil in DIL:
        times += (dist >= 0) & (dist <= window) & (dist % dil == 0)
    logs = np.where(times > 0, np.log(np.maximum(times, 1)), NEG)
    put("dilmask", np.concatenate([logs[0:P, 0:P], logs[P:S, :]], axis=1))
    causal = np.where(dist >= 0, 0.0, NEG)
    put("causal", np.concatenate([causal[0:P, 0:P], causal[P:S, :]], axis=1))
    put("eps", np.full((P, 1), EPS))
    put("gmask", (i[None, :] // GB == i[:, None] // GB) & (i[None, :] >= i[:, None]))
    put("selhead", i[:, None] // GDK == np.arange(GH)[None, :])
    put("first4", np.tile([4.0, 3.0, 2.0, 1.0], (P, 1)))
    return c


def kernel(**inputs):
    import concourse.bacc as bacc
    from concourse.bass_utils import run_bass_kernel_spmd

    w = {k: np.asarray(a) for k, a in inputs.items()}

    def tiles(m):
        k, n = m.shape
        return m.reshape(k // P, P, n // P, P).transpose(2, 1, 0, 3).reshape(n // P, P, k)

    def blocks(m, order):
        b = np.stack([m[r * P:(r + 1) * P, c * P:(c + 1) * P] for r, c in order])
        return b.reshape(-1, 8, P, P).transpose(0, 2, 1, 3).reshape(-1, P, 8 * P)

    def token_tiles(m):
        k, n = m.shape
        return m.reshape(2, KD // 2, P, n // S, S).transpose(3, 0, 2, 1, 4).reshape(n // P, P, k)

    def cols(v):
        return v.reshape(-1, P).T

    parts = []
    packa = np.zeros((DEPTH + 1, P, A_W), np.float32)
    packf = np.zeros((DEPTH, P, F_W), np.float32)
    packb = np.zeros((P, B_W), np.float32)

    def put(pack, table, name, value):
        lo, hi = table[name]
        value = value.reshape(value.shape[0], -1)
        assert value.shape[1] == hi - lo, name
        pack[:value.shape[0], lo:hi] = value

    for l in range(DEPTH):
        wi = w["w_in"][l]
        small = 4 * DNH * P
        parts.append(tiles(wi[:, :small]))
        parts.append(tiles(wi[:, small + 2 * DNH:-SWAH * SWAD]))
        parts.append(token_tiles(wi[:, -SWAH * SWAD:]))
        parts.append(tiles(w["w_out"][l]))
        up = tiles(w["ffn_up"][l])
        down = blocks(w["ffn_down"][l], [(k, m) for k in range(NP_FF) for m in range(KD)])
        for p in range(NP_FF + DOWN_LAG):
            if p < NP_FF:
                parts.append(up[[p, NP_FF + p]])
            if p >= DOWN_LAG:
                parts.append(down[p - DOWN_LAG:p - DOWN_LAG + 1])
        put(packa[l], A_COLS, "pre", cols(w["pre_mix_norm"][l]))
        put(packa[l], A_COLS, "post", cols(w["post_mix_norm"][l]))
        put(packa[l], A_COLS, "conv", w["dn_conv"][l].reshape(CONV, 12, P).transpose(2, 1, 0))
        put(packa[l], A_COLS, "onorm", w["dn_out_norm"][l].reshape(P, 1))
        lo = A_COLS["alog"][0]
        packa[l, 32:32 + DNH, lo] = w["dn_a_log"][l]
        lo = A_COLS["dt"][0]
        packa[l, 32:32 + DNH, lo] = w["dn_dt_bias"][l]
        ba = np.zeros((P, KD, 64), np.float32)
        ba[:, :, 0:DNH] = wi[:, small:small + DNH].reshape(KD, P, DNH).transpose(1, 0, 2)
        ba[:, :, 32:32 + DNH] = wi[:, small + DNH:small + 2 * DNH].reshape(KD, P, DNH).transpose(1, 0, 2)
        put(packa[l], A_COLS, "wba", ba)
        put(packf[l], F_COLS, "pre", cols(w["pre_ffn_norm"][l]))
        put(packf[l], F_COLS, "post", cols(w["post_ffn_norm"][l]))
        put(packf[l], F_COLS, "conv", w["ffn_conv"][l].reshape(FCONV, 2, NP_FF, P).transpose(3, 2, 1, 0))
        put(packf[l], F_COLS, "bias", w["ffn_conv_bias"][l].reshape(2, NP_FF, P).transpose(2, 1, 0))

    w2 = w["w_in_2"][0]
    edges = np.cumsum([GH * GDK, GH * GDK, GH * GDV, GRANK, GH * GDV, 512, 512, 512, 512])
    gq, gk, gv, glr, gog, cu, dq, dk, dv = np.split(w2, edges[:-1], axis=1)
    ct = tiles(cu)
    parts += [tiles(gq), tiles(gk), ct[[0, 2, 1, 3]], tiles(gog), token_tiles(gv), tiles(dq), tiles(dk), token_tiles(dv),
              tiles(w["w_out_2"][0])]
    ups, downs = [], []
    for e in range(NE):
        ups.append(np.concatenate([tiles(w["expert_w_gate_2"][0, e]), tiles(w["expert_w_up_2"][0, e])]))
        downs.append(blocks(w["expert_w_down_2"][0, e], [(k, m) for m in range(KD) for k in range(2)]))
    parts.append(ups[0])
    for e in range(NE - 1):
        parts += [ups[e + 1], downs[e]]
    parts.append(downs[-1])
    wtiles = np.concatenate(parts)
    assert wtiles.shape == (ALL_TILES, P, KD * P)

    put(packb, B_COLS, "mix", cols(w["mix_norm_g_2"][0]))
    put(packb, B_COLS, "ffn", cols(w["ffn_norm_g_2"][0]))
    put(packb, B_COLS, "wglr", glr.reshape(KD, P, GRANK).transpose(1, 0, 2))
    router = np.concatenate([w["router_group_w_2"][0], w["router_expert_w_2"][0]], axis=1)
    put(packb, B_COLS, "wrt", router.reshape(KD, P, NR).transpose(1, 0, 2))
    put(packb, B_COLS, "rbias", np.concatenate([w["router_group_b_2"][0], w["router_expert_b_2"][0]]).reshape(1, NR))
    put(packb, B_COLS, "glab", w["gla_gate_b_2"][0].reshape(P, 1))
    put(packb, B_COLS, "gatew", w["gla_gate_w_2"][0])
    put(packb, B_COLS, "convw", w["conv_w_2"][0].reshape(CW, 2, P).transpose(2, 1, 0))
    for name, key in (("convb", "conv_b_2"), ("cng", "conv_norm_g_2"), ("cnb", "conv_norm_b_2")):
        put(packb, B_COLS, name, cols(w[key][0]))
    for name, key in (("glan", "gla_norm_g_2"), ("qn", "diff_qnorm_g_2"), ("kn", "diff_knorm_g_2")):
        put(packb, B_COLS, name, np.tile(w[key][0], 2).reshape(P, 1))
    put(packb, B_COLS, "subln", w["diff_subln_g_2"][0].reshape(P, 1))
    put(packb, B_COLS, "lam", np.stack([w[f"diff_{n}_2"][0] for n in ("lq1", "lk1", "lq2", "lk2")], axis=1))

    arrays = {
        "xt": np.ascontiguousarray(w["x"][0].T.reshape(KD, P, S).transpose(1, 0, 2)),
        "wtiles": wtiles, "consts": shape_constants(), "packa": packa, "packf": packf, "packb": packb,
    }
    nc = bacc.Bacc("TRN2", target_bir_lowering=False, num_devices=1)
    args = [nc.dram_tensor(name, arr.shape, F32, kind="ExternalInput").ap() for name, arr in arrays.items()]
    out = nc.dram_tensor("out", (P, KD, S), F32, kind="ExternalOutput").ap()
    block_program(nc, *args, out)
    got = run_bass_kernel_spmd(nc, [arrays], core_ids=[0]).results[0]["out"]
    return got.transpose(1, 0, 2).reshape(1, D, S).transpose(0, 2, 1)
```
